# Optimizing a Trainium2 kernel written in Bass

```python
import math
import jax, jax.numpy as jnp
from jax import lax
import numpy as np

D_MODEL = 1024
BATCH = 1
SEQ = 512
DEPTH = 2

N_POOL_LAYERS = DEPTH // 2
N_ATTN_LAYERS = DEPTH - N_POOL_LAYERS
POOL_WINDOWS = (2, 4, 8, 16)
N_POOL_GROUPS = len(POOL_WINDOWS)
POOL_GROUP_DIM = D_MODEL // N_POOL_GROUPS
BRANCHES = ((128, 1), (512, 4), (2048, 16))
N_BRANCHES = len(BRANCHES)
HEAD_DIM = 64
N_HEADS = D_MODEL // HEAD_DIM
D_ATTN = N_HEADS * HEAD_DIM
ATTN_BLOCK = 128
D_FF = 2816
CONV_WIDTH = 3
EPS = 1e-6
ADA_SCALE = 0.5


def _rmsnorm(x, g):
    x32 = x.astype(jnp.float32)
    y = x32 * lax.rsqrt(jnp.mean(x32 * x32, axis=-1, keepdims=True) + EPS)
    return (y * g.astype(jnp.float32)).astype(x.dtype)

def _modulate(h, shift, scale):
    return h * (1 + scale[:, None, :]) + shift[:, None, :]

def _alibi_slopes(n):
    def pow2(m):
        start = 2.0 ** (-(2.0 ** -(math.log2(m) - 3)))
        return [start ** (i + 1) for i in range(m)]
    if math.log2(n).is_integer():
        s = pow2(n)
    else:
        c = 2 ** math.floor(math.log2(n))
        s = pow2(c) + pow2(2 * c)[0::2][: n - c]
    s = np.asarray(s, dtype=np.float32)
    return -np.sort(-s)

def _pool_mixer(h, w_in, w_grp, scale, w_out):
    b, s, _ = h.shape
    u = (h @ w_in).reshape(b, s, N_POOL_GROUPS, POOL_GROUP_DIM)
    u32 = u.astype(jnp.float32)
    csum = jnp.cumsum(u32, axis=1)
    t = jnp.arange(s)
    outs = []
    for g, w in enumerate(POOL_WINDOWS):
        cs = csum[:, :, g]
        lag = jnp.pad(cs, ((0, 0), (w, 0), (0, 0)))[:, :s]
        count = jnp.minimum(t + 1, w).astype(jnp.float32)[None, :, None]
        pooled = (cs - lag) / count - u32[:, :, g]
        outs.append(jnp.einsum('bsc,cd->bsd', pooled.astype(h.dtype), w_grp[g]))
    y = jnp.concatenate(outs, axis=-1) * scale
    return y @ w_out

def _causal_dwconv(a, w, bias):
    s = a.shape[1]
    ap = jnp.pad(a, ((0, 0), (CONV_WIDTH - 1, 0), (0, 0)))
    y = bias
    for k in range(CONV_WIDTH):
        y = y + ap[:, k:k + s] * w[k]
    return y

def _conv_ffn(h, w_up, conv_w, conv_b, w_down):
    a, v = jnp.split(h @ w_up, 2, axis=-1)
    a = _causal_dwconv(a, conv_w, conv_b)
    return (jax.nn.silu(a) * v) @ w_down

def _dilated_branch(q, k, v, window, dilation, slopes):
    b, s, h, dh = q.shape
    n_steps = window // dilation
    blk = max(ATTN_BLOCK, n_steps)
    sub_len = s // dilation
    nb = -(-sub_len // blk)
    sub_pad = nb * blk

    def to_sub(t):
        t = t.reshape(b, sub_len, dilation, h, dh).transpose(0, 2, 1, 3, 4).reshape(b * dilation, sub_len, h, dh)
        return jnp.pad(t, ((0, 0), (0, sub_pad - sub_len), (0, 0), (0, 0)))

    def with_prev(t):
        tb = t.reshape(-1, nb, blk, h, dh)
        prev = jnp.pad(tb, ((0, 0), (1, 0), (0, 0), (0, 0), (0, 0)))[:, :nb]
        return jnp.concatenate([prev, tb], axis=2)

    qb = to_sub(q).reshape(-1, nb, blk, h, dh)
    kb = with_prev(to_sub(k))
    vb = with_prev(to_sub(v))

    scores = jnp.einsum('bnqhd,bnkhd->bnhqk', qb, kb).astype(jnp.float32) * (dh ** -0.5)
    qi = jnp.arange(blk)[:, None] + blk
    ki = jnp.arange(2 * blk)[None, :]
    delta = qi - ki
    key_idx = jnp.arange(nb)[:, None] * blk + jnp.arange(2 * blk)[None, :] - blk
    valid = ((delta >= 0) & (delta <= n_steps))[None] & (key_idx >= 0)[:, None, :]
    bias = -slopes[:, None, None] * (delta * dilation).astype(jnp.float32)[None]
    scores = jnp.where(valid[None, :, None], scores + bias[None, None], -jnp.inf)
    lse = jax.nn.logsumexp(scores, axis=-1)
    p = jnp.exp(scores - lse[..., None])
    out = jnp.einsum('bnhqk,bnkhd->bnqhd', p.astype(v.dtype), vb)

    out = out.reshape(b, dilation, sub_pad, h, dh)[:, :, :sub_len]
    out = out.transpose(0, 2, 1, 3, 4).reshape(b, s, h, dh)
    lse = lse.transpose(0, 1, 3, 2).reshape(b, dilation, sub_pad, h)[:, :, :sub_len]
    lse = lse.transpose(0, 2, 1, 3).reshape(b, s, h)
    return out, lse

def _dilated_attention(h, kv, w_q, w_o, slopes):
    b, s, _ = h.shape
    q = (h @ w_q).reshape(b, s, N_BRANCHES, N_HEADS, HEAD_DIM)
    outs, lses = [], []
    for g, (window, dil) in enumerate(BRANCHES):
        o, l = _dilated_branch(q[:, :, g], kv[:, :, 0, g], kv[:, :, 1, g], window, dil, slopes[g])
        outs.append(o)
        lses.append(l)
    wts = jax.nn.softmax(jnp.stack(lses, axis=0), axis=0)
    o = jnp.sum(wts[..., None] * jnp.stack(outs, axis=0).astype(jnp.float32), axis=0)
    return o.reshape(b, s, D_ATTN).astype(h.dtype) @ w_o

def first_inputs(seed: int = 0) -> dict:
    key = jax.random.key(seed)
    ks = jax.random.split(key, 24)

    def nrm(k, shape, scale):
        return jax.random.normal(k, shape, jnp.float32) * scale

    D, F, G = D_MODEL, D_FF, N_BRANCHES
    return {
        "x": nrm(ks[0], (BATCH, SEQ, D), 1.0),
        "c": nrm(ks[1], (BATCH, D), 1.0),
        "ada_w": nrm(ks[2], (DEPTH, D, 6 * D), ADA_SCALE * D ** -0.5),
        "ada_b": nrm(ks[3], (DEPTH, 6 * D), 0.02),
        "norm1_g": 1.0 + nrm(ks[4], (DEPTH, D), 0.05),
        "norm2_g": 1.0 + nrm(ks[5], (DEPTH, D), 0.05),
        "pool_w_in": nrm(ks[6], (N_POOL_LAYERS, D, D), D ** -0.5),
        "pool_w_grp": nrm(ks[7], (N_POOL_LAYERS, N_POOL_GROUPS, POOL_GROUP_DIM, POOL_GROUP_DIM), POOL_GROUP_DIM ** -0.5),
        "pool_scale": 1.0 + nrm(ks[8], (N_POOL_LAYERS, D), 0.1),
        "pool_w_out": nrm(ks[9], (N_POOL_LAYERS, D, D), D ** -0.5),
        "kv_norm_g": 1.0 + nrm(ks[10], (D,), 0.05),
        "kv_ada_w": nrm(ks[11], (D, 2 * D), ADA_SCALE * D ** -0.5),
        "kv_ada_b": nrm(ks[12], (2 * D,), 0.02),
        "w_kv": nrm(ks[13], (D, 2 * G * D_ATTN), D ** -0.5),
        "attn_w_q": nrm(ks[14], (N_ATTN_LAYERS, D, G * D_ATTN), D ** -0.5),
        "attn_w_o": nrm(ks[15], (N_ATTN_LAYERS, D_ATTN, D), D_ATTN ** -0.5),
        "ffn_w_up": nrm(ks[16], (DEPTH, D, 2 * F), D ** -0.5),
        "ffn_conv_w": nrm(ks[17], (DEPTH, CONV_WIDTH, F), CONV_WIDTH ** -0.5),
        "ffn_conv_b": nrm(ks[18], (DEPTH, F), 0.02),
        "ffn_w_down": nrm(ks[19], (DEPTH, F, D), F ** -0.5),
        "final_g": 1.0 + nrm(ks[20], (D,), 0.05),
    }

def first_block(x, c, ada_w, ada_b, norm1_g, norm2_g, pool_w_in, pool_w_grp, pool_scale, pool_w_out,
              kv_norm_g, kv_ada_w, kv_ada_b, w_kv, attn_w_q, attn_w_o,
              ffn_w_up, ffn_conv_w, ffn_conv_b, ffn_w_down, final_g):
    b, s, _ = x.shape
    cond = jax.nn.silu(c)
    slopes = jnp.asarray(_alibi_slopes(N_BRANCHES * N_HEADS)).reshape(N_BRANCHES, N_HEADS)
    kv = None
    for layer in range(DEPTH):
        mod = cond @ ada_w[layer] + ada_b[layer]
        sh1, sc1, g1, sh2, sc2, g2 = jnp.split(mod, 6, axis=-1)
        h = _modulate(_rmsnorm(x, norm1_g[layer]), sh1, sc1)
        if layer < N_POOL_LAYERS:
            y = _pool_mixer(h, pool_w_in[layer], pool_w_grp[layer], pool_scale[layer], pool_w_out[layer])
        else:
            if layer == N_POOL_LAYERS:
                kv_shift, kv_scale = jnp.split(cond @ kv_ada_w + kv_ada_b, 2, axis=-1)
                hkv = _modulate(_rmsnorm(x, kv_norm_g), kv_shift, kv_scale)
                kv = (hkv @ w_kv).reshape(b, s, 2, N_BRANCHES, N_HEADS, HEAD_DIM)
            j = layer - N_POOL_LAYERS
            y = _dilated_attention(h, kv, attn_w_q[j], attn_w_o[j], slopes)
        x = x + g1[:, None, :] * y
        h = _modulate(_rmsnorm(x, norm2_g[layer]), sh2, sc2)
        x = x + g2[:, None, :] * _conv_ffn(h, ffn_w_up[layer], ffn_conv_w[layer], ffn_conv_b[layer], ffn_w_down[layer])
    return _rmsnorm(x, final_g)


GRID_W = 64
CTX_LEN = 256
N_HEADS_A = 4
DH_A = 64
DV_A = 2 * DH_A
WIDTH_A = N_HEADS_A * DV_A
N_HEADS_B = 4
DK_B = 64
DV_B = 64
WIDTH_BK = N_HEADS_B * DK_B
WIDTH_B = N_HEADS_B * DV_B
FN_GROUPS = 4
FN_GROUP_DIM = 64
WIDTH_C = FN_GROUPS * FN_GROUP_DIM
MIX_WIDTH = WIDTH_A + WIDTH_B + WIDTH_C
PROJ_SIZES = (WIDTH_A, WIDTH_A, WIDTH_A, WIDTH_BK, WIDTH_BK, WIDTH_BK, WIDTH_B, WIDTH_B, WIDTH_C)
PROJ_WIDTH = 3 * WIDTH_A + 3 * WIDTH_BK + 2 * WIDTH_B + WIDTH_C
CONV_W = 3
Q_BLOCK = 128
CHUNK = 64
ROPE_BASE = 10000.0


def rms_norm(x, w):
    xf = x.astype(jnp.float32)
    y = xf * lax.rsqrt(jnp.mean(xf * xf, axis=-1, keepdims=True) + EPS)
    return (y * w.astype(jnp.float32)).astype(x.dtype)

def modulate(h, shift, scale):
    return h * (1 + scale) + shift

def flip(a):
    return jnp.flip(a, axis=1)

def axial_rope(rows):
    pos_r = jnp.repeat(jnp.arange(rows), GRID_W).astype(jnp.float32)
    pos_c = jnp.tile(jnp.arange(GRID_W), rows).astype(jnp.float32)
    half = DH_A // 2
    inv_freq = ROPE_BASE ** (-jnp.arange(0, half, 2, dtype=jnp.float32) / half)
    ang_r = pos_r[:, None] * inv_freq
    ang_c = pos_c[:, None] * inv_freq
    ang = jnp.concatenate([ang_r, ang_r, ang_c, ang_c], axis=-1)
    return jnp.cos(ang), jnp.sin(ang)

def _rotate_half(p):
    h = p.shape[-1] // 2
    return jnp.concatenate([-p[..., h:], p[..., :h]], axis=-1)

def apply_axial_rope(t, cos, sin):
    t_row, t_col = jnp.split(t, 2, axis=-1)
    rot = jnp.concatenate([_rotate_half(t_row), _rotate_half(t_col)], axis=-1)
    cos = cos[None, :, None, None, :]
    sin = sin[None, :, None, None, :]
    return (t * cos + rot * sin).astype(t.dtype)

def diff_attend(q, k, v, lam):
    s = jnp.einsum('bqhcd,bkhcd->bhcqk', q, k).astype(jnp.float32) * (DH_A ** -0.5)
    p = jax.nn.softmax(s, axis=-1)
    a = p[:, :, 0] - lam * p[:, :, 1]
    return jnp.einsum('bhqk,bkhd->bqhd', a, v.astype(jnp.float32))

def diff_attend_blocks(q, k, v, lam):
    b, l = q.shape[:2]
    nb = l // Q_BLOCK
    qb = q.reshape(b, nb, Q_BLOCK, N_HEADS_A, 2, DH_A).transpose(1, 0, 2, 3, 4, 5)
    o = lax.map(lambda blk: diff_attend(blk, k, v, lam), qb)
    return o.transpose(1, 0, 2, 3, 4).reshape(b, l, N_HEADS_A, DV_A)

def diff_head_norm(o, w, lam_init):
    b, l = o.shape[:2]
    return (rms_norm(o, w) * (1.0 - lam_init)).reshape(b, l, WIDTH_A)

def log_forget(z, lb):
    zf = z.astype(jnp.float32)
    return jnp.logaddexp(jnp.log(lb), jnp.log1p(-lb) + jax.nn.log_sigmoid(zf))

def hgrn_scan(q, k, v, logf, s0):
    b, l, h, _ = q.shape
    dv = v.shape[-1]
    nc = l // CHUNK

    def chunks(a):
        return a.reshape(b, nc, CHUNK, h, a.shape[-1]).transpose(1, 0, 3, 2, 4)

    lower = jnp.tril(jnp.ones((CHUNK, CHUNK), dtype=bool))[:, :, None]

    def step(state, blk):
        qc, kc, vc, gc = blk
        cum = jnp.cumsum(gc, axis=2)
        rel = jnp.where(lower, cum[:, :, :, None, :] - cum[:, :, None, :, :], -jnp.inf)
        scores = jnp.einsum('bhtd,bhsd,bhtsd->bhts', qc, kc, jnp.exp(rel))
        o = (jnp.einsum('bhts,bhsv->bhtv', scores, vc)
             + jnp.einsum('bhtd,bhdv->bhtv', qc * jnp.exp(cum), state))
        cum_end = cum[:, :, -1:, :]
        state = (jnp.exp(cum_end)[:, :, 0, :, None] * state
                 + jnp.einsum('bhsd,bhsv->bhdv', kc * jnp.exp(cum_end - cum), vc))
        return state, o

    state, o = lax.scan(step, s0, (chunks(q), chunks(k), chunks(v), chunks(logf)))
    return o.transpose(1, 0, 3, 2, 4).reshape(b, l, h, dv), state

def hgrn_final_state(k, v, logf):
    tail = flip(jnp.cumsum(flip(logf), axis=1)) - logf
    return jnp.einsum('blhk,blhv->bhkv', k * jnp.exp(tail), v)

def hgrn_bidir(m, s_fwd, s_bwd):
    o_f, st_f = hgrn_scan(m['qh'], m['kf'], m['vh'], m['gf'], s_fwd)
    o_b, st_b = hgrn_scan(flip(m['qh']), flip(m['kb']), flip(m['vh']), flip(m['gb']), s_bwd)
    return o_f + flip(o_b), st_f, st_b

def hgrn_out(o, og, w):
    b, l = o.shape[:2]
    return (rms_norm(o, w) * jax.nn.silu(og.astype(jnp.float32))).reshape(b, l, WIDTH_B)

def fourier_mix(u, w):
    b, l, _ = u.shape
    ug = u.astype(jnp.float32).reshape(b, l, FN_GROUPS, FN_GROUP_DIM)
    y = jnp.fft.fft2(ug, axes=(1, 3), norm='ortho').real.reshape(b, l, WIDTH_C)
    return y.astype(u.dtype) @ w

def conv_ffn(h, w_up, conv_w, conv_b, w_down):
    u = h @ w_up
    up = jnp.pad(u, ((0, 0), (1, 1), (0, 0)))
    u = up[:, :-2] * conv_w[0] + up[:, 1:-1] * conv_w[1] + up[:, 2:] * conv_w[2] + conv_b
    gate, val = jnp.split(u, 2, axis=-1)
    return (jax.nn.silu(gate) * val) @ w_down

def unpack(p, lb):
    b, l, _ = p.shape
    idx = np.cumsum(PROJ_SIZES)[:-1].tolist()
    qa, ka, va, qh, zf, zb, ih, gh, uf = jnp.split(p, idx, axis=-1)
    gf = log_forget(zf, lb[0]).reshape(b, l, N_HEADS_B, DK_B)
    gb = log_forget(zb, lb[1]).reshape(b, l, N_HEADS_B, DK_B)
    return {
        'qa': qa.reshape(b, l, N_HEADS_A, 2, DH_A),
        'ka': ka.reshape(b, l, N_HEADS_A, 2, DH_A),
        'va': va.reshape(b, l, N_HEADS_A, DV_A),
        'qh': qh.reshape(b, l, N_HEADS_B, DK_B).astype(jnp.float32),
        'gf': gf, 'gb': gb,
        'kf': -jnp.expm1(gf), 'kb': -jnp.expm1(gb),
        'vh': ih.reshape(b, l, N_HEADS_B, DV_B).astype(jnp.float32),
        'og': gh.reshape(b, l, N_HEADS_B, DV_B),
        'uf': uf,
    }

def merge(att, rec, four, w_out, dt):
    return jnp.concatenate([att.astype(dt), rec.astype(dt), four.astype(dt)], axis=-1) @ w_out

def second_inputs(seed: int = 0) -> dict:
    key = jax.random.key(seed)
    ks = jax.random.split(key, 20)
    f32 = jnp.float32

    def nrm(k, shape, s):
        return s * jax.random.normal(k, shape, f32)

    return {
        'x': nrm(ks[0], (BATCH, SEQ, D_MODEL), 1.0),
        'c': nrm(ks[1], (BATCH, D_MODEL), 1.0),
        'ctx': nrm(ks[2], (BATCH, CTX_LEN, D_MODEL), 1.0),
        'c_ctx': nrm(ks[3], (D_MODEL,), 1.0),
        'w_ada': nrm(ks[4], (DEPTH, D_MODEL, 6 * D_MODEL), 0.5 * D_MODEL ** -0.5),
        'b_ada': nrm(ks[5], (DEPTH, 6 * D_MODEL), 0.02),
        'norm1_w': 1.0 + nrm(ks[6], (DEPTH, D_MODEL), 0.05),
        'norm2_w': 1.0 + nrm(ks[7], (DEPTH, D_MODEL), 0.05),
        'w_in': nrm(ks[8], (DEPTH, D_MODEL, PROJ_WIDTH), D_MODEL ** -0.5),
        'lam_qk': nrm(ks[9], (DEPTH, 4, DH_A), 0.1),
        'subln_w': 1.0 + nrm(ks[10], (DEPTH, DV_A), 0.05),
        'lb_param': nrm(ks[11], (DEPTH, 2, WIDTH_BK), 0.5),
        'hgrn_norm_w': 1.0 + nrm(ks[12], (DEPTH, DV_B), 0.05),
        'w_fnet': nrm(ks[13], (DEPTH, WIDTH_C, WIDTH_C), WIDTH_C ** -0.5),
        'w_out': nrm(ks[14], (DEPTH, MIX_WIDTH, D_MODEL), MIX_WIDTH ** -0.5),
        'w_up': nrm(ks[15], (DEPTH, D_MODEL, 2 * D_FF), D_MODEL ** -0.5),
        'conv_w': jnp.array([0.0, 1.0, 0.0], f32)[None, :, None] + nrm(ks[16], (DEPTH, CONV_W, 2 * D_FF), 0.2),
        'conv_b': nrm(ks[17], (DEPTH, 2 * D_FF), 0.02),
        'w_down': nrm(ks[18], (DEPTH, D_FF, D_MODEL), D_FF ** -0.5),
        'final_norm_w': 1.0 + nrm(ks[19], (D_MODEL,), 0.05),
    }

def second_block(x, c, ctx, c_ctx, w_ada, b_ada, norm1_w, norm2_w, w_in, lam_qk, subln_w,
              lb_param, hgrn_norm_w, w_fnet, w_out, w_up, conv_w, conv_b, w_down, final_norm_w):
    b, l, _ = x.shape
    rows = l // GRID_W
    cos, sin = axial_rope(rows)
    lb_all = jnp.cumsum(jax.nn.softmax(lb_param.astype(jnp.float32), axis=0), axis=0)
    lb_all = lb_all - lb_all[0:1]
    c_act = jax.nn.silu(c)
    cc_act = jax.nn.silu(c_ctx)
    xc = ctx
    for li in range(DEPTH):
        last = li == DEPTH - 1
        dt = x.dtype
        mod = c_act @ w_ada[li] + b_ada[li]
        sh1, sc1, g1, sh2, sc2, g2 = jnp.split(mod[:, None, :], 6, axis=-1)
        mod_c = cc_act @ w_ada[li] + b_ada[li]
        sh1c, sc1c, g1c, sh2c, sc2c, g2c = jnp.split(mod_c[None, None, :], 6, axis=-1)
        lam_init = 0.8 - 0.6 * math.exp(-0.3 * li)
        lq1, lk1, lq2, lk2 = lam_qk[li].astype(jnp.float32)
        lam = jnp.exp(jnp.sum(lq1 * lk1)) - jnp.exp(jnp.sum(lq2 * lk2)) + lam_init

        m = unpack(modulate(rms_norm(x, norm1_w[li]), sh1, sc1) @ w_in[li], lb_all[li])
        mc = unpack(modulate(rms_norm(xc, norm1_w[li]), sh1c, sc1c) @ w_in[li], lb_all[li])

        k_all = jnp.concatenate([mc['ka'], apply_axial_rope(m['ka'], cos, sin)], axis=1)
        v_all = jnp.concatenate([mc['va'], m['va']], axis=1)
        att = diff_head_norm(diff_attend_blocks(apply_axial_rope(m['qa'], cos, sin), k_all, v_all, lam),
                             subln_w[li], lam_init)

        if last:
            s_f = hgrn_final_state(mc['kf'], mc['vh'], mc['gf'])
            s_b = hgrn_final_state(flip(mc['kb']), flip(mc['vh']), flip(mc['gb']))
        else:
            zeros = jnp.zeros((xc.shape[0], N_HEADS_B, DK_B, DV_B), jnp.float32)
            o_c, s_f, s_b = hgrn_bidir(mc, zeros, zeros)
        o_l, _, _ = hgrn_bidir(m, s_f, s_b)
        rec = hgrn_out(o_l, m['og'], hgrn_norm_w[li])

        four = fourier_mix(m['uf'], w_fnet[li])

        x = x + g1 * merge(att, rec, four, w_out[li], dt)
        x = x + g2 * conv_ffn(modulate(rms_norm(x, norm2_w[li]), sh2, sc2),
                              w_up[li], conv_w[li], conv_b[li], w_down[li])

        if not last:
            att_c = diff_head_norm(diff_attend(mc['qa'], mc['ka'], mc['va'], lam), subln_w[li], lam_init)
            rec_c = hgrn_out(o_c, mc['og'], hgrn_norm_w[li])
            four_c = fourier_mix(mc['uf'], w_fnet[li])
            xc = xc + g1c * merge(att_c, rec_c, four_c, w_out[li], dt)
            xc = xc + g2c * conv_ffn(modulate(rms_norm(xc, norm2_w[li]), sh2c, sc2c),
                                     w_up[li], conv_w[li], conv_b[li], w_down[li])
    return rms_norm(x, final_norm_w)


def setup_inputs(seed=0):
    out = dict(first_inputs(seed))
    for name, value in second_inputs(seed + 1).items():
        if name != "x":
            out[name + "_2"] = value
    return out


def reference(
    x, c, ada_w, ada_b, norm1_g, norm2_g, pool_w_in, pool_w_grp, pool_scale, pool_w_out,
    kv_norm_g, kv_ada_w, kv_ada_b, w_kv, attn_w_q, attn_w_o, ffn_w_up, ffn_conv_w, ffn_conv_b,
    ffn_w_down, final_g, c_2, ctx_2, c_ctx_2, w_ada_2, b_ada_2, norm1_w_2, norm2_w_2, w_in_2,
    lam_qk_2, subln_w_2, lb_param_2, hgrn_norm_w_2, w_fnet_2, w_out_2, w_up_2, conv_w_2,
    conv_b_2, w_down_2, final_norm_w_2,
):
    x = first_block(
        x, c, ada_w, ada_b, norm1_g, norm2_g, pool_w_in, pool_w_grp, pool_scale, pool_w_out,
        kv_norm_g, kv_ada_w, kv_ada_b, w_kv, attn_w_q, attn_w_o, ffn_w_up, ffn_conv_w,
        ffn_conv_b, ffn_w_down, final_g,
    )
    return second_block(
        x, c_2, ctx_2, c_ctx_2, w_ada_2, b_ada_2, norm1_w_2, norm2_w_2, w_in_2, lam_qk_2,
        subln_w_2, lb_param_2, hgrn_norm_w_2, w_fnet_2, w_out_2, w_up_2, conv_w_2, conv_b_2,
        w_down_2, final_norm_w_2,
    )


_drawn_inputs = setup_inputs


def setup_inputs(seed=0):
    import zlib

    import numpy as np

    out = dict(_drawn_inputs(seed))
    spreads = {}
    factors = {'norm1_g': 3.443,
     'kv_norm_g': 6.249,
     'kv_ada_b': 8.0,
     'ffn_conv_b': 8.0,
     'norm1_w_2': 2.738,
     'lam_qk_2': 3.605,
     'subln_w_2': 4.532,
     'hgrn_norm_w_2': 8.0,
     'conv_b_2': 6.706,
     'norm2_w_2': 4.69}
    for name, (base, spread) in spreads.items():
        noise = np.random.default_rng([zlib.crc32(name.encode()), seed]).standard_normal(out[name].shape)
        drawn = base * np.exp(spread * noise) if base else spread * noise
        out[name] = __import__('jax').numpy.asarray(drawn.astype(out[name].dtype))
    for name, factor in factors.items():
        out[name] = (out[name] * factor).astype(out[name].dtype)
    return out
```

```python
import math
from contextlib import ExitStack

import numpy as np
import concourse.bass as bass
from concourse import mybir

F32 = mybir.dt.float32
F32R = mybir.dt.float32r
ALU = mybir.AluOpType
ACT = mybir.ActivationFunctionType
AX = mybir.AxisListType.X

P = 128
D = 1024
KT = D // P
TX, TC = 512, 256
TA = TX + TC
FF = 2816
FT = FF // P
NBR, NH1, HD = 3, 16, 64
EPS = 1e-6
ITEM = KT * 2 * P
FGROUPS = [(0, 8), (8, 8), (16, 6)]
BIG = 1.0e30
LAM0 = [0.8 - 0.6 * math.exp(-0.3 * li) for li in range(2)]
LEVELS = 7


class Columns:
    def __init__(self):
        self.at, self.n = {}, 0

    def add(self, name, n):
        self.at[name] = (self.n, n)
        self.n += n

    def __getitem__(self, name):
        return self.at[name][0]


def vector_columns():
    c = Columns()
    for name, n in (("c", 8), ("cc", 16), ("ada_b", 96), ("kv_ada_b", 16), ("b_ada", 96),
                    ("norm1_g", 16), ("norm2_g", 16), ("kv_norm_g", 8), ("final_g", 8), ("pool_scale", 8),
                    ("norm1_w", 16), ("norm2_w", 16), ("final_w", 8), ("conv1_b", 44), ("conv1_w", 132),
                    ("conv2_b", 88), ("conv2_w", 264), ("subln", 2), ("hgrn_w", 2), ("lam", 8), ("lb", 8)):
        c.add(name, n)
    return c


VC = vector_columns()
NVEC = VC.n


def work_columns():
    c = Columns()
    for name, n in (("cond", 8), ("condc", 16), ("mod1", 48), ("kvmod", 16), ("mod2", 96), ("gs", 16), ("gs2", 16),
                    ("lam", 8), ("lb", 24), ("mx", 16), ("nb", 16), ("sum", 16), ("rs", 16)):
        c.add(name, n)
    return c


WC = work_columns()


def weight_plan():
    plan = [("ada0", 24, 8), ("pool_in", 4, 8), ("grp", 2, 4), ("pool_out", 4, 8)]
    plan += ffn_plan("f0")
    plan += [("ada1", 24, 8), ("kvada", 8, 8), ("wq", 12, 8), ("wk", 12, 8), ("wv0", 4, 8), ("wv1", 8, 8), ("wo", 4, 8)]
    plan += ffn_plan("f1")
    for li in range(2):
        plan += [(f"ada2_{li}", 24, 8), (f"in_{li}a", 4, 8), (f"in_{li}b", 5, 8), (f"in_{li}v", 3, 8),
                 (f"out_{li}", 4, 8)]
        plan += ffn_plan(f"g{li}")
    return plan


def ffn_plan(name):
    out = []
    for g, (_, n) in enumerate(FGROUPS):
        out += [(f"{name}up{g}", n, 8), (f"{name}down{g}", 4, n)]
    return out


PLAN = weight_plan()
N_ITEMS = sum(n for _, n, _ in PLAN)


class Signal:

    def __init__(self, handle):
        self.handle, self.n = handle, 0

    def after(self, count):
        was, self.n = self.n, self.n + count
        return was


class Step:

    def __init__(self, i, u):
        self.i, self.u = i, u
        self.l = i * 2 + u


class Stage:
    def __init__(self, base, n, kt):
        self.base, self.n, self.kt = base, n, kt


class Ahead:

    def __init__(self, s):
        self.i, self.u, self.l = s.i + 1, s.u, s.l + 2


def steps(eng, first, last, body):
    n = last - first
    if n >= 4:
        with eng.Fori(first // 2, last // 2) as i:
            for u in range(2):
                body(Step(i, u))
    else:
        for l in range(first, last - n % 2):
            body(Step(l // 2, l % 2))
    if n % 2:
        body(Step(last // 2, 0))


class Program:
    def __init__(self, nc, ctx, aps, out, upto=None):
        self.nc, self.ctx, self.aps, self.out, self.upto = nc, ctx, aps, out, upto
        self.item = 0
        self.kt_of = [kt for _, n, kt in PLAN for _ in range(n)]
        self.plan = list(PLAN)
        self.freed = {}
        self.place_memory()
        s = lambda name: Signal(ctx.enter_context(nc.semaphore(name)))
        self.landed = [ctx.enter_context(nc.semaphore(f"weights_landed{k}")) for k in range(2)]
        self.hi_split = s("hi_split")
        self.lo_split = s("lo_split")
        self.raw_used = s("raw_used")
        self.tiles_done = s("tiles_done")
        self.freed_act = s("freed_by_scalar")
        self.freed_dve = s("freed_by_vector")
        self.act_step = s("act_step")
        self.dve_step = s("dve_step")
        self.pe_step = s("pe_step")
        self.pool_step = s("pool_step")
        self.loaded = s("loaded")
        self.stored = [s(f"stored{k}") for k in range(2)]
        self.started = s("started")
        self.out_stored = s("out_stored")

    def place_memory(self):
        nc = self.nc
        self.cursor = (nc.sbuf_base + 31) // 32 * 32
        self.end = nc.sbuf_top // 32 * 32

        def sb(name, shape, dt=F32):
            at = self.cursor
            self.cursor += (int(np.prod(shape[1:])) * 4 + 31) // 32 * 32
            return nc.alloc_sbuf_tensor_at(name, shape, dt, offset=at)

        self.X = sb("x_res", [P, KT, TA])
        self.HH = sb("h_hi", [P, KT, TA], F32R)
        self.HL = sb("h_lo", [P, KT, TA], F32R)
        self.RAW = sb("w_raw", [P, 2, ITEM])
        self.split_at = self.cursor
        self.WH = sb("w_hi", [P, 2, ITEM], F32R)
        self.WL = sb("w_lo", [P, 2, ITEM], F32R)
        self.split_end = self.cursor
        self.VEC = sb("vec", [P, NVEC])
        self.WK = sb("work_vec", [P, WC.n])
        self.ONES = sb("ones", [P, P])
        self.IDENT = sb("ident", [P, P])
        self.HALF = sb("ones_by_half", [P, P])
        self.arena = self.cursor
        self.B = [self.ctx.enter_context(nc.psum_tensor(f"bank{k}", [P, 512], F32)) for k in range(8)]

    def region(self, stage, spec, start=None, end=None):
        at = self.arena if start is None else start
        end = self.end if end is None else end
        out = []
        for name, shape, dt in spec:
            size = int(np.prod(shape[1:])) * mybir.dt.size(dt)
            out.append(self.nc.alloc_sbuf_tensor_at(f"{stage}_{name}", shape, dt, offset=at))
            at += (size + 31) // 32 * 32
            assert at <= end, (stage, name, at - end)
        return out

    def vec(self, name, k=0, n=1):
        return self.VEC[:, VC[name] + k:VC[name] + k + n]

    def wk(self, name, k=0, n=1):
        return self.WK[:, WC[name] + k:WC[name] + k + n]

    def fetch(self, sync, m, kt, slot, wait=None):
        if wait is not None:
            sync.wait_ge(wait[0], wait[1])
        src = self.aps["weights"][bass.ds(m, 1), :, 0:kt * 256].rearrange("a p n -> p (a n)")
        sync.dma_start(self.RAW[:, slot, 0:kt * 256], src).then_inc(self.landed[slot], 16)

    def take(self, name):
        got, n, kt = self.plan.pop(0)
        assert got == name, (got, name)
        base = self.item
        self.item += n
        return base, n, kt

    def stream(self, sync, base, n, kt, signal, before):
        def one(s):
            self.fetch(sync, s.l + (base + 2), kt, (base + s.u) % 2, (signal.handle, s.l + (before + 1)))
        steps(sync, 0, n - 2, one)
        for l in (n, n + 1):
            m = base + l
            if m < N_ITEMS:
                self.fetch(sync, m, self.kt_of[m], m % 2, (signal.handle, before + l - 1))

    def wait_landed(self, eng, base, s):
        slot = (base + s.u) % 2
        eng.wait_ge(self.landed[slot], s.i * 16 + 16 * ((base + s.u) // 2 + 1))
        return slot

    def split_hi(self, act, st, s):
        slot = self.wait_landed(act, st.base, s)
        if not (isinstance(s.l, int) and s.l < 2):
            act.wait_ge(self.tiles_done.handle, s.l * st.tpi + (st.done0 - st.tpi))
        n = st.kt * 256
        act.activation(self.WH[:, slot, 0:n], self.RAW[:, slot, 0:n], ACT.Copy).then_inc(self.hi_split.handle, 1)

    def split_lo(self, dve, st, s):
        slot = (st.base + s.u) % 2
        dve.wait_ge(self.hi_split.handle, s.l + (st.hi0 + 1))
        n = st.kt * 256
        dve.tensor_tensor(self.WL[:, slot, 0:n], self.RAW[:, slot, 0:n], self.WH[:, slot, 0:n].bitcast(F32),
                          ALU.subtract).then_inc(self.lo_split.handle, 1)

    def product(self, st, block, pe_tile, tpi, act_epi=None, dve_epi=None, freed=None, distance=4,
                sync_extra=None, pool_epi=None, act_wait=True):
        st.tpi, st.done0 = tpi, self.tiles_done.after(tpi * st.n)
        st.hi0, st.lo0 = self.hi_split.after(st.n), self.lo_split.after(st.n)
        st.free0 = freed.after(tpi * st.n)
        done, n = self.tiles_done.handle, st.n

        @block.sync
        def _(sync):
            self.stream(sync, st.base, n, st.kt, self.lo_split, st.lo0)

        @block.scalar
        def _(act):
            def epi(s):
                if act_epi is not None:
                    act_epi(act, s)

            for l in (0, 1):
                self.split_hi(act, st, Step(0, l))

            def both(s):
                epi(s)
                self.split_hi(act, st, Ahead(s))
            steps(act, 0, n - 2, both)
            for l in (n - 2, n - 1):
                epi(Step(l // 2, l % 2))
            if sync_extra is not None:
                sync_extra(act)

        @block.vector
        def _(dve):
            def epi(s):
                if dve_epi is not None:
                    dve_epi(dve, s)

            for l in (0, 1):
                self.split_lo(dve, st, Step(0, l))

            def both(s):
                epi(s)
                self.split_lo(dve, st, Ahead(s))
            steps(dve, 0, n - 2, both)
            for l in (n - 2, n - 1):
                epi(Step(l // 2, l % 2))

        @block.tensor
        def _(pe):
            def item(s):
                slot = (st.base + s.u) % 2
                pe.wait_ge(self.lo_split.handle, s.l + (st.lo0 + 1))
                for t in range(tpi):
                    pe.wait_ge(freed.handle, s.l * tpi + (st.free0 + t + 1 - distance))
                    pe_tile(pe, slot, s, t).then_inc(done, 1)
            steps(pe, 0, n, item)

        if pool_epi is not None:
            @block.gpsimd
            def _(pool):
                pool_epi(pool)

    def three(self, pe, out, w, x, start, stop):
        (wh, wl), (xh, xl) = w, x
        pe.matmul(out, wh, xh, start=start, stop=False)
        pe.matmul(out, wh, xl, start=False, stop=False)
        return pe.matmul(out, wl, xh, start=False, stop=stop)

    def feature_tile(self, kt, hi, lo, ctx):
        def tile(pe, slot, s, t):
            parts = [(self.B[2 * s.u + t][:, :], 0, TX)]
            if ctx:
                parts.append((self.B[4 + 2 * s.u + t][:, 0:TC], TX, TA))
            for out, a, b in parts:
                for k in range(kt):
                    c = k * 256 + t * P
                    mm = self.three(pe, out, (self.WH[:, slot, c:c + P], self.WL[:, slot, c:c + P]),
                                    (hi[:, k, a:b], lo[:, k, a:b]), k == 0, k == kt - 1)
            return mm
        return tile

    def token_tile(self, blocks):
        def tile(pe, slot, s, t):
            for k in range(KT):
                c = k * 256
                x = (self.HH[:, k, blocks[t]], self.HL[:, k, blocks[t]])
                w = (self.WH[:, slot, c:c + 256], self.WL[:, slot, c:c + 256])
                (wh, wl), (xh, xl) = w, x
                pe.matmul(self.B[t][:, 0:256], xh, wh, start=k == 0, stop=False)
                pe.matmul(self.B[t][:, 0:256], xl, wh, start=False, stop=False)
                mm = pe.matmul(self.B[t][:, 0:256], xh, wl, start=False, stop=k == KT - 1)
            return mm
        return tile

    def act_ready(self, act):
        act.wait_ge(self.started.handle, 1)

    def begin(self):
        nc, a = self.nc, self.aps
        with nc.Block() as block:
            @block.sync
            def _(sync):
                for t, src in ((self.VEC[:, :], a["vectors"]), (self.IDENT[:, :], a["ident"]),
                               (self.HALF[:, :], a["half"]), (self.X[:, :, 0:TX], a["xT"]), (self.X[:, :, TX:TA], a["ctxT"])):
                    sync.dma_start(t, src).then_inc(self.loaded.handle, 16)
                for m in range(2):
                    self.fetch(sync, m, self.kt_of[m], m)

            n = self.loaded.after(80)

            @block.gpsimd
            def _(pool):
                pool.memset(self.ONES[:, :], 1.0)

            @block.vector
            def _(dve):
                dve.memset(self.wk("mx", 0, 16), 0.0).then_inc(self.freed_dve.handle, 8)

            @block.scalar
            def _(act):
                act.wait_ge(self.loaded.handle, n + 80)
                act.activation(self.wk("cond", 0, 8), self.vec("c", 0, 8), ACT.Silu).then_inc(self.freed_act.handle, 8)
                act.activation(self.wk("condc", 0, 16), self.vec("cc", 0, 16), ACT.Silu).then_inc(self.started.handle, 1)
                for k in range(2):
                    act.activation(self.wk("rs", k), self.vec("c", k), ACT.Copy).then_inc(self.stored[k].handle, 16)
        self.freed_dve.after(8)
        self.freed_act.after(8)
        self.started.after(1)
        for k in range(2):
            self.stored[k].after(16)

    def ada(self, name, cond, ncol, bias, dest):
        base, n, kt = self.take(name)
        used0 = self.raw_used.after(n)
        width = 2 * n * ncol
        with self.nc.Block() as block:
            @block.sync
            def _(sync):
                self.stream(sync, base, n, kt, self.raw_used, used0)

            @block.tensor
            def _(pe):
                def item(s):
                    slot = self.wait_landed(pe, base, s)
                    for t in range(2):
                        out = self.B[0][:, bass.ds((s.l * 2 + t) * ncol, ncol)]
                        for k in range(kt):
                            c = k * 256 + t * P
                            mm = pe.matmul(out, self.RAW[:, slot, c:c + P], self.wk(cond, k * ncol, ncol),
                                           start=k == 0, stop=k == kt - 1)
                    mm.then_inc(self.raw_used.handle, 1)
                steps(pe, 0, n, item)

            @block.vector
            def _(dve):
                dve.wait_ge(self.raw_used.handle, used0 + n)
                for j in range(ncol):
                    cols = slice(j, width, ncol)
                    dve.tensor_tensor(self.wk(dest, 0, width)[:, cols], self.B[0][:, cols],
                                      self.vec(*bias, 2 * n), ALU.add)

    def norm(self, g, mods=None, ctx=False, final=False):
        W = TA if ctx else TX
        spans = [(0, TX)] + ([(TX, TA)] if ctx else [])
        tag = f"norm{self.item}_{g[0]}"
        SQ, R = self.region(tag, [("sq", [P, KT, W], F32), ("rstd", [P, W], F32)])
        a0, d0, p0, g0 = (x.n for x in (self.act_step, self.dve_step, self.pe_step, self.pool_step))
        A, V, E, G = (x.handle for x in (self.act_step, self.dve_step, self.pe_step, self.pool_step))
        gs = [self.wk("gs", 0, 8), self.wk("gs2", 0, 8)]

        def mod(j, kind, k):
            col, stride = mods[j][kind], mods[j][2]
            return self.WK[:, col + stride * k:col + stride * k + 1]

        with self.nc.Block() as block:
            @block.scalar
            def _(act):
                for q in range(4):
                    act.activation(SQ[:, 2 * q:2 * q + 2, :], self.X[:, 2 * q:2 * q + 2, 0:W], ACT.Square).then_inc(A, 1)
                act.wait_ge(V, d0 + 2)
                act.activation(R[:, :], R[:, :], ACT.Sqrt).then_inc(A, 1)
                for k in range(KT):
                    act.wait_ge(V, d0 + 3 + k)
                    if final:
                        act.activation(self.X[:, k, 0:W], SQ[:, k, :], ACT.Copy, scale=self.vec(g[0], g[1] + k)).then_inc(A, 1)
                        continue
                    for j, (s, e) in enumerate(spans):
                        ins = act.activation(self.HH[:, k, s:e], SQ[:, k, s:e], ACT.Identity,
                                             scale=gs[j][:, k:k + 1], bias=mod(j, 0, k))
                    ins.then_inc(A, 1)

            @block.vector
            def _(dve):
                if not final:
                    for j in range(len(spans)):
                        col, stride = mods[j][1], mods[j][2]
                        dve.scalar_tensor_tensor(gs[j], self.WK[:, col:col + 8 * stride:stride], 1.0,
                                                 self.vec(g[0], g[1], 8), ALU.add, ALU.mult)
                for q in range(1, 4):
                    dve.wait_ge(A, a0 + q + 1)
                    dve.tensor_tensor(SQ[:, 0:2, :], SQ[:, 0:2, :], SQ[:, 2 * q:2 * q + 2, :], ALU.add)
                    dve.drain()
                dve.tensor_tensor(SQ[:, 0, :], SQ[:, 0, :], SQ[:, 1, :], ALU.add).then_inc(V, 1)
                dve.wait_ge(E, p0 + 1)
                for b, (s, e) in enumerate(spans):
                    dve.tensor_scalar(R[:, s:e], self.B[b][:, 0:e - s], 1.0 / D, EPS, ALU.mult, ALU.add)
                dve.drain()
                dve.reciprocal(R[:, :], R[:, :]).then_inc(V, 1)
                dve.wait_ge(A, a0 + 5)

                def scale(k):
                    dve.tensor_tensor(SQ[:, k, :], self.X[:, k, 0:W], R[:, :], ALU.mult).then_inc(V, 1)

                def low(k):
                    dve.wait_ge(A, a0 + 6 + k)
                    dve.wait_ge(G, g0 + 1 + k)
                    dve.tensor_tensor(self.HL[:, k, 0:W], SQ[:, k, :], self.HH[:, k, 0:W].bitcast(F32), ALU.subtract)
                for k in range(KT):
                    scale(k)
                    if not final and k >= 2:
                        low(k - 2)
                if not final:
                    low(KT - 2)
                    low(KT - 1)

            @block.tensor
            def _(pe):
                pe.wait_ge(V, d0 + 1)
                for b, (s, e) in enumerate(spans):
                    mm = pe.matmul(self.B[b][:, 0:e - s], self.ONES[:, :], SQ[:, 0, s:e], start=True, stop=True)
                mm.then_inc(E, 1)

            if not final:
                @block.gpsimd
                def _(pool):
                    for k in range(KT):
                        pool.wait_ge(A, a0 + 6 + k)
                        for j, (s, e) in enumerate(spans):
                            ins = pool.tensor_scalar(SQ[:, k, s:e], SQ[:, k, s:e], gs[j][:, k:k + 1], mod(j, 0, k),
                                                     ALU.mult, ALU.add)
                        ins.then_inc(G, 1)
        self.act_step.after(5 + KT)
        self.dve_step.after(2 + KT)
        self.pe_step.after(1)
        if not final:
            self.pool_step.after(KT)

    def residual_epilogue(self, st, gate, ctx):
        def epi(dve, s):
            for t in range(2):
                dve.wait_ge(self.tiles_done.handle, s.l * 2 + (st.done0 + t + 1))
                m = s.l * 2 + t
                outs = [(self.B[2 * s.u + t][:, :], 0, TX, gate[0])]
                if ctx:
                    outs.append((self.B[4 + 2 * s.u + t][:, 0:TC], TX, TA, gate[1]))
                for bank, a, b, (col, stride) in outs:
                    x = self.X[:, bass.ds(m, 1), a:b].rearrange("p a n -> p (a n)")
                    ins = dve.scalar_tensor_tensor(x, bank, self.WK[:, bass.ds(m * stride + col, 1)], x,
                                                   ALU.mult, ALU.add)
                ins.then_inc(self.freed_dve.handle, 1)
        return epi

    def add_product(self, name, gate, hi=None, lo=None, ctx=False):
        st = Stage(*self.take(name))
        hi, lo = (self.HH, self.HL) if hi is None else (hi, lo)
        with self.nc.Block() as block:
            self.product(st, block, self.feature_tile(st.kt, hi, lo, ctx), 2,
                         dve_epi=self.residual_epilogue(st, gate, ctx), freed=self.freed_dve)

    def plain_product(self, name, dest, first, ctx=False):
        st = Stage(*self.take(name))

        def epi(act, s):
            for t in range(2):
                act.wait_ge(self.tiles_done.handle, s.l * 2 + (st.done0 + t + 1))
                self.act_ready(act)
                d = dest[:, bass.ds(s.l * 2 + (first + t), 1), :].rearrange("p a n -> p (a n)")
                ins = act.activation(d[:, 0:TX], self.B[2 * s.u + t][:, :], ACT.Copy)
                if ctx:
                    ins = act.activation(d[:, TX:TA], self.B[4 + 2 * s.u + t][:, 0:TC], ACT.Copy)
                ins.then_inc(self.freed_act.handle, 1)
        with self.nc.Block() as block:
            self.product(st, block, self.feature_tile(st.kt, self.HH, self.HL, ctx), 2, act_epi=epi,
                         freed=self.freed_act)

    def ffn(self, name, gate, wcol, bcol, centered):
        ctx = centered and name == "g0"
        W = TA if ctx else TX
        spans = [(0, TX)] + ([(TX, TA)] if ctx else [])
        taps = 2 * FT if centered else FT
        GH, GL, CA, CV = self.region(name, [("g_hi", [P, 8, W], F32R), ("g_lo", [P, 8, W], F32R),
                                            ("conv_a", [P, 2, W], F32), ("conv_v", [P, 2, W], F32)])
        for g, (first, _) in enumerate(FGROUPS):
            st = Stage(*self.take(f"{name}up{g}"))
            a0, v0 = self.act_step.after(3 * st.n), self.dve_step.after(2 * st.n)
            A, V = self.act_step.handle, self.dve_step.handle

            def col(base, tap, s, half):
                return self.VEC[:, bass.ds(s.l + (base + taps * tap + half * FT + first), 1)]

            def banks(s, t):
                out = [(self.B[2 * s.u + t][:, :], 0, TX)]
                if ctx:
                    out.append((self.B[4 + 2 * s.u + t][:, 0:TC], TX, TA))
                return out

            def act_epi(act, s):
                act.wait_ge(self.tiles_done.handle, s.l * 2 + (st.done0 + 2))
                act.wait_ge(V, s.l * 2 + (v0 - 2))
                self.act_ready(act)
                here = 1 if centered else 2
                for t, dst in enumerate((CA, CV) if centered else (CA,)):
                    for bank, a, b in banks(s, t):
                        ins = act.activation(dst[:, s.u, a:b], bank, ACT.Identity, scale=col(wcol, here, s, t),
                                             bias=col(bcol, 0, s, t))
                ins.then_inc(A, 1)
                act.wait_ge(*((self.freed_dve.handle, s.l * 2 + (st.free0 + 2)) if centered else
                              (V, s.l * 2 + (v0 + 1))))
                act.activation(CA[:, s.u, :], CA[:, s.u, :], ACT.Silu).then_inc(A, 1)
                act.wait_ge(*((V, s.l * 2 + (v0 + 1)) if centered else
                              (self.freed_dve.handle, s.l * 2 + (st.free0 + 2))))
                self.act_ready(act)
                act.activation(GH[:, bass.ds(s.l, 1), :].rearrange("p a n -> p (a n)"), CA[:, s.u, :],
                               ACT.Copy).then_inc(A, 1)

            def dve_epi(dve, s):
                dve.wait_ge(A, s.l * 3 + (a0 + 1))
                for tap, back in (((0, 1), (2, -1)) if centered else ((1, 1), (0, 2))):
                    for t, dst in enumerate((CA, CV) if centered else (CA,)):
                        for bank, a, b in banks(s, t):
                            n = b - a
                            to = dst[:, s.u, a + max(back, 0):b + min(back, 0)]
                            ins = dve.scalar_tensor_tensor(to, bank[:, max(-back, 0):n - max(back, 0)],
                                                           col(wcol, tap, s, t), to, ALU.mult, ALU.add)
                    if back > 0 and not (back == 2):
                        dve.drain()
                if centered:
                    ins.then_inc(self.freed_dve.handle, 2)
                else:
                    ins.then_inc(V, 1)
                dve.wait_ge(A, s.l * 3 + (a0 + 2))
                if centered:
                    dve.tensor_tensor(CA[:, s.u, :], CA[:, s.u, :], CV[:, s.u, :], ALU.mult).then_inc(V, 1)
                else:
                    dve.tensor_tensor(CA[:, s.u, :], CA[:, s.u, :], self.B[2 * s.u + 1][:, :],
                                      ALU.mult).then_inc(self.freed_dve.handle, 2)
                dve.wait_ge(A, s.l * 3 + (a0 + 3))
                low = GL[:, bass.ds(s.l, 1), :].rearrange("p a n -> p (a n)")
                high = GH[:, bass.ds(s.l, 1), :].rearrange("p a n -> p (a n)")
                dve.tensor_tensor(low, CA[:, s.u, :], high.bitcast(F32), ALU.subtract).then_inc(V, 1)

            with self.nc.Block() as block:
                self.product(st, block, self.feature_tile(KT, self.HH, self.HL, ctx), 2, act_epi=act_epi,
                             dve_epi=dve_epi, freed=self.freed_dve)
            self.add_product(f"{name}down{g}", gate, GH, GL, ctx)

    def pool_mixer(self):
        U, CS, DF, RC, ON, PH, PL = self.region("pool", [
            ("u", [P, KT, TX], F32), ("csum", [P, 2, TX], F32), ("pooled", [P, 2, TX], F32), ("edge", [P, 4, 16], F32),
            ("ones", [P, TX], F32), ("p_hi", [P, KT, TX], F32R), ("p_lo", [P, KT, TX], F32R)])
        self.plain_product("pool_in", U, 0)
        a0, v0 = self.act_step.after(KT), self.dve_step.after(2 * KT)
        A, V = self.act_step.handle, self.dve_step.handle
        l0 = self.loaded.after(16)
        with self.nc.Block() as block:
            @block.sync
            def _(sync):
                sync.dma_start(RC[:, :, :], self.aps["pool_edge"]).then_inc(self.loaded.handle, 16)

            @block.vector
            def _(dve):
                dve.memset(ON[:, :], 1.0)
                dve.wait_ge(self.loaded.handle, l0 + 16)
                dve.drain()
                for k in range(KT):
                    w = 2 << (k // 2)
                    cs, df, u = CS[:, k % 2, :], DF[:, k % 2, :], U[:, k, :]
                    if k >= 2:
                        dve.wait_ge(A, a0 + k - 1)
                    dve.tensor_tensor_scan(cs, ON[:, :], u, 0.0, ALU.mult, ALU.add)
                    dve.drain()
                    dve.tensor_tensor(df[:, w:], cs[:, w:], cs[:, :-w], ALU.subtract)
                    dve.tensor_tensor(df[:, 0:w], cs[:, 0:w], RC[:, k // 2, 0:w], ALU.mult)
                    dve.drain()
                    dve.scalar_tensor_tensor(df[:, w:], df[:, w:], 1.0 / w, u[:, w:], ALU.mult, ALU.subtract)
                    dve.tensor_tensor(df[:, 0:w], df[:, 0:w], u[:, 0:w], ALU.subtract).then_inc(V, 1)
                    dve.wait_ge(A, a0 + k + 1)
                    dve.tensor_tensor(PL[:, k, :], df, PH[:, k, :].bitcast(F32), ALU.subtract).then_inc(V, 1)

            @block.scalar
            def _(act):
                for k in range(KT):
                    act.wait_ge(V, v0 + 2 * k + 1)
                    act.activation(PH[:, k, :], DF[:, k % 2, :], ACT.Copy).then_inc(A, 1)

        st = Stage(*self.take("grp"))
        TMP = CS

        def tile(pe, slot, s, t):
            T = 4 * s.u + t
            for k in range(2):
                c = (2 * t + k) * P
                mm = self.three(pe, self.B[t][:, :], (self.WH[:, slot, c:c + P], self.WL[:, slot, c:c + P]),
                                (PH[:, 2 * (T // 2) + k, :], PL[:, 2 * (T // 2) + k, :]), k == 0, k == 1)
            return mm

        a1, v1 = self.act_step.after(8), self.dve_step.after(8)

        def act_epi(act, s):
            for t in range(4):
                T = 4 * s.u + t
                act.wait_ge(self.tiles_done.handle, st.done0 + T + 1)
                if T >= 2:
                    act.wait_ge(V, v1 + T - 1)
                scale = self.vec("pool_scale", T)
                act.activation(self.HH[:, T, 0:TX], self.B[t][:, :], ACT.Copy, scale=scale).then_inc(A, 1)
                act.activation(TMP[:, T % 2, :], self.B[t][:, :], ACT.Copy, scale=scale).then_inc(self.freed_act.handle, 1)

        def dve_epi(dve, s):
            for t in range(4):
                T = 4 * s.u + t
                dve.wait_ge(A, a1 + T + 1)
                dve.wait_ge(self.freed_act.handle, st.free0 + T + 1)
                dve.tensor_tensor(self.HL[:, T, 0:TX], TMP[:, T % 2, :], self.HH[:, T, 0:TX].bitcast(F32),
                                  ALU.subtract).then_inc(V, 1)
        with self.nc.Block() as block:
            self.product(st, block, tile, 4, act_epi=act_epi, dve_epi=dve_epi, freed=self.freed_act)
        self.add_product("pool_out", [(WC["mod1"] + 16, 1)])

    def spill_product(self, name, dram, tokens=None):
        st = Stage(*self.take(name))
        tpi = 2 if tokens is None else 4
        shape = [P, 2, 2, TX] if tokens is None else [P, 2, 4, 256]
        ST, = self.region(f"{name}_stage", [("out", shape, F32)], start=self.arena + 40960)
        s0 = [x.after(16 * ((st.n + 1 - k) // 2)) for k, x in enumerate(self.stored)]

        def epi(act, s):
            act.wait_ge(self.stored[s.u].handle, s.i * 16 + s0[s.u])
            for t in range(tpi):
                act.wait_ge(self.tiles_done.handle, s.l * tpi + (st.done0 + t + 1))
                src = self.B[2 * s.u + t][:, :] if tokens is None else self.B[t][:, 0:256]
                act.activation(ST[:, s.u, t, :], src, ACT.Copy).then_inc(self.freed_act.handle, 1)
            act.wait_ge(self.freed_act.handle, s.l * tpi + (st.free0 + tpi))
            if tokens is None:
                dst = dram[bass.ds(s.l * 2, 2), :, :].rearrange("t p n -> p t n")
            else:
                dst = dram[:, :, bass.ds(s.l * 256, 256)].rearrange("b p n -> p b n")
            act.dma_start(dst, ST[:, s.u, :, :]).then_inc(self.stored[s.u].handle, 16)

        tile = self.feature_tile(KT, self.HH, self.HL, False) if tokens is None else self.token_tile(tokens)
        with self.nc.Block() as block:
            self.product(st, block, tile, tpi, act_epi=epi, freed=self.freed_act)

    def dilated_attention(self, shift1, kvshift):
        nc = self.nc
        dram = lambda n, shape: nc.dram_tensor(n, shape, F32, kind="Internal").ap()
        q_d, k_d = dram("q_scratch", (24, P, TX)), dram("k_scratch", (24, P, TX))
        v0_d, v1_d = dram("v0_scratch", (4, P, D)), dram("v1_scratch", (4, P, 2 * D))
        self.norm(("norm1_g", 8), [(shift1, shift1 + 8, 1)])
        self.spill_product("wq", q_d)
        self.norm(("kv_norm_g", 0), [(kvshift, kvshift + 8, 1)])
        self.spill_product("wk", k_d)
        self.spill_product("wv0", v0_d, [slice(P * b, P * b + P) for b in range(4)])
        self.spill_product("wv1", v1_d, [slice(b, TX, 4) for b in range(4)])

        D0, D12, SL, Q, K, V, SC, E, PT = self.region("att1", [
            ("dist0", [P, 4, TX], F32), ("dist12", [P, 2, P], F32), ("slopes", [P, NBR * NH1], F32),
            ("q", [P, 2, NBR, TX], F32), ("k", [P, 2, NBR, TX], F32), ("v", [P, 2, NBR, 4, P], F32),
            ("scores", [P, 2, TA], F32), ("exps", [P, 2, TA], F32), ("turned", [P, 2, TA], F32)])
        sem = lambda name: self.ctx.enter_context(nc.semaphore(name))
        qkv = [sem(f"qkv_loaded{k}") for k in range(2)]
        scored, turned, summed = sem("scored"), sem("turned"), sem("values_summed")
        biased, maxed, normed = sem("biased"), sem("maxed"), sem("normed")
        exped, copied = sem("exped"), sem("copied")
        o_hi, o_lo = sem("o_hi"), sem("o_lo")
        scale = HD ** -0.5
        UNITS = 8
        l0 = self.loaded.after(48)
        stored = [x.n for x in self.stored]
        q_v, k_v = (d.rearrange("(g t) p n -> t p g n", g=NBR) for d in (q_d, k_d))

        with nc.Block() as block:
            @block.sync
            def _(sync):
                for t, name in ((D0[:, :, :], "dist0"), (D12[:, :, :], "dist12"), (SL[:, :], "slopes")):
                    sync.dma_start(t, self.aps[name]).then_inc(self.loaded.handle, 16)
                for k in range(2):
                    sync.wait_ge(self.stored[k].handle, stored[k])

                def load(hp, u):
                    one = lambda a: a[bass.ds(hp, 1)].rearrange("a p g n -> p (a g) n")
                    sync.dma_start(Q[:, u, :, :], one(q_v)).then_inc(qkv[u], 16)
                    sync.dma_start(K[:, u, :, :], one(k_v)).then_inc(qkv[u], 16)
                    for g in range(NBR):
                        src = v0_d if g == 0 else v1_d
                        col = hp * P + (D if g == 2 else 0)
                        sync.dma_start(V[:, u, g, :, :],
                                       src[:, :, bass.ds(col, P)].rearrange("b p n -> p b n")).then_inc(qkv[u], 16)
                for u in range(2):
                    load(u, u)
                with sync.Fori(0, 3) as i:
                    for u in range(2):
                        sync.wait_ge(summed, i * (2 * UNITS) + UNITS * (u + 1))
                        load(i * 2 + (2 + u), u)

            def unit(x):
                return x // UNITS, x % UNITS // 4, x % 4

            @block.tensor
            def _(pe):
                def scores(i, x):
                    u, h, c = unit(x)
                    a, b = HD * h, HD * h + HD
                    if x % UNITS == 0:
                        pe.wait_ge(qkv[u], i * 80 + 80)
                    pe.wait_ge(biased, i * 16 + (x + 1))
                    own = slice(c, TX, 4)
                    pe.matmul(self.B[x % 2][:, :], Q[a:b, u, 0, own], K[a:b, u, 0, :], start=True, stop=True)
                    for g in (1, 2):
                        lo = (g - 1) * P
                        mm = pe.matmul(self.B[2 + x % 2][:, lo:lo + P], Q[a:b, u, g, own], K[a:b, u, g, own],
                                       start=True, stop=True)
                    mm.then_inc(scored, 1)

                def turn(i, x):
                    pe.wait_ge(normed, i * 16 + (x + 1))
                    pe.wait_ge(copied, i * 16 + (x + 2))
                    for j in range(6):
                        bank, lo = (self.B[4], j * P) if j < 4 else (self.B[5], (j - 4) * P)
                        mm = pe.transpose(bank[:, lo:lo + P], E[:, x % 2, j * P:j * P + P], self.IDENT[:, :])
                    mm.then_inc(turned, 1)

                def values(i, x):
                    u, h, c = unit(x)
                    pe.wait_ge(copied, i * 16 + (x + 3))
                    if x % UNITS == 0:
                        pe.wait_ge(o_lo, i * 2 + (u + 1))
                    out = self.B[6 + u][HD * h:HD * h + HD, c * P:c * P + P]
                    for j in range(6):
                        g, b = (0, j) if j < 4 else (j - 3, c)
                        mm = pe.matmul(out, V[:, u, g, b, HD * h:HD * h + HD], PT[:, x % 2, j * P:j * P + P],
                                       start=j == 0, stop=j == 5)
                    mm.then_inc(summed, 1)

                with pe.Fori(0, 4) as i:
                    for x in range(18):
                        if x < 16:
                            scores(i, x)
                        if 1 <= x < 17:
                            turn(i, x - 1)
                        if x >= 2:
                            values(i, x - 2)

            @block.vector
            def _(dve):
                dve.memset(self.wk("sum", 0, 1), 0.0).then_inc(biased, 2)
                dve.memset(self.wk("sum", 1, 1), 0.0).then_inc(o_lo, 2)
                dve.wait_ge(self.loaded.handle, l0 + 48)

                def bias_max(i, x):
                    u, h, c = unit(x)
                    sl = lambda g: SL[:, bass.ds(i * 4 + (2 * u + h + NH1 * g), 1)]
                    p = x % 2
                    dve.wait_ge(scored, i * 16 + (x + 1))
                    dve.wait_ge(exped, i * 16 + (x + 1))
                    dve.scalar_tensor_tensor(SC[:, p, 0:TX], D0[:, c, :], sl(0), self.B[p][:, :], ALU.mult, ALU.add)
                    for g in (1, 2):
                        lo = (g - 1) * P
                        ins = dve.scalar_tensor_tensor(SC[:, p, TX + lo:TX + lo + P], D12[:, g - 1, :], sl(g),
                                                       self.B[2 + p][:, lo:lo + P], ALU.mult, ALU.add)
                    ins.then_inc(biased, 1)
                    dve.drain()
                    dve.reduce_max(self.wk("mx", p), SC[:, p, :], AX)
                    dve.drain()
                    dve.tensor_scalar(self.wk("nb", p), self.wk("mx", p), -scale, None, ALU.mult).then_inc(maxed, 1)

                def normalise(i, x):
                    p = x % 2
                    dve.wait_ge(exped, i * 16 + (x + 3))
                    dve.reciprocal(self.wk("rs", p), self.wk("sum", p))
                    dve.drain()
                    dve.tensor_scalar(E[:, p, :], E[:, p, :], self.wk("rs", p), None, ALU.mult).then_inc(normed, 1)

                with dve.Fori(0, 4) as i:
                    for x in range(17):
                        if x < 16:
                            bias_max(i, x)
                        if x >= 1:
                            normalise(i, x - 1)
                    for u in range(2):
                        dve.wait_ge(o_hi, i * 2 + (u + 1))
                        src = self.B[6 + u][:, :].rearrange("p (c j) -> p c j", c=4)
                        one = lambda t: t[:, bass.ds(i * 2 + u, 1), 0:TX].rearrange("p a (j c) -> p c (a j)", c=4)
                        dve.tensor_tensor(one(self.HL), src, one(self.HH).bitcast(F32), ALU.subtract).then_inc(o_lo, 1)

            @block.scalar
            def _(act):
                act.activation(self.wk("rs", 2, 1), self.ONES[:, 0:1], ACT.Copy).then_inc(exped, 2)
                act.activation(self.wk("rs", 3, 1), self.ONES[:, 0:1], ACT.Copy).then_inc(copied, 2)

                def exp(i, x):
                    p = x % 2
                    act.wait_ge(maxed, i * 16 + (x + 1))
                    if x >= 2:
                        act.wait_ge(turned, i * 16 + (x - 1))
                    act.activation(E[:, p, :], SC[:, p, :], ACT.Exp, scale=scale, bias=self.wk("nb", p),
                                   accum_out=self.wk("sum", p)).then_inc(exped, 1)

                def copy(i, x):
                    p = x % 2
                    act.wait_ge(turned, i * 16 + (x + 1))
                    if x >= 2:
                        act.wait_ge(summed, i * 16 + (x - 1))
                    act.activation(PT[:, p, 0:TX], self.B[4][:, :], ACT.Copy)
                    act.activation(PT[:, p, TX:TA], self.B[5][:, 0:256], ACT.Copy).then_inc(copied, 1)

                with act.Fori(0, 4) as i:
                    for x in range(17):
                        if x < 16:
                            exp(i, x)
                        if x >= 1:
                            copy(i, x - 1)
                    for u in range(2):
                        act.wait_ge(summed, i * 16 + UNITS * (u + 1))
                        self.act_ready(act)
                        src = self.B[6 + u][:, :].rearrange("p (c j) -> p c j", c=4)
                        dst = self.HH[:, bass.ds(i * 2 + u, 1), 0:TX].rearrange("p a (j c) -> p c (a j)", c=4)
                        act.activation(dst, src, ACT.Copy).then_inc(o_hi, 1)

    def token_product(self, name, dest):
        st = Stage(*self.take(name))
        nb = TA // P

        def epi(act, s):
            for t in range(nb):
                act.wait_ge(self.tiles_done.handle, s.l * nb + (st.done0 + t + 1))
                self.act_ready(act)
                act.activation(dest[:, t, bass.ds(s.l * 256, 256)], self.B[t][:, 0:256],
                               ACT.Copy).then_inc(self.freed_act.handle, 1)
        with self.nc.Block() as block:
            self.product(st, block, self.token_tile([slice(P * b, P * b + P) for b in range(nb)]), nb,
                         act_epi=epi, freed=self.freed_act, distance=nb)

    def rope(self, F, li):
        CS, PM, T = self.region(f"rope{li}", [("cos_sin", [P, 2, TX], F32), ("perm", [P, P], F32),
                                              ("tmp", [P, 2, TX], F32)], self.split_at, self.split_end)
        tiles = list(range(8, 12)) + list(range(4))
        l0, p0, v0 = self.loaded.after(32), self.pe_step.after(8), self.dve_step.after(8)
        with self.nc.Block() as block:
            @block.sync
            def _(sync):
                sync.dma_start(CS[:, :, :], self.aps["rope_cs"]).then_inc(self.loaded.handle, 16)
                sync.dma_start(PM[:, :], self.aps["rope_perm"]).then_inc(self.loaded.handle, 16)

            @block.tensor
            def _(pe):
                pe.wait_ge(self.loaded.handle, l0 + 32)
                for x, t in enumerate(tiles):
                    if x >= 4:
                        pe.wait_ge(self.dve_step.handle, v0 + x - 3)
                    pe.matmul(self.B[x % 4][:, :], PM[:, :], F[:, t, 0:TX], start=True,
                              stop=True).then_inc(self.pe_step.handle, 1)

            @block.vector
            def _(dve):
                dve.wait_ge(self.loaded.handle, l0 + 32)
                for x, t in enumerate(tiles):
                    dve.wait_ge(self.pe_step.handle, p0 + x + 1)
                    dve.tensor_tensor(T[:, x % 2, :], CS[:, 1, :], self.B[x % 4][:, :],
                                      ALU.mult).then_inc(self.dve_step.handle, 1)
                    dve.tensor_tensor(F[:, t, 0:TX], F[:, t, 0:TX], CS[:, 0, :], ALU.mult)
                    dve.drain()
                    dve.tensor_tensor(F[:, t, 0:TX], F[:, t, 0:TX], T[:, x % 2, :], ALU.add)

    def lambdas(self):
        pr, = self.region("lam", [("prod", [P, 16], F32)])
        V, A, E = (x.handle for x in (self.dve_step, self.act_step, self.pe_step))
        v0, a0, p0 = self.dve_step.after(3), self.act_step.after(3), self.pe_step.after(1)
        lam, lb = self.vec("lam", 0, 8), self.vec("lb", 0, 8)
        with self.nc.Block() as block:
            @block.vector
            def _(dve):
                dve.tensor_tensor(pr[:, 0:4], lam[:, 0:8:2], lam[:, 1:8:2], ALU.mult).then_inc(V, 1)
                dve.tensor_tensor(pr[:, 4:8], lb[:, 4:8], lb[:, 0:4], ALU.subtract)
                dve.drain()
                dve.scalar_tensor_tensor(pr[:, 8:12], pr[:, 4:8], -1.0, pr[:, 4:8], ALU.mult, ALU.min).then_inc(V, 1)
                dve.wait_ge(A, a0 + 2)
                dve.scalar_tensor_tensor(self.wk("lb", 0, 4), pr[:, 4:8], 0.0, pr[:, 12:16], ALU.min, ALU.subtract)
                dve.tensor_scalar(pr[:, 4:8], pr[:, 4:8], -1.0, 0.0, ALU.mult, ALU.min)
                dve.drain()
                dve.tensor_tensor(self.wk("lb", 4, 4), pr[:, 4:8], pr[:, 12:16], ALU.subtract)
                dve.drain()
                dve.tensor_tensor(self.wk("lb", 8, 4), self.wk("lb", 4, 4), self.wk("lb", 0, 4), ALU.subtract).then_inc(V, 1)
                dve.wait_ge(A, a0 + 3)
                dve.tensor_tensor(self.wk("lam", 2, 2), self.wk("lam", 4, 4)[:, 0:4:2], self.wk("lam", 4, 4)[:, 1:4:2],
                                  ALU.subtract)
                dve.drain()
                for li in range(2):
                    dve.tensor_scalar(self.wk("lam", li), self.wk("lam", 2 + li), LAM0[li], None, ALU.add)
                for li in range(2):
                    dve.tensor_scalar(self.vec("subln", li), self.vec("subln", li), 1.0 - LAM0[li], None, ALU.mult)

            @block.tensor
            def _(pe):
                pe.wait_ge(V, v0 + 1)
                pe.matmul(self.B[0][:, 0:4], self.ONES[:, :], pr[:, 0:4], start=True, stop=True).then_inc(E, 1)

            @block.scalar
            def _(act):
                act.wait_ge(V, v0 + 2)
                act.activation(pr[:, 12:16], pr[:, 8:12], ACT.Exp).then_inc(A, 1)
                act.wait_ge(A, a0 + 1)
                act.activation(pr[:, 12:16], pr[:, 12:16], ACT.Ln, bias=1.0).then_inc(A, 1)
                act.wait_ge(E, p0 + 1)
                act.activation(self.wk("lam", 4, 4), self.B[0][:, 0:4], ACT.Exp).then_inc(A, 1)

    def diff_attention(self, F, VT, li):
        nc = self.nc
        E, PT = self.region(f"att2_{li}", [("exps", [P, 2, 2, TA], F32), ("turned", [P, 2, TA], F32)],
                            self.split_at, self.split_end)
        units = [(h, b) for h in range(4) for b in range(4 if li else 6)]
        N = len(units)
        per = N // 4
        if li == 0:
            self.att2 = {n: Signal(self.ctx.enter_context(nc.semaphore(n))) for n in
                         ("d_scored", "d_turned", "d_summed", "d_maxed", "d_combined", "d_exped", "d_copied", "d_out")}
        q = self.att2
        S = {n: (x.handle, x.after({"d_scored": 2, "d_maxed": 2, "d_exped": 2}.get(n, 1) * (4 if n == "d_out" else N)))
             for n, x in q.items()}
        scale = HD ** -0.5

        def wait(eng, name, count):
            if count > 0:
                eng.wait_ge(S[name][0], S[name][1] + count)

        def parts(x):
            return ([(0, TX)] if units[x][1] < 4 else []) + [(TX, TA)]

        def blocks(x):
            return range(6) if units[x][1] < 4 else range(4, 6)

        with nc.Block() as block:
            @block.tensor
            def _(pe):
                def scores(x, c):
                    h, b = units[x]
                    wait(pe, "d_exped", 2 * (x - 1) + c + 1)
                    rows = slice(HD * c, HD * c + HD)
                    for lo, hi in parts(x):
                        bank = self.B[c] if lo == 0 else self.B[2 + c]
                        mm = pe.matmul(bank[:, 0:hi - lo], F[rows, 8 + h, b * P:b * P + P], F[rows, h, lo:hi],
                                       start=True, stop=True)
                    mm.then_inc(S["d_scored"][0], 1)

                def turn(x):
                    wait(pe, "d_combined", x + 1)
                    wait(pe, "d_copied", x)
                    for j in blocks(x):
                        bank, lo = (self.B[4], j * P) if j < 4 else (self.B[5], (j - 4) * P)
                        mm = pe.transpose(bank[:, lo:lo + P], E[:, x % 2, 0, j * P:j * P + P], self.IDENT[:, :])
                    mm.then_inc(S["d_turned"][0], 1)

                def values(x):
                    h, b = units[x]
                    wait(pe, "d_copied", x + 1)
                    if b == 0:
                        wait(pe, "d_out", h)
                    out = self.B[6][:, b * P:b * P + P] if b < 4 else self.B[7][:, (b - 4) * P:(b - 4) * P + P]
                    js = list(blocks(x))
                    for j in js:
                        mm = pe.matmul(out, VT[:, j, h * P:h * P + P], PT[:, x % 2, j * P:j * P + P],
                                       start=j == js[0], stop=j == js[-1])
                    mm.then_inc(S["d_summed"][0], 1)

                for x in range(N + 2):
                    if x < N:
                        scores(x, 0)
                        scores(x, 1)
                    if 1 <= x <= N:
                        turn(x - 1)
                    if x >= 2:
                        values(x - 2)

            @block.vector
            def _(dve):
                def maxima(x, c):
                    wait(dve, "d_scored", 2 * x + c + 1)
                    m = self.wk("mx", 2 * c, 2)
                    if len(parts(x)) == 2:
                        dve.reduce_max(m[:, 0:1], self.B[c][:, :], AX)
                        dve.reduce_max(m[:, 1:2], self.B[2 + c][:, 0:TC], AX)
                        dve.drain()
                        dve.tensor_tensor(m[:, 0:1], m[:, 0:1], m[:, 1:2], ALU.max)
                    else:
                        dve.reduce_max(m[:, 0:1], self.B[2 + c][:, 0:TC], AX)
                    dve.drain()
                    dve.tensor_scalar(self.wk("nb", 2 * (x % 2) + c), m[:, 0:1], -scale, None,
                                      ALU.mult).then_inc(S["d_maxed"][0], 1)

                def combine(x):
                    p = x % 2
                    wait(dve, "d_exped", 2 * x + 2)
                    sums = self.wk("sum", 4 * p, 4)
                    rs = self.wk("rs", 2 * p, 2)
                    if len(parts(x)) == 2:
                        dve.tensor_tensor(sums[:, 0:4:2], sums[:, 0:4:2], sums[:, 1:4:2], ALU.add)
                        dve.drain()
                        dve.reciprocal(rs, sums[:, 0:4:2])
                    else:
                        dve.reciprocal(rs, sums[:, 1:4:2])
                    dve.drain()
                    a, b = parts(x)[0][0], TA
                    dve.tensor_scalar(E[:, p, 1, a:b], E[:, p, 1, a:b], rs[:, 1:2], self.wk("lam", li),
                                      ALU.mult, ALU.mult)
                    dve.drain()
                    dve.scalar_tensor_tensor(E[:, p, 0, a:b], E[:, p, 0, a:b], rs[:, 0:1], E[:, p, 1, a:b],
                                             ALU.mult, ALU.subtract).then_inc(S["d_combined"][0], 1)
                for x in range(N + 1):
                    if x < N:
                        maxima(x, 0)
                        maxima(x, 1)
                    if x >= 1:
                        combine(x - 1)

            @block.scalar
            def _(act):
                def exps(x, c):
                    p = x % 2
                    wait(act, "d_maxed", 2 * x + c + 1)
                    wait(act, "d_turned", x - 1)
                    for lo, hi in parts(x):
                        bank = self.B[c] if lo == 0 else self.B[2 + c]
                        ins = act.activation(E[:, p, c, lo:hi], bank[:, 0:hi - lo], ACT.Exp, scale=scale,
                                             bias=self.wk("nb", 2 * p + c),
                                             accum_out=self.wk("sum", 4 * p + 2 * c + (lo > 0)))
                    ins.then_inc(S["d_exped"][0], 1)

                def copy(x):
                    wait(act, "d_turned", x + 1)
                    wait(act, "d_summed", x - 1)
                    for lo, hi in parts(x):
                        ins = act.activation(PT[:, x % 2, lo:hi], self.B[4 if lo == 0 else 5][:, 0:hi - lo], ACT.Copy)
                    ins.then_inc(S["d_copied"][0], 1)

                def head(h):
                    wait(act, "d_summed", per * (h + 1))
                    ins = act.activation(F[:, 8 + h, 0:TX], self.B[6][:, :], ACT.Copy)
                    if li == 0:
                        ins = act.activation(F[:, 8 + h, TX:TA], self.B[7][:, 0:TC], ACT.Copy)
                    ins.then_inc(S["d_out"][0], 1)

                for x in range(N + 2):
                    if x < N:
                        exps(x, 0)
                        exps(x, 1)
                    if 1 <= x <= N:
                        copy(x - 1)
                    if x >= 2 and (x - 2) % per == per - 1:
                        head((x - 2) // per)

    def head_norms(self, name, src, tiles, ones, inverse, weight, dest, W, gates=None):
        T1, RS = self.region(f"{name}_hn", [("a", [P, 2, TA], F32), ("r", [P, 2, TA], F32)],
                             self.split_at, self.split_end)
        G = None if gates is None else self.region(f"{name}_g", [("g", [P, 2, TA], F32)],
                                                   self.split_at + 16 * TA, self.split_end)[0]
        V, A, E = (x.handle for x in (self.dve_step, self.act_step, self.pe_step))
        n = len(tiles)
        v0, a0, p0 = self.dve_step.after(3 * n), self.act_step.after(4 * n), self.pe_step.after(n)
        spans = [(0, TX)] + ([(TX, TA)] if W == TA else [])
        with self.nc.Block() as block:
            @block.scalar
            def _(act):
                for x, t in enumerate(tiles):
                    p = x % 2
                    if x >= 2:
                        act.wait_ge(V, v0 + 3 * (x - 2) + 3)
                    act.activation(T1[:, p, 0:W], src[:, t, 0:W], ACT.Square).then_inc(A, 1)
                    act.wait_ge(V, v0 + 3 * x + 1)
                    act.activation(RS[:, p, 0:W], RS[:, p, 0:W], ACT.Sqrt).then_inc(A, 1)
                    if gates is not None:
                        act.activation(G[:, p, 0:W], gates[:, x, 0:W], ACT.Silu).then_inc(A, 1)
                    else:
                        act.activation(T1[:, p, 0:1], T1[:, p, 0:1], ACT.Copy).then_inc(A, 1)
                    act.wait_ge(V, v0 + 3 * x + 2)
                    act.activation(self.HH[:, dest + x, 0:W], T1[:, p, 0:W], ACT.Copy).then_inc(A, 1)

            @block.tensor
            def _(pe):
                for x in range(n):
                    pe.wait_ge(A, a0 + 4 * x + 1)
                    if x >= 2:
                        pe.wait_ge(V, v0 + 3 * (x - 2) + 1)
                    for b, (s, e) in enumerate(spans):
                        mm = pe.matmul(self.B[2 * (x % 2) + b][:, 0:e - s], ones, T1[:, x % 2, s:e],
                                       start=True, stop=True)
                    mm.then_inc(E, 1)

            @block.vector
            def _(dve):
                for x, t in enumerate(tiles):
                    p = x % 2
                    dve.wait_ge(E, p0 + x + 1)
                    for b, (s, e) in enumerate(spans):
                        dve.tensor_scalar(RS[:, p, s:e], self.B[2 * p + b][:, 0:e - s], inverse, EPS, ALU.mult, ALU.add)
                    dve.drain()
                    dve.reciprocal(RS[:, p, 0:W], RS[:, p, 0:W]).then_inc(V, 1)
                    dve.wait_ge(A, a0 + 4 * x + 3)
                    dve.scalar_tensor_tensor(T1[:, p, 0:W], src[:, t, 0:W], weight, RS[:, p, 0:W], ALU.mult, ALU.mult)
                    dve.drain()
                    if gates is not None:
                        dve.tensor_tensor(T1[:, p, 0:W], T1[:, p, 0:W], G[:, p, 0:W], ALU.mult).then_inc(V, 1)
                    else:
                        dve.memset(self.wk("sum", 15), 0.0).then_inc(V, 1)
                    dve.wait_ge(A, a0 + 4 * x + 4)
                    dve.tensor_tensor(self.HL[:, dest + x, 0:W], T1[:, p, 0:W], self.HH[:, dest + x, 0:W].bitcast(F32),
                                      ALU.subtract).then_inc(V, 1)

    def fourier(self, F, li):
        nb = 4 if li else 6
        CL, F64, WF, AB = self.region(f"four{li}", [
            ("dft", [P, 2, 4, TX], F32), ("dft64", [P, 2 * P], F32), ("w", [P, 2, 256], F32), ("ab", [P, nb, 2, 256], F32)],
            self.split_at, self.split_end)
        V, A, E = (x.handle for x in (self.dve_step, self.act_step, self.pe_step))
        segs = [(0, TX, [0, 1, 2, 3], 1)] + ([(TX, TA, [4, 5], 2)] if li == 0 else [])
        ns = len(segs)
        n_act = nb + 2 * ns + 2
        l0, p0, a0, v0 = self.loaded.after(48), self.pe_step.after(nb + 2 * ns + 2), self.act_step.after(n_act), self.dve_step.after(2)
        W = segs[-1][1]
        TMP, = self.region(f"four{li}t", [("t", [P, 1, TA], F32)], self.arena_tail, self.end)
        with self.nc.Block() as block:
            @block.sync
            def _(sync):
                sync.dma_start(CL[:, :, :, :], self.aps["dft"]).then_inc(self.loaded.handle, 16)
                sync.dma_start(F64[:, :], self.aps["dft64"]).then_inc(self.loaded.handle, 16)
                sync.dma_start(WF[:, :, :], self.aps["w_fnet"][li]).then_inc(self.loaded.handle, 16)

            @block.tensor
            def _(pe):
                pe.wait_ge(self.loaded.handle, l0 + 48)
                for b in range(nb):
                    if b >= 4:
                        pe.wait_ge(A, a0 + b - 3)
                    for j in range(2):
                        mm = pe.matmul(self.B[b % 4][:, 256 * j:256 * j + 256], F[:, 16 + j, b * P:b * P + P],
                                       F64[:, :], start=True, stop=True)
                    mm.then_inc(E, 1)
                for x, (s, e, bl, step) in enumerate(segs):
                    pe.wait_ge(A, a0 + nb)
                    for j in range(2):
                        for y, b in enumerate(bl):
                            for z in range(2):
                                mm = pe.matmul(self.B[4 + 2 * x + j][:, 0:e - s], AB[:, b, j, z * P:z * P + P],
                                               CL[:, z, y, 0:TX:step], start=(y, z) == (0, 0),
                                               stop=(y, z) == (len(bl) - 1, 1))
                        mm.then_inc(E, 1)
                pe.wait_ge(A, a0 + nb + 2 * ns)
                for m in range(2):
                    for x, (s, e, _, _) in enumerate(segs):
                        for j in range(2):
                            mm = pe.matmul(self.B[2 * m + x][:, 0:e - s], WF[:, j, m * P:m * P + P], F[:, 16 + j, s:e],
                                           start=j == 0, stop=j == 1)
                    mm.then_inc(E, 1)

            @block.scalar
            def _(act):
                for b in range(nb):
                    act.wait_ge(E, p0 + b + 1)
                    act.activation(AB[:, b, :, :].rearrange("p a n -> p (a n)"), self.B[b % 4][:, :], ACT.Copy).then_inc(A, 1)
                for x, (s, e, _, _) in enumerate(segs):
                    for j in range(2):
                        act.wait_ge(E, p0 + nb + 2 * x + j + 1)
                        act.activation(F[:, 16 + j, s:e], self.B[4 + 2 * x + j][:, 0:e - s], ACT.Copy,
                                       scale=((e - s) * 64.0) ** -0.5).then_inc(A, 1)
                for m in range(2):
                    act.wait_ge(E, p0 + nb + 2 * ns + m + 1)
                    if m == 1:
                        act.wait_ge(V, v0 + 1)
                    for x, (s, e, _, _) in enumerate(segs):
                        act.activation(self.HH[:, 6 + m, s:e], self.B[2 * m + x][:, 0:e - s], ACT.Copy)
                    for x, (s, e, _, _) in enumerate(segs):
                        ins = act.activation(TMP[:, 0, s:e], self.B[2 * m + x][:, 0:e - s], ACT.Copy)
                    ins.then_inc(A, 1)

            @block.vector
            def _(dve):
                for m in range(2):
                    dve.wait_ge(A, a0 + nb + 2 * ns + m + 1)
                    dve.tensor_tensor(self.HL[:, 6 + m, 0:W], TMP[:, 0, 0:W], self.HH[:, 6 + m, 0:W].bitcast(F32),
                                      ALU.subtract).then_inc(V, 1)

    def recurrence(self, F, VT, li):
        lat = li == 1
        nb = 4 if lat else 6
        W = nb * P
        NB = TA // P
        KS, T2, ST, TOT, ET = self.region(f"rec{li}", [
            ("ks", [P, 4, TA], F32), ("t2", [P, 4, TA], F32), ("states", [P, 2 * NB, 2, HD], F32),
            ("total", [P, 4, NB], F32), ("exptotal", [P, 4, NB], F32)], self.split_at, self.split_end)
        KTT, ACC = self.region(f"rec{li}k", [("kt", [P, NB, 2, 256], F32)], self.split_at + 16 * TA, self.split_end) + \
            self.region(f"rec{li}a", [("acc", [P, 2, nb // 2, 4, P], F32)], self.split_at + 16 * TA, self.split_end)
        DB, = self.region(f"rec{li}d", [("d", [P, 2, 2, TA], F32)], self.split_at, self.split_end)
        MK, = self.region(f"rec{li}m", [("masks", [P, 2 * LEVELS, P], mybir.dt.int32)], self.arena_tail, self.end)
        RM = KS[:, 0, :]
        Z, K, T1, Q = F[:, 4:8, :], F[:, 0:4, :], F[:, 8:12, :], F[:, 12:14, :]
        l0 = self.loaded.after(32)
        V, A, E, G = (x.handle for x in (self.dve_step, self.act_step, self.pe_step, self.pool_step))
        v0, a0, p0 = self.dve_step.n, self.act_step.n, self.pe_step.n
        second = 1 if li else 0
        a, c, ca = self.wk("lb", 0, 4), self.wk("lb", 4, 4), self.wk("lb", 8, 4)
        with self.nc.Block() as block:
            @block.sync
            def _(sync):
                sync.dma_start(MK[:, :, :], self.aps["level_masks"]).then_inc(self.loaded.handle, 16)
                sync.dma_start(RM, self.aps["block_reset"]).then_inc(self.loaded.handle, 16)

            @block.vector
            def _(dve):
                for t in range(4):
                    dve.scalar_tensor_tensor(T1[:, t, :], Z[:, t, :], -1.0, Z[:, t, :], ALU.mult, ALU.min).then_inc(V, 1)
                for t in range(4):
                    dve.wait_ge(A, a0 + 2 * t + 2)
                    dve.scalar_tensor_tensor(T1[:, t, :], Z[:, t, :], 0.0, T1[:, t, :], ALU.min, ALU.subtract)
                    dve.drain()
                    dve.tensor_tensor(K[:, t, :], T1[:, t, :], Z[:, t, :], ALU.subtract).then_inc(V, 1)
                if second:
                    for t in range(4):
                        dve.drain()
                        dve.tensor_scalar(Z[:, t, :], T1[:, t, :], ca[:, t:t + 1], None, ALU.add)
                        dve.drain()
                        dve.scalar_tensor_tensor(Z[:, t, :], Z[:, t, :], -1.0, Z[:, t, :], ALU.mult, ALU.min).then_inc(V, 1)
                        dve.tensor_scalar(T1[:, t, :], T1[:, t, :], c[:, t:t + 1], a[:, t:t + 1], ALU.add, ALU.max)
                dve.wait_ge(self.loaded.handle, l0 + 32)
                for t in range(4):
                    if second:
                        dve.wait_ge(A, a0 + 12 + 2 * t + 2)
                        dve.tensor_tensor(T1[:, t, :], T1[:, t, :], Z[:, t, :], ALU.add)
                    dve.drain()
                    dve.tensor_tensor_scan(Z[:, t, :], RM, T1[:, t, :], 0.0, ALU.mult, ALU.add)
                dve.drain()
                last = Z.rearrange("p t (b n) -> p t b n", n=P)[:, :, :, P - 1:P]
                dve.tensor_copy(TOT[:, :, :], last.rearrange("p t b n -> p t (b n)"))
                dve.drain()
                dve.tensor_tensor(Z[:, 2:4, :], Z[:, 2:4, :], T1[:, 2:4, :], ALU.subtract)
                dve.drain()
                for t in range(4):
                    view = lambda x: x[:, t, :].rearrange("p (b n) -> p b n", n=P)
                    dve.tensor_tensor(view(T2), TOT[:, t, :].rearrange("p (b n) -> p b n", n=1).to_broadcast([P, NB, P]),
                                      view(Z), ALU.subtract).then_inc(V, 1)
                n = v0 + 12 + 4 * second
                done = a0 + 12 + 8 * second
                dve.wait_ge(A, done + 9)
                dve.tensor_tensor(KS[:, 0:2, :], K[:, 0:2, :], T2[:, 0:2, :], ALU.mult).then_inc(V, 1)
                dve.tensor_tensor(KS[:, 2:4, :], K[:, 2:4, :], T1[:, 2:4, :], ALU.mult).then_inc(V, 1)
                dve.drain()
                dve.tensor_tensor(T1[:, 0:2, 0:W], Q[:, :, 0:W], T1[:, 0:2, 0:W], ALU.mult)
                dve.tensor_tensor(T1[:, 2:4, 0:W], Q[:, :, 0:W], T2[:, 2:4, 0:W], ALU.mult).then_inc(V, 1)
                for d in range(2):
                    dve.memset(ST[:, d * NB, :, :], 0.0)
                dve.wait_ge(E, p0 + 2 * NB)
                order = [[4, 5, 0, 1, 2, 3], [5, 4, 3, 2, 1, 0]]
                for pos in range(NB - 1):
                    dve.drain()
                    for d in range(2):
                        b = order[d][pos]
                        x = d * NB + b
                        for j in range(2):
                            u = self.B[x // 4][:, (x % 4) * P + j * HD:(x % 4) * P + j * HD + HD]
                            dve.scalar_tensor_tensor(ST[:, d * NB + pos + 1, j, :], ST[:, d * NB + pos, j, :],
                                                     ET[:, 2 * d + j, b:b + 1], u, ALU.mult, ALU.add)

            @block.scalar
            def _(act):
                for t in range(4):
                    act.wait_ge(V, v0 + t + 1)
                    act.activation(T1[:, t, :], T1[:, t, :], ACT.Exp).then_inc(A, 1)
                    act.wait_ge(A, a0 + 2 * t + 1)
                    act.activation(T1[:, t, :], T1[:, t, :], ACT.Ln, bias=1.0).then_inc(A, 1)
                for t in range(4):
                    act.wait_ge(V, v0 + 4 + t + 1)
                    act.activation(K[:, t, :], K[:, t, :], ACT.Exp, bias=c[:, t:t + 1] if second else 0.0).then_inc(A, 1)
                if second:
                    for t in range(4):
                        act.wait_ge(V, v0 + 8 + t + 1)
                        act.activation(Z[:, t, :], Z[:, t, :], ACT.Exp).then_inc(A, 1)
                        act.wait_ge(A, a0 + 12 + 2 * t + 1)
                        act.activation(Z[:, t, :], Z[:, t, :], ACT.Ln, bias=1.0).then_inc(A, 1)
                n = v0 + 8 + 4 * second
                for t in range(4):
                    act.wait_ge(V, n + t + 1)
                    act.activation(T2[:, t, :], T2[:, t, :], ACT.Exp).then_inc(A, 1)
                    act.activation(T1[:, t, :], Z[:, t, :], ACT.Exp).then_inc(A, 1)
                act.activation(ET[:, :, :], TOT[:, :, :], ACT.Exp).then_inc(A, 1)
                done = a0 + 12 + 8 * second + 9
                for b in range(NB):
                    act.wait_ge(E, p0 + b + 1)
                    if b == 0:
                        act.wait_ge(V, n + 4 + 3)
                    act.activation(KTT[:, b, :, :].rearrange("p a n -> p (a n)"), self.B[4 + b % 4][:, :],
                                   ACT.Copy).then_inc(A, 1)

            @block.tensor
            def _(pe):
                n = v0 + 12 + 4 * second
                done = a0 + 12 + 8 * second + 9
                pe.wait_ge(V, n + 2)
                for b in range(NB):
                    if b >= 4:
                        pe.wait_ge(A, done + b - 3)
                    for t in range(4):
                        mm = pe.transpose(self.B[4 + b % 4][:, t * P:t * P + P], KS[:, t, b * P:b * P + P], self.IDENT[:, :])
                    mm.then_inc(E, 1)
                for b in range(NB):
                    pe.wait_ge(A, done + b + 1)
                    for d in range(2):
                        x = d * NB + b
                        for h in range(4):
                            r, j = h % 2, h // 2
                            lo = (x % 4) * P + j * HD
                            mm = pe.matmul(self.B[x // 4][HD * r:HD * r + HD, lo:lo + HD], KTT[:, b, d, h * HD:h * HD + HD],
                                           VT[:, b, 2 * 256 + h * HD:2 * 256 + h * HD + HD], start=True, stop=True)
                    mm.then_inc(E, 1)
        self.dve_step.after(12 + 4 * second + 3)
        self.act_step.after(12 + 8 * second + 9 + NB)
        self.pe_step.after(2 * NB)

        jobs = [None] + [(lv, d) for lv in range(LEVELS) for d in range(2)]
        J = len(jobs)
        v0, a0, p0, g0 = self.dve_step.n, self.act_step.n, self.pe_step.n, self.pool_step.n
        if li == 0:
            self.read_out = Signal(self.ctx.enter_context(self.nc.semaphore("pairs_read_out")))
            self.paired = Signal(self.ctx.enter_context(self.nc.semaphore("pairs_done")))
        c0, s0 = self.read_out.after(J * nb), self.paired.after(J * nb)

        def halves(x, lv, tiles=None):
            m = 1 << lv
            v = x.rearrange("p t (n m) -> p t n m", m=2 * m)
            return v[:, :, :, 0:m], v[:, :, :, m:2 * m], v

        with self.nc.Block() as block:
            @block.gpsimd
            def _(pool):
                for n, job in enumerate(jobs):
                    if n >= 2:
                        pool.wait_ge(self.paired.handle, s0 + (n - 1) * nb)
                    if job is None:
                        pool.tensor_tensor(DB[:, 0, :, 0:W], K[:, 0:2, 0:W], K[:, 2:4, 0:W], ALU.add).then_inc(G, 1)
                        continue
                    lv, d = job
                    m = 1 << lv
                    cl, cr, cv = halves(Z[:, 2 * d:2 * d + 2, 0:W], lv)
                    dl, dr, _ = halves(DB[:, n % 2, :, 0:W], lv)
                    at = m - 1 if d == 0 else m
                    mid = cv[:, :, :, at:at + 1].to_broadcast([P, 2, W // (2 * m), m])
                    pool.tensor_tensor(dl, mid, cl, ALU.subtract)
                    pool.tensor_tensor(dr, cr, mid, ALU.subtract).then_inc(G, 1)

            @block.scalar
            def _(act):
                for n, job in enumerate(jobs):
                    if job is None:
                        continue
                    act.wait_ge(G, g0 + n + 1)
                    act.activation(DB[:, n % 2, :, 0:W], DB[:, n % 2, :, 0:W], ACT.Exp).then_inc(A, 1)

            @block.vector
            def _(dve):
                def decay(n):
                    lv, d = jobs[n]
                    dve.wait_ge(A, a0 + n)
                    xl, xr, _ = halves(DB[:, n % 2, :, 0:W], lv)
                    ql, qr, _ = halves(Q[:, :, 0:W], lv)
                    kl, kr, _ = halves(K[:, 2 * d:2 * d + 2, 0:W], lv)
                    dve.tensor_tensor(xl, xl, kl if d == 0 else ql, ALU.mult)
                    dve.tensor_tensor(xr, xr, qr if d == 0 else kr, ALU.mult).then_inc(V, 1)

                for n, job in enumerate(jobs):
                    if n + 1 < J:
                        decay(n + 1)
                    for y in range(nb):
                        dve.wait_ge(self.paired.handle, s0 + n * nb + y + 1)
                        acc = ACC[:, y % 2, y // 2, :, :]
                        bank = self.B[(n * nb + y) % 8][:, :].rearrange("p (a n) -> p a n", a=4)
                        if job is None:
                            every = self.IDENT[:, :].rearrange("p (a n) -> p a n", a=1).to_broadcast([P, 4, P])
                            ins = dve.tensor_tensor(acc, every, bank, ALU.mult)
                        else:
                            mask = MK[:, n - 1:n, :].to_broadcast([P, 4, P])
                            ins = dve.copy_predicated(acc, mask, bank)
                        ins.then_inc(self.read_out.handle, 1)
                    dve.drain()

            @block.tensor
            def _(pe):
                for n, job in enumerate(jobs):
                    if job is None:
                        pe.wait_ge(G, g0 + 1)
                    else:
                        pe.wait_ge(V, v0 + n)
                    for y in range(nb):
                        if n * nb + y >= 8:
                            pe.wait_ge(self.read_out.handle, c0 + n * nb + y - 7)
                        r, pair = y % 2, y // 2
                        rows = slice(HD * r, HD * r + HD)
                        for q in range(4):
                            b, j = 2 * pair + q // 2, q % 2
                            x = DB[rows, n % 2, j, b * P:b * P + P]
                            other = Q[rows, j, b * P:b * P + P] if job is None else x
                            mm = pe.matmul(self.B[(n * nb + y) % 8][:, q * P:q * P + P], x, other, start=True, stop=True)
                        mm.then_inc(self.paired.handle, 1)
        self.pool_step.after(J)
        self.act_step.after(J - 1)
        self.dve_step.after(J - 1)

        p0, a0 = self.pe_step.after(nb), self.act_step.after(nb)
        order = [[4, 5, 0, 1, 2, 3], [5, 4, 3, 2, 1, 0]]
        with self.nc.Block() as block:
            @block.tensor
            def _(pe):
                for b in range(nb):
                    if b >= 4:
                        pe.wait_ge(A, a0 + b - 3)
                    for h in range(4):
                        r, j = h % 2, h // 2
                        rows = slice(HD * r, HD * r + HD)
                        out = self.B[2 * (b % 4) + r][rows, j * P:j * P + P]
                        pe.matmul(out, VT[:, b, 512 + h * HD:512 + h * HD + HD], ACC[:, r, b // 2, 2 * (b % 2) + j, :],
                                  start=True, stop=False)
                        for d in range(2):
                            mm = pe.matmul(out, ST[rows, d * NB + order[d].index(b), j, :],
                                           T1[rows, 2 * d + j, b * P:b * P + P], start=False, stop=d == 1)
                    mm.then_inc(E, 1)

            @block.scalar
            def _(act):
                for b in range(nb):
                    act.wait_ge(E, p0 + b + 1)
                    for r in range(2):
                        rows = slice(HD * r, HD * r + HD)
                        src = self.B[2 * (b % 4) + r][rows, 0:256].rearrange("p (j n) -> p j n", j=2)
                        ins = act.activation(F[rows, 4:6, b * P:b * P + P], src, ACT.Copy)
                    ins.then_inc(A, 1)

    def second_block(self):
        m2 = WC["mod2"]
        self.lambdas()
        for li in range(2):
            ctx = li == 0

            def segs(q, scale=True):
                return [(m2 + 16 * q + j, m2 + 16 * q + 16 + j, 2) for j in range(2)]

            def gate(q):
                return [(m2 + 16 * q + j, 2) for j in range(2)]
            self.ada(f"ada2_{li}", "condc", 2, ("b_ada", 48 * li), "mod2")
            self.norm(("norm1_w", 8 * li), segs(0), ctx=True)
            F, VT = self.region(f"proj{li}", [("f", [P, 18, TA], F32), ("v", [P, TA // P, TA], F32)])
            self.arena_tail = self.arena + 18 * TA * 4 + TA // P * TA * 4
            self.plain_product(f"in_{li}a", F, 0, True)
            self.plain_product(f"in_{li}b", F, 8, ctx)
            self.token_product(f"in_{li}v", VT)
            self.rope(F, li)
            self.diff_attention(F, VT, li)
            W = TA if ctx else TX
            self.head_norms(f"a{li}", F, [8, 9, 10, 11], self.ONES[:, :], 1.0 / (2 * HD), self.vec("subln", li), 0, W)
            self.fourier(F, li)
            self.recurrence(F, VT, li)
            self.head_norms(f"r{li}", F, [4, 5], self.HALF[:, :], 1.0 / HD, self.vec("hgrn_w", li), 4, W,
                            gates=F[:, 14:16, :])
            if self.upto == f"cat{li}":
                return
            self.add_product(f"out_{li}", gate(2), ctx=ctx)
            if self.upto == f"mix{li}":
                return
            self.norm(("norm2_w", 8 * li), segs(3), ctx=ctx)
            self.ffn(f"g{li}", gate(5), VC["conv2_w"] + 132 * li, VC["conv2_b"] + 44 * li, True)
            if self.upto == f"b2_{li}":
                return
        self.norm(("final_w", 0), final=True)

    def finish(self):
        n = self.out_stored.after(16)
        with self.nc.Block() as block:
            @block.sync
            def _(sync):
                sync.dma_start(self.out, self.X[:, :, 0:TX]).then_inc(self.out_stored.handle, 16)
                sync.wait_ge(self.out_stored.handle, n + 16)

    def build(self):
        m1 = WC["mod1"]
        def stop(name):
            return self.upto == name
        self.begin()
        self.ada("ada0", "cond", 1, ("ada_b", 0), "mod1")
        self.norm(("norm1_g", 0), [(m1, m1 + 8, 1)])
        self.pool_mixer()
        if stop("pool"): return self.finish()
        self.norm(("norm2_g", 0), [(m1 + 24, m1 + 32, 1)])
        self.ffn("f0", [(m1 + 40, 1)], VC["conv1_w"], VC["conv1_b"], False)
        if stop("ffn0"): return self.finish()
        self.ada("ada1", "cond", 1, ("ada_b", 48), "mod1")
        self.ada("kvada", "cond", 1, ("kv_ada_b", 0), "kvmod")
        self.dilated_attention(m1, WC["kvmod"])
        self.add_product("wo", [(m1 + 16, 1)])
        if stop("attn"): return self.finish()
        self.norm(("norm2_g", 8), [(m1 + 24, m1 + 32, 1)])
        self.ffn("f1", [(m1 + 40, 1)], VC["conv1_w"] + 66, VC["conv1_b"] + 22, False)
        self.norm(("final_g", 0), final=True)
        if stop("first"): return self.finish()
        self.second_block()
        self.finish()


def program(nc, aps, out, upto=None):
    with ExitStack() as ctx:
        Program(nc, ctx, aps, out, upto).build()


def cols(v):
    v = np.asarray(v)
    return v.reshape(-1, P).T


def items(w, order=None):
    w = np.asarray(w)
    K, N = w.shape
    kt = K // P
    if order is not None:
        w = w.reshape(K, N // P, P)[:, order].reshape(K, -1)
        N = w.shape[1]
    out = w.reshape(kt, P, N // 256, 256).transpose(2, 1, 0, 3).reshape(N // 256, P, kt * 256)
    if kt < KT:
        out = np.concatenate([out, np.zeros((N // 256, P, ITEM - kt * 256), w.dtype)], axis=2)
    return out


def ffn_items(up, down):
    out = []
    pairs = [t for j in range(FT) for t in (j, FT + j)]
    both = items(up, pairs)
    for first, n in FGROUPS:
        out += [both[first:first + n], items(down[first * P:(first + n) * P])]
    return out


def group_items(w):
    w = np.asarray(w).reshape(4, 2, P, 2, P)
    w = w.transpose(0, 3, 2, 1, 4).reshape(2, 4, P, 2 * P)
    w = w.transpose(0, 2, 1, 3).reshape(2, P, 8 * P)
    return np.concatenate([w, np.zeros((2, P, ITEM - 8 * P), w.dtype)], axis=2)


def weight_array(g):
    w = [items(g["ada_w"][0]), items(g["pool_w_in"][0]), group_items(g["pool_w_grp"][0]), items(g["pool_w_out"][0])]
    w += ffn_items(g["ffn_w_up"][0], g["ffn_w_down"][0])
    kv = items(g["w_kv"])
    w += [items(g["ada_w"][1]), items(g["kv_ada_w"]), items(g["attn_w_q"][0]), kv[:12], kv[12:16], kv[16:24],
          items(g["attn_w_o"][0])]
    w += ffn_items(g["ffn_w_up"][1], g["ffn_w_down"][1])
    for li in range(2):
        w += [items(g["w_ada_2"][li]),
              items(g["w_in_2"][li], [4, 5, 6, 7, 14, 15, 16, 17, 0, 1, 2, 3, 12, 13, 20, 21, 22, 23, 8, 9, 10, 11, 18, 19]),
              items(g["w_out_2"][li])]
        w += ffn_items(g["w_up_2"][li], g["w_down_2"][li])
    out = np.concatenate(w)
    assert out.shape == (N_ITEMS, P, ITEM), (out.shape, N_ITEMS)
    return out


def vector_array(g):
    out = np.zeros((P, NVEC), np.float32)

    def put(name, a):
        at, n = VC.at[name]
        assert a.shape == (P, n), (name, a.shape, n)
        out[:, at:at + n] = a
    put("c", cols(g["c"]))
    put("cc", np.stack([cols(g["c_2"]), cols(g["c_ctx_2"])], axis=2).reshape(P, 16))
    for name, key in (("ada_b", "ada_b"), ("kv_ada_b", "kv_ada_b"), ("b_ada", "b_ada_2"), ("norm1_g", "norm1_g"),
                      ("norm2_g", "norm2_g"), ("kv_norm_g", "kv_norm_g"), ("final_g", "final_g"),
                      ("pool_scale", "pool_scale"), ("norm1_w", "norm1_w_2"), ("norm2_w", "norm2_w_2"),
                      ("final_w", "final_norm_w_2"), ("conv1_b", "ffn_conv_b"), ("conv1_w", "ffn_conv_w"),
                      ("conv2_b", "conv_b_2"), ("conv2_w", "conv_w_2"), ("subln", "subln_w_2"),
                      ("lb", "lb_param_2")):
        put(name, cols(g[key]))
    put("hgrn_w", np.concatenate([g["hgrn_norm_w_2"].T, g["hgrn_norm_w_2"].T]))
    lam = g["lam_qk_2"].transpose(2, 0, 1).reshape(64, 8)
    put("lam", np.concatenate([lam, np.zeros_like(lam)]))
    return out


def alibi_slopes(n):
    def pow2(m):
        start = 2.0 ** (-(2.0 ** -(math.log2(m) - 3)))
        return [start ** (i + 1) for i in range(m)]
    c = 2 ** math.floor(math.log2(n))
    s = pow2(c) if c == n else pow2(c) + pow2(2 * c)[0::2][: n - c]
    return -np.sort(-np.asarray(s, np.float32))


def constants():
    out = {"ident": np.eye(P, dtype=np.float32)}
    edge = np.zeros((4, 16), np.float32)
    for g in range(4):
        w = 2 << g
        edge[g] = 1.0 / np.minimum(np.arange(16) + 1, w)
    key = np.arange(TX)
    dist = np.full((P, 4, TX), BIG, np.float32)
    for c in range(4):
        back = (4 * np.arange(P) + c)[:, None] - key[None]
        ok = (back >= 0) & (back <= 128)
        dist[:, c][ok] = back[ok]
    back = np.arange(P)[:, None] - np.arange(P)[None]
    near = np.full((P, 2, P), BIG, np.float32)
    near[:, 0][back >= 0] = 4.0 * back[back >= 0]
    ok = (back >= 0) & (back % 4 == 0)
    near[:, 1][ok] = 4.0 * back[ok]
    out["dist0"], out["dist12"] = dist, near
    out["slopes"] = np.broadcast_to(-alibi_slopes(NBR * NH1) * HD ** 0.5, (P, NBR * NH1)).astype(np.float32)
    masks = np.zeros((P, 2 * LEVELS, P), np.int32)
    a, b = np.arange(P)[:, None], np.arange(P)[None]
    for lv in range(LEVELS):
        same = a >> (lv + 1) == b >> (lv + 1)
        for d in range(2):
            masks[:, 2 * lv + d] = same & ((a >> lv & 1) == d) & ((b >> lv & 1) == 1 - d)
    out["level_masks"] = masks
    out["block_reset"] = np.broadcast_to((np.arange(TA) % P != 0).astype(np.float32), (P, TA)).copy()
    out["half"] = np.kron(np.eye(2), np.ones((HD, HD))).astype(np.float32)
    inv = 10000.0 ** (-np.arange(0, 32, 2, dtype=np.float32) / np.float32(32))
    t = np.arange(TX)
    ang_r = (t // 64).astype(np.float32)[:, None] * inv.astype(np.float32)
    ang_c = (t % 64).astype(np.float32)[:, None] * inv.astype(np.float32)
    ang = np.concatenate([ang_r, ang_r, ang_c, ang_c] * 2, axis=1).T
    out["rope_cs"] = np.stack([np.cos(ang), np.sin(ang)], axis=1).astype(np.float32)
    perm = np.zeros((P, P), np.float32)
    for lo in range(0, P, 32):
        for i in range(16):
            perm[lo + i + 16, lo + i] = -1.0
            perm[lo + i, lo + i + 16] = 1.0
    out["rope_perm"] = perm
    n = np.arange(TX)
    ang = 2 * np.pi * (np.outer(n, n) % TX) / TX
    out["dft"] = np.stack([np.cos(ang), -np.sin(ang)]).reshape(2, 4, P, TX).transpose(2, 0, 1, 3).astype(np.float32)
    n = np.arange(64)
    ang = 2 * np.pi * (np.outer(n, n) % 64) / 64
    out["dft64"] = np.concatenate([np.kron(np.eye(2), np.cos(ang)), np.kron(np.eye(2), np.sin(ang))], axis=1).astype(np.float32)
    out["pool_edge"] = np.broadcast_to(edge, (P, 4, 16)).copy()
    return out


def host_inputs(g):
    g = {k: np.asarray(v) for k, v in g.items()}
    return {
        "weights": weight_array(g), "vectors": vector_array(g),
        "xT": np.ascontiguousarray(g["x"][0].T.reshape(KT, P, TX).transpose(1, 0, 2)),
        "ctxT": np.ascontiguousarray(g["ctx_2"][0].T.reshape(KT, P, TC).transpose(1, 0, 2)),
        "w_fnet": np.ascontiguousarray(g["w_fnet_2"].reshape(2, 2, P, 256).transpose(0, 2, 1, 3)),
        **constants(),
    }


def kernel(**inputs):
    import concourse.bacc as bacc
    from concourse.bass_utils import run_bass_kernel_spmd

    nc = bacc.Bacc("TRN2", target_bir_lowering=False, num_devices=1)
    arrays = host_inputs(inputs)
    aps = {n: nc.dram_tensor(n, a.shape, mybir.dt.from_np(a.dtype), kind="ExternalInput").ap()
           for n, a in arrays.items()}
    out = nc.dram_tensor("out", (P, KT, TX), F32, kind="ExternalOutput").ap()
    program(nc, aps, out)
    r = run_bass_kernel_spmd(nc, [arrays], core_ids=[0])
    y = r.results[0]["out"]
    return np.ascontiguousarray(y.transpose(1, 0, 2).reshape(D, TX).T)[None]
```

```python
import math
from contextlib import ExitStack

import numpy as np
import concourse.bass as bass
from concourse import mybir

F32 = mybir.dt.float32
F32R = mybir.dt.float32r
ALU = mybir.AluOpType
ACT = mybir.ActivationFunctionType
AX = mybir.AxisListType.X

P = 128
D = 1024
KT = D // P
TX, TC = 512, 256
TA = TX + TC
FF = 2816
FT = FF // P
NBR, NH1, HD = 3, 16, 64
EPS = 1e-6
ITEM = KT * 2 * P
FGROUPS = [(0, 8), (8, 8), (16, 6)]
BIG = 1.0e30
LAM0 = [0.8 - 0.6 * math.exp(-0.3 * li) for li in range(2)]
LEVELS = 7


class Columns:
    def __init__(self):
        self.at, self.n = {}, 0

    def add(self, name, n):
        self.at[name] = (self.n, n)
        self.n += n

    def __getitem__(self, name):
        return self.at[name][0]


def vector_columns():
    c = Columns()
    for name, n in (("c", 8), ("cc", 16), ("ada_b", 96), ("kv_ada_b", 16), ("b_ada", 96),
                    ("norm1_g", 16), ("norm2_g", 16), ("kv_norm_g", 8), ("final_g", 8), ("pool_scale", 8),
                    ("norm1_w", 16), ("norm2_w", 16), ("final_w", 8), ("conv1_b", 44), ("conv1_w", 132),
                    ("conv2_b", 88), ("conv2_w", 264), ("subln", 2), ("hgrn_w", 2), ("lam", 8), ("lb", 8)):
        c.add(name, n)
    return c


VC = vector_columns()
NVEC = VC.n


def work_columns():
    c = Columns()
    for name, n in (("cond", 8), ("condc", 16), ("mod1", 48), ("mod1b", 48), ("kvmod", 16), ("mod2", 96), ("mod2b", 96), ("gs", 16), ("gs2", 16),
                    ("lam", 8), ("lb", 24), ("mx", 16), ("nb", 16), ("sum", 16), ("rs", 16)):
        c.add(name, n)
    return c


WC = work_columns()


def weight_plan():
    plan = [("pool_in", 4, 8), ("grp", 2, 4), ("pool_out", 4, 8)]
    plan += ffn_plan("f0")
    plan += [("wq", 12, 8), ("wk", 12, 8), ("wv0", 4, 8), ("wv1", 8, 8), ("wo", 4, 8)]
    plan += ffn_plan("f1")
    for li in range(2):
        plan += [(f"in_{li}a", 4, 8), (f"in_{li}b", 5, 8), (f"in_{li}v", 3, 8),
                 (f"out_{li}", 4, 8)]
        plan += ffn_plan(f"g{li}")
    return plan


def ffn_plan(name):
    out = []
    for g, (_, n) in enumerate(FGROUPS):
        out += [(f"{name}up{g}", n, 8), (f"{name}down{g}", 4, n)]
    return out


PLAN = weight_plan()
N_ITEMS = sum(n for _, n, _ in PLAN)
MODS = [("first", 16), ("shift", 4), ("scale", 4), ("ada1", 24), ("kvada", 8), ("ada2_0", 24), ("ada2_1", 24)]
MOD_BASE = {name: sum(n for _, n in MODS[:k]) for k, (name, _) in enumerate(MODS)}
N_MODS = sum(n for _, n in MODS)


class Signal:

    def __init__(self, handle):
        self.handle, self.n = handle, 0

    def after(self, count):
        was, self.n = self.n, self.n + count
        return was


class Step:

    def __init__(self, i, u):
        self.i, self.u = i, u
        self.l = i * 2 + u


class Ready:

    def __init__(self, handle, first, step):
        self.handle, self.first, self.step = handle, first, step

    def at(self, k):
        return self.first + self.step * k


class Stage:
    def __init__(self, base, n, kt):
        self.base, self.n, self.kt = base, n, kt


class Rider:

    def __init__(self, name, cond, ncol, runs):
        self.name, self.cond, self.ncol, self.runs = name, cond, ncol, runs
        self.base, self.n = MOD_BASE[name], dict(MODS)[name]
        self.k = 0


class Next:

    def __init__(self, s):
        self.i, self.u, self.l = s.i + s.u, 1 - s.u, s.l + 1


class Ahead:

    def __init__(self, s):
        self.i, self.u, self.l = s.i + 1, s.u, s.l + 2


def steps(eng, first, last, body):
    n = last - first
    if n >= 4:
        with eng.Fori(first // 2, last // 2) as i:
            for u in range(2):
                body(Step(i, u))
    else:
        for l in range(first, last - n % 2):
            body(Step(l // 2, l % 2))
    if n % 2:
        body(Step(last // 2, 0))


class Program:
    def __init__(self, nc, ctx, aps, out, upto=None):
        self.nc, self.ctx, self.aps, self.out, self.upto = nc, ctx, aps, out, upto
        self.pre = 0
        self.riders_done = []
        self.item = 0
        self.kt_of = [kt for _, n, kt in PLAN for _ in range(n)]
        self.plan = list(PLAN)
        self.freed = {}
        self.place_memory()
        s = lambda name: Signal(ctx.enter_context(nc.semaphore(name)))
        self.landed = [ctx.enter_context(nc.semaphore(f"weights_landed{k}")) for k in range(2)]
        self.hi_split = s("hi_split")
        self.lo_split = s("lo_split")
        self.raw_used = s("raw_used")
        self.mods_landed = [ctx.enter_context(nc.semaphore(f"mods_landed{k}")) for k in range(4)]
        self.ride_landed = [s(f"ride_landed{k}") for k in range(2)]
        self.ride_shared = s("ride_shared")
        self.ride_added = s("ride_added")
        self.ride_summed = s("ride_summed")
        self.tiles_done = s("tiles_done")
        self.freed_act = s("freed_by_scalar")
        self.freed_dve = s("freed_by_vector")
        self.act_step = s("act_step")
        self.dve_step = s("dve_step")
        self.pe_step = s("pe_step")
        self.pool_step = s("pool_step")
        self.loaded = s("loaded")
        self.stored = [s(f"stored{k}") for k in range(2)]
        self.started = s("started")
        self.out_stored = s("out_stored")

    def place_memory(self):
        nc = self.nc
        self.cursor = (nc.sbuf_base + 31) // 32 * 32
        self.end = nc.sbuf_top // 32 * 32

        def sb(name, shape, dt=F32):
            at = self.cursor
            self.cursor += (int(np.prod(shape[1:])) * 4 + 31) // 32 * 32
            return nc.alloc_sbuf_tensor_at(name, shape, dt, offset=at)

        self.X = sb("x_res", [P, KT, TA])
        self.HH = sb("h_hi", [P, KT, TA], F32R)
        self.HL = sb("h_lo", [P, KT, TA], F32R)
        self.RAW = sb("w_raw", [P, 2, ITEM])
        self.split_at = self.cursor
        self.WH = sb("w_hi", [P, 2, ITEM], F32R)
        self.WL = sb("w_lo", [P, 2, ITEM], F32R)
        self.split_end = self.cursor
        self.VEC = sb("vec", [P, NVEC])
        self.WK = sb("work_vec", [P, WC.n])
        self.ONES = sb("ones", [P, P])
        self.IDENT = sb("ident", [P, P])
        self.HALF = sb("ones_by_half", [P, P])
        self.arena = self.cursor
        self.ride_at = self.end - 2 * ITEM * 4 - 4 * 256 * 4
        self.RIDE = nc.alloc_sbuf_tensor_at("ride_raw", [P, 2, ITEM], F32, offset=self.ride_at)
        self.RACC = nc.alloc_sbuf_tensor_at("ride_acc", [P, 2, 2, 256], F32, offset=self.ride_at + 2 * ITEM * 4)
        self.B = [self.ctx.enter_context(nc.psum_tensor(f"bank{k}", [P, 512], F32)) for k in range(8)]

    def region(self, stage, spec, start=None, end=None):
        at = self.arena if start is None else start
        end = self.end if end is None else end
        out = []
        for name, shape, dt in spec:
            size = int(np.prod(shape[1:])) * mybir.dt.size(dt)
            out.append(self.nc.alloc_sbuf_tensor_at(f"{stage}_{name}", shape, dt, offset=at))
            at += (size + 31) // 32 * 32
            assert at <= end, (stage, name, at - end)
        return out

    def vec(self, name, k=0, n=1):
        return self.VEC[:, VC[name] + k:VC[name] + k + n]

    def wk(self, name, k=0, n=1):
        return self.WK[:, WC[name] + k:WC[name] + k + n]

    def fetch(self, sync, m, kt, slot, wait=None):
        if wait is not None:
            sync.wait_ge(wait[0], wait[1])
        src = self.aps["weights"][bass.ds(m, 1), :, 0:kt * 256].rearrange("a p n -> p (a n)")
        sync.dma_start(self.RAW[:, slot, 0:kt * 256], src).then_inc(self.landed[slot], 16)

    def take(self, name):
        got, n, kt = self.plan.pop(0)
        assert got == name, (got, name)
        base = self.item
        self.item += n
        return base, n, kt

    def stream(self, sync, st, rider, ride):
        lo, n = self.lo_split.handle, st.n

        def one(s):
            self.fetch(sync, s.l + (st.base + 2), st.kt, (st.base + s.u) % 2, (lo, s.l + (st.lo0 + 1)))

        def both(s):
            one(s)
            self.ride_fetch(sync, rider, s, 2)
        first, last = st.pre, max(st.pre, n - 2)
        if ride:
            if rider.k == 0:
                for l in range(2):
                    self.ride_fetch(sync, rider, Step(0, l), 0)
            for l in range(0, first):
                self.ride_fetch(sync, rider, Step(0, l), 2)
            mid = ride - 2
            steps(sync, first, mid, both)
            if mid < last:
                steps(sync, mid, last, one)
            first = last
        else:
            steps(sync, first, last, one)
        for l in range(last, n + st.post):
            m = st.base + l + 2
            if m < N_ITEMS:
                self.fetch(sync, m, self.kt_of[m], m % 2, (lo, st.lo0 + l + 1))
            if ride == n and l < n and rider.k + l + 2 < rider.n:
                self.ride_fetch(sync, rider, Step(l // 2, l % 2), 2)

    def split_hi(self, act, st, s, kt=None):
        slot = (st.base + s.u) % 2
        act.wait_ge(self.landed[slot], s.i * 16 + 16 * ((st.base + s.u) // 2 + 1))
        if not (isinstance(s.l, int) and s.l < 2):
            act.wait_ge(self.tiles_done.handle, s.l * st.tpi + (st.done0 - st.tpi))
        n = (kt or st.kt) * 256
        act.activation(self.WH[:, slot, 0:n], self.RAW[:, slot, 0:n], ACT.Copy).then_inc(self.hi_split.handle, 1)

    def split_lo(self, dve, st, s, kt=None):
        slot = (st.base + s.u) % 2
        dve.wait_ge(self.hi_split.handle, s.l + (st.hi0 + 1))
        n = (kt or st.kt) * 256
        dve.tensor_tensor(self.WL[:, slot, 0:n], self.RAW[:, slot, 0:n], self.WH[:, slot, 0:n].bitcast(F32),
                          ALU.subtract).then_inc(self.lo_split.handle, 1)

    def ride_fetch(self, sync, rd, s, ahead):
        slot = s.u
        if ahead:
            sync.wait_ge(self.ride_added.handle, s.l + (self.ride0 + 1))
        src = self.aps["mods"][bass.ds(s.l + (rd.base + rd.k + ahead), 1), :, :].rearrange("a p n -> p (a n)")
        sync.dma_start(self.RIDE[:, slot, :], src).then_inc(self.ride_landed[slot].handle, 16)

    def weigh_by_vector(self, dve, item, acc, cond, stride=1):
        for k in range(KT):
            w, c = item[:, k * 256:k * 256 + 256], cond[:, k * stride:k * stride + 1]
            if k == 0:
                ins = dve.tensor_scalar(acc, w, c, None, ALU.mult)
            else:
                dve.drain()
                ins = dve.scalar_tensor_tensor(acc, w, c, acc, ALU.mult, ALU.add)
        return ins

    def weigh_by_pool(self, pool, item, acc, cond, stride=1):
        rows = item.rearrange("p (k n) -> p k n", k=KT)
        c = cond[:, 0:(KT - 1) * stride + 1:stride].rearrange("p (k a) -> p k a", a=1)
        pool.tensor_tensor(rows, rows, c.broadcast_to([P, KT, 256]), ALU.mult)
        half = KT // 2
        while half >= 1:
            pool.drain()
            dst = item[:, 0:half * 256] if half > 1 else acc
            ins = pool.tensor_tensor(dst, item[:, 0:half * 256], item[:, half * 256:2 * half * 256], ALU.add)
            half //= 2
        return ins

    def ride_add(self, pool, rd, s):
        if rd.ncol == 1:
            pool.wait_ge(self.ride_landed[s.u].handle, s.i * 16 + (self.ride_landed[s.u].n + 16))
        else:
            pool.wait_ge(self.ride_shared.handle, s.l + (self.ride_shared.n + 1))
        pool.wait_ge(self.ride_summed.handle, s.l + (self.ride0 + 1))
        cond = self.wk(rd.cond, rd.ncol - 1, KT * rd.ncol - rd.ncol + 1)
        ins = self.weigh_by_pool(pool, self.RIDE[:, s.u, :], self.RACC[:, s.u, rd.ncol - 1, :], cond, rd.ncol)
        ins.then_inc(self.ride_added.handle, 1)

    def ride_share(self, dve, rd, s):
        dve.wait_ge(self.ride_landed[s.u].handle, s.i * 16 + (self.ride_landed[s.u].n + 16))
        dve.wait_ge(self.ride_summed.handle, s.l + (self.ride0 + 1))
        ins = self.weigh_by_vector(dve, self.RIDE[:, s.u, :], self.RACC[:, s.u, 0, :], self.wk(rd.cond, 0, 15), 2)
        ins.then_inc(self.ride_shared.handle, 1)

    def ride_sum(self, pe, rd, s):
        pe.wait_ge(self.ride_added.handle, s.l + (self.ride0 + 1))
        for t in range(2):
            for j in range(rd.ncol):
                col = s.i * (2 * rd.ncol) + (256 + rd.k * rd.ncol + t * rd.ncol + j)
                mm = pe.matmul(self.B[5 + 2 * s.u][:, bass.ds(col, 1)], self.RACC[:, s.u, j, t * P:t * P + P],
                               self.ONES[:, 0:1], start=True, stop=True)
        mm.then_inc(self.ride_summed.handle, 1)

    def ride_finish(self, dve, rd):
        dve.wait_ge(self.ride_summed.handle, self.ride_summed.n)
        nc_ = rd.ncol
        for first, n, dest, bias in rd.runs:
            for u in range(2):
                src = self.B[5 + 2 * u][:, 256 + first * nc_:256 + (first + n) * nc_].rearrange(
                    "p (i t j) -> p i t j", t=2, j=nc_)
                out = self.WK[:, dest:dest + 2 * n * nc_].rearrange("p (i u t j) -> p i u t j", u=2, t=2, j=nc_)
                b = self.VEC[:, bias:bias + 2 * n].rearrange("p (i u t) -> p i u t", u=2, t=2)
                for j in range(nc_):
                    dve.tensor_tensor(out[:, :, u, :, j], src[:, :, :, j], b[:, :, u, :], ALU.add)

    def product(self, st, block, pe_tile, tpi, act_epi=None, dve_epi=None, freed=None, distance=4,
                post=True, rider=None, ready=False):
        st.tpi, st.done0 = tpi, self.tiles_done.after(tpi * st.n)
        st.pre, st.post = self.pre, 2 if post and st.base + st.n < N_ITEMS else 0
        self.pre = st.post
        st.hi0, st.lo0 = (x.after(st.n - st.pre + st.post) - st.pre for x in (self.hi_split, self.lo_split))
        st.free0 = freed.after(tpi * st.n)
        done, n = self.tiles_done.handle, st.n
        ride = 0 if rider is None else min(n, rider.n - rider.k)
        self.ride0 = self.ride_added.n
        assert ride in (0, n) or rider.ncol == 1

        @block.sync
        def _(sync):
            self.stream(sync, st, rider, ride)

        def program(eng, epilogue, split, share=False):
            if share and rider.k == 0:
                self.ride_share(eng, rider, Step(0, 0))
            for l in range(st.pre, 2):
                split(eng, st, Step(0, l))

            def both(s):
                if share:
                    self.ride_share(eng, rider, Next(s))
                if epilogue is not None:
                    epilogue(eng, s)
                split(eng, st, Ahead(s))
            steps(eng, 0, n - 2, both)
            for l in (n - 2, n - 1):
                if share and rider.k + l + 1 < rider.n:
                    self.ride_share(eng, rider, Next(Step(l // 2, l % 2)))
                if epilogue is not None:
                    epilogue(eng, Step(l // 2, l % 2))
                if st.post:
                    split(eng, st, Step((l + 2) // 2, l % 2), self.kt_of[st.base + l + 2])

        @block.scalar
        def _(act):
            program(act, act_epi, self.split_hi)

        @block.vector
        def _(dve):
            program(dve, dve_epi, self.split_lo, share=ride > 0 and rider.ncol == 2)

        @block.tensor
        def _(pe):
            def item(s, riding=False):
                slot = (st.base + s.u) % 2
                pe.wait_ge(self.lo_split.handle, s.l + (st.lo0 + 1))
                for t in range(tpi):
                    pe.wait_ge(freed.handle, s.l * tpi + (st.free0 + t + 1 - distance))
                    if riding and t == 1:
                        self.ride_sum(pe, rider, s)
                    pe_tile(pe, slot, s, t).then_inc(done, 1)
            first = 0
            if ready:
                item(Step(0, 0), ride > 0)
                item(Step(0, 1), ride > 0)
                first = 2
            if ride:
                steps(pe, first, ride, lambda s: item(s, True))
                first = ride
            if first < n:
                steps(pe, first, n, item)

        if ride:
            @block.gpsimd
            def _(pool):
                steps(pool, 0, ride, lambda s: self.ride_add(pool, rider, s))
            if rider.ncol == 2:
                self.ride_shared.after(ride)
            self.ride_added.after(ride)
            self.ride_summed.after(ride)
            for x in self.ride_landed:
                x.after(8 * ride)
            rider.k += ride
            if rider.k == rider.n:
                self.riders_done.append(rider)

    def end_rides(self, block):
        @block.vector
        def _(dve):
            for rd in self.riders_done:
                self.ride_finish(dve, rd)
        self.riders_done = []

    def three(self, pe, out, w, x, start, stop):
        (wh, wl), (xh, xl) = w, x
        pe.matmul(out, wh, xh, start=start, stop=False)
        pe.matmul(out, wh, xl, start=False, stop=False)
        return pe.matmul(out, wl, xh, start=False, stop=stop)

    def feature_tile(self, kt, hi, lo, ctx, ready=None):
        def tile(pe, slot, s, t):
            parts = [(self.B[2 * s.u + t][:, :], 0, TX)]
            if ctx:
                parts.append((self.B[4 + 2 * s.u + t][:, 0:TC], TX, TA))
            for out, a, b in parts:
                for k in range(kt):
                    if ready is not None and isinstance(s.l, int) and (s.l, t, a) == (0, 0, 0):
                        pe.wait_ge(ready.handle, ready.at(k))
                    c = k * 256 + t * P
                    mm = self.three(pe, out, (self.WH[:, slot, c:c + P], self.WL[:, slot, c:c + P]),
                                    (hi[:, k, a:b], lo[:, k, a:b]), k == 0, k == kt - 1)
            return mm
        return tile

    def token_tile(self, blocks):
        def tile(pe, slot, s, t):
            for k in range(KT):
                c = k * 256
                x = (self.HH[:, k, blocks[t]], self.HL[:, k, blocks[t]])
                w = (self.WH[:, slot, c:c + 256], self.WL[:, slot, c:c + 256])
                (wh, wl), (xh, xl) = w, x
                pe.matmul(self.B[t][:, 0:256], xh, wh, start=k == 0, stop=False)
                pe.matmul(self.B[t][:, 0:256], xl, wh, start=False, stop=False)
                mm = pe.matmul(self.B[t][:, 0:256], xh, wl, start=False, stop=k == KT - 1)
            return mm
        return tile

    def act_ready(self, act):
        act.wait_ge(self.started.handle, 1)

    def begin(self):
        nc, a = self.nc, self.aps
        n_mods, turn = dict(MODS)["first"], 4
        land = self.mods_landed

        FIRST, = self.region("first", [("mods", [P, turn, ITEM], F32)], self.split_at, self.split_end)

        def acc(k):
            return self.RACC[:, k // 2, k % 2, :]
        added = [(self.dve_step, 3, k) for k in range(3)] + [(self.pool_step, 1, 0)]
        self.dve_step.after(n_mods // turn * 3)
        self.pool_step.after(n_mods // turn)

        def weighed(eng, i, k):
            signal, per, place = added[k]
            eng.wait_ge(signal.handle, i * per + (place + 1))

        def weigh_item(eng, i, k):
            eng.wait_ge(land[k], i * 16 + 16)
            eng.wait_ge(self.raw_used.handle, i * turn + (k + 1))
            by = self.weigh_by_pool if k == turn - 1 else self.weigh_by_vector
            by(eng, FIRST[:, k, :], acc(k), self.wk("cond", 0, KT)).then_inc(added[k][0].handle, 1)
        with nc.Block() as block:
            @block.sync
            def _(sync):
                sync.dma_start(self.VEC[:, :], a["vectors"]).then_inc(self.loaded.handle, 16)

                def mod(m, k):
                    sync.dma_start(FIRST[:, k, :], a["mods"][bass.ds(m, 1), :, :].rearrange("a p n -> p (a n)")
                                   ).then_inc(land[k], 16)
                for k in range(turn):
                    mod(k, k)
                with sync.Fori(0, n_mods // turn - 1) as i:
                    for k in range(turn):
                        weighed(sync, i, k)
                        mod(i * turn + (k + turn), k)
                for m in range(2):
                    self.fetch(sync, m, self.kt_of[m], m)

            @block.gpsimd
            def _(pool):
                pool.memset(self.ONES[:, :], 1.0).then_inc(self.raw_used.handle, 4)
                pool.wait_ge(self.started.handle, 1)
                pool.drain()
                with pool.Fori(0, n_mods // turn) as i:
                    weigh_item(pool, i, turn - 1)

            @block.vector
            def _(dve):
                dve.memset(self.wk("mx", 0, 16), 0.0).then_inc(self.freed_dve.handle, 8)
                dve.wait_ge(self.started.handle, 1)
                with dve.Fori(0, n_mods // turn) as i:
                    for k in range(turn - 1):
                        weigh_item(dve, i, k)
                dve.wait_ge(self.raw_used.handle, n_mods + 4)
                half, quarter = n_mods, n_mods // 2
                for dest, src, n in ((0, 0, half), (half, half, quarter), (half + 3 * quarter, half + quarter, quarter)):
                    dve.tensor_tensor(self.wk("mod1", dest, n), self.B[0][:, src:src + n], self.vec("ada_b", dest, n),
                                      ALU.add)

            @block.scalar
            def _(act):
                act.dma_start(self.X[:, :, 0:TX], a["xT"]).then_inc(self.loaded.handle, 16)
                act.wait_ge(self.loaded.handle, 32)
                act.activation(self.wk("cond", 0, 8), self.vec("c", 0, 8), ACT.Silu).then_inc(self.freed_act.handle, 8)
                act.activation(self.wk("condc", 0, 16), self.vec("cc", 0, 16), ACT.Silu).then_inc(self.started.handle, 1)
                act.activation(self.wk("nb", 0, 2), self.vec("c", 0, 2), ACT.Copy).then_inc(self.ride_summed.handle, 2)
                for k in range(2):
                    act.activation(self.wk("rs", k), self.vec("c", k), ACT.Copy).then_inc(self.stored[k].handle, 16)
                for t, src in ((self.IDENT[:, :], a["ident"]), (self.HALF[:, :], a["half"]),
                               (self.X[:, :, TX:TA], a["ctxT"])):
                    act.dma_start(t, src).then_inc(self.loaded.handle, 16)
                act.wait_ge(self.loaded.handle, 80)

            @block.tensor
            def _(pe):
                with pe.Fori(0, n_mods // turn) as i:
                    for k in range(turn):
                        weighed(pe, i, k)
                        for t in range(2):
                            out = self.B[0][:, bass.ds(i * (2 * turn) + (2 * k + t), 1)]
                            mm = pe.matmul(out, acc(k)[:, t * P:t * P + P], self.ONES[:, 0:1], start=True, stop=True)
                        mm.then_inc(self.raw_used.handle, 1)
        self.loaded.after(80)
        self.ride_summed.after(2)
        self.freed_dve.after(8)
        self.freed_act.after(8)
        self.started.after(1)
        for k in range(2):
            self.stored[k].after(16)

    def norm(self, g, mods=None, ctx=False, final=False):
        W = TA if ctx else TX
        spans = [(0, TX)] + ([(TX, TA)] if ctx else [])
        tag = f"norm{self.item}_{g[0]}"
        SQ, R = self.region(tag, [("sq", [P, KT, W], F32), ("rstd", [P, W], F32)])
        a0, d0, p0, g0 = (x.n for x in (self.act_step, self.dve_step, self.pe_step, self.pool_step))
        A, V, E, G = (x.handle for x in (self.act_step, self.dve_step, self.pe_step, self.pool_step))
        gs = [self.wk("gs", 0, 8), self.wk("gs2", 0, 8)]

        def mod(j, kind, k):
            col, stride = mods[j][kind], mods[j][2]
            return self.WK[:, col + stride * k:col + stride * k + 1]

        with self.nc.Block() as block:
            @block.scalar
            def _(act):
                for q in range(4):
                    act.activation(SQ[:, 2 * q:2 * q + 2, :], self.X[:, 2 * q:2 * q + 2, 0:W], ACT.Square).then_inc(A, 1)
                act.wait_ge(V, d0 + 2)
                act.activation(R[:, :], R[:, :], ACT.Sqrt).then_inc(A, 1)
                for k in range(KT):
                    act.wait_ge(V, d0 + 3 + k)
                    if final:
                        act.activation(self.X[:, k, 0:W], SQ[:, k, :], ACT.Copy, scale=self.vec(g[0], g[1] + k)).then_inc(A, 1)
                        continue
                    for j, (s, e) in enumerate(spans):
                        ins = act.activation(self.HH[:, k, s:e], SQ[:, k, s:e], ACT.Identity,
                                             scale=gs[j][:, k:k + 1], bias=mod(j, 0, k))
                    ins.then_inc(A, 1)

            @block.vector
            def _(dve):
                if not final:
                    for j in range(len(spans)):
                        col, stride = mods[j][1], mods[j][2]
                        dve.scalar_tensor_tensor(gs[j], self.WK[:, col:col + 8 * stride:stride], 1.0,
                                                 self.vec(g[0], g[1], 8), ALU.add, ALU.mult)
                for q in range(1, 4):
                    dve.wait_ge(A, a0 + q + 1)
                    dve.tensor_tensor(SQ[:, 0:2, :], SQ[:, 0:2, :], SQ[:, 2 * q:2 * q + 2, :], ALU.add)
                    dve.drain()
                dve.tensor_tensor(SQ[:, 0, :], SQ[:, 0, :], SQ[:, 1, :], ALU.add).then_inc(V, 1)
                dve.wait_ge(E, p0 + 1)
                for b, (s, e) in enumerate(spans):
                    dve.tensor_scalar(R[:, s:e], self.B[b][:, 0:e - s], 1.0 / D, EPS, ALU.mult, ALU.add)
                dve.drain()
                dve.reciprocal(R[:, :], R[:, :]).then_inc(V, 1)
                dve.wait_ge(A, a0 + 5)

                def scale(k):
                    dve.tensor_tensor(SQ[:, k, :], self.X[:, k, 0:W], R[:, :], ALU.mult).then_inc(V, 1)

                def low(k):
                    dve.wait_ge(A, a0 + 6 + k)
                    dve.wait_ge(G, g0 + 1 + k)
                    dve.tensor_tensor(self.HL[:, k, 0:W], SQ[:, k, :], self.HH[:, k, 0:W].bitcast(F32), ALU.subtract)
                for k in range(KT):
                    scale(k)
                    if not final and k >= 2:
                        low(k - 2)
                if not final:
                    low(KT - 2)
                    low(KT - 1)

            @block.tensor
            def _(pe):
                pe.wait_ge(V, d0 + 1)
                for b, (s, e) in enumerate(spans):
                    mm = pe.matmul(self.B[b][:, 0:e - s], self.ONES[:, :], SQ[:, 0, s:e], start=True, stop=True)
                mm.then_inc(E, 1)

            if not final:
                @block.gpsimd
                def _(pool):
                    for k in range(KT):
                        pool.wait_ge(A, a0 + 6 + k)
                        for j, (s, e) in enumerate(spans):
                            ins = pool.tensor_scalar(SQ[:, k, s:e], SQ[:, k, s:e], gs[j][:, k:k + 1], mod(j, 0, k),
                                                     ALU.mult, ALU.add)
                        ins.then_inc(G, 1)
        self.act_step.after(5 + KT)
        self.dve_step.after(2 + KT)
        self.pe_step.after(1)
        if not final:
            self.pool_step.after(KT)

    def residual_epilogue(self, st, gate, ctx):
        def epi(dve, s):
            for t in range(2):
                dve.wait_ge(self.tiles_done.handle, s.l * 2 + (st.done0 + t + 1))
                m = s.l * 2 + t
                outs = [(self.B[2 * s.u + t][:, :], 0, TX, gate[0])]
                if ctx:
                    outs.append((self.B[4 + 2 * s.u + t][:, 0:TC], TX, TA, gate[1]))
                for bank, a, b, (col, stride) in outs:
                    x = self.X[:, bass.ds(m, 1), a:b].rearrange("p a n -> p (a n)")
                    ins = dve.scalar_tensor_tensor(x, bank, self.WK[:, bass.ds(m * stride + col, 1)], x,
                                                   ALU.mult, ALU.add)
                ins.then_inc(self.freed_dve.handle, 1)
        return epi

    def add_product(self, name, gate, hi=None, lo=None, ctx=False, rider=None, ready=None, block=None):
        st = Stage(*self.take(name))
        hi, lo = (self.HH, self.HL) if hi is None else (hi, lo)

        def body(block):
            self.product(st, block, self.feature_tile(st.kt, hi, lo, ctx, ready), 2,
                         dve_epi=self.residual_epilogue(st, gate, ctx), freed=self.freed_dve, rider=rider,
                         ready=ready is not None)
        if block is not None:
            return body(block)
        with self.nc.Block() as block:
            body(block)
            self.end_rides(block)

    def plain_product(self, name, dest, first, ctx=False, rider=None):
        st = Stage(*self.take(name))

        def epi(act, s):
            for t in range(2):
                act.wait_ge(self.tiles_done.handle, s.l * 2 + (st.done0 + t + 1))
                self.act_ready(act)
                d = dest[:, bass.ds(s.l * 2 + (first + t), 1), :].rearrange("p a n -> p (a n)")
                ins = act.activation(d[:, 0:TX], self.B[2 * s.u + t][:, :], ACT.Copy)
                if ctx:
                    ins = act.activation(d[:, TX:TA], self.B[4 + 2 * s.u + t][:, 0:TC], ACT.Copy)
                ins.then_inc(self.freed_act.handle, 1)
        with self.nc.Block() as block:
            self.product(st, block, self.feature_tile(st.kt, self.HH, self.HL, ctx), 2, act_epi=epi,
                         freed=self.freed_act, rider=rider)
            self.end_rides(block)

    def ffn(self, name, gate, wcol, bcol, centered, rider=None):
        ctx = centered and name == "g0"
        W = TA if ctx else TX
        GH, GL, CA, CV = self.region(name, [("g_hi", [P, 8, W], F32R), ("g_lo", [P, 8, W], F32R),
                                            ("conv_a", [P, 2, W], F32), ("conv_v", [P, 2, W], F32)],
                                     end=self.ride_at)
        with self.nc.Block() as block:
            for g in range(len(FGROUPS)):
                self.ffn_group(block, name, g, gate, wcol, bcol, centered, rider, (GH, GL, CA, CV))
            self.end_rides(block)

    def ffn_group(self, block, name, g, gate, wcol, bcol, centered, rider, tensors):
        GH, GL, CA, CV = tensors
        first = FGROUPS[g][0]
        ctx = centered and name == "g0"
        W = TA if ctx else TX
        taps = 2 * FT if centered else FT
        st = Stage(*self.take(f"{name}up{g}"))
        a0, v0 = self.act_step.after(3 * st.n), self.dve_step.after(2 * st.n)
        A, V = self.act_step.handle, self.dve_step.handle

        def col(base, tap, s, half):
            return self.VEC[:, bass.ds(s.l + (base + taps * tap + half * FT + first), 1)]

        def banks(s, t):
            out = [(self.B[2 * s.u + t][:, :], 0, TX)]
            if ctx:
                out.append((self.B[4 + 2 * s.u + t][:, 0:TC], TX, TA))
            return out

        def act_epi(act, s):
            act.wait_ge(self.tiles_done.handle, s.l * 2 + (st.done0 + 2))
            act.wait_ge(V, s.l * 2 + (v0 - 2))
            self.act_ready(act)
            here = 1 if centered else 2
            for t, dst in enumerate((CA, CV) if centered else (CA,)):
                for bank, a, b in banks(s, t):
                    ins = act.activation(dst[:, s.u, a:b], bank, ACT.Identity, scale=col(wcol, here, s, t),
                                         bias=col(bcol, 0, s, t))
            ins.then_inc(A, 1)
            act.wait_ge(*((self.freed_dve.handle, s.l * 2 + (st.free0 + 2)) if centered else
                          (V, s.l * 2 + (v0 + 1))))
            act.activation(CA[:, s.u, :], CA[:, s.u, :], ACT.Silu).then_inc(A, 1)
            act.wait_ge(*((V, s.l * 2 + (v0 + 1)) if centered else
                          (self.freed_dve.handle, s.l * 2 + (st.free0 + 2))))
            self.act_ready(act)
            act.activation(GH[:, bass.ds(s.l, 1), :].rearrange("p a n -> p (a n)"), CA[:, s.u, :],
                           ACT.Copy).then_inc(A, 1)

        def dve_epi(dve, s):
            dve.wait_ge(A, s.l * 3 + (a0 + 1))
            for tap, back in (((0, 1), (2, -1)) if centered else ((1, 1), (0, 2))):
                for t, dst in enumerate((CA, CV) if centered else (CA,)):
                    for bank, a, b in banks(s, t):
                        n = b - a
                        to = dst[:, s.u, a + max(back, 0):b + min(back, 0)]
                        ins = dve.scalar_tensor_tensor(to, bank[:, max(-back, 0):n - max(back, 0)],
                                                       col(wcol, tap, s, t), to, ALU.mult, ALU.add)
                if back > 0 and not (back == 2):
                    dve.drain()
            if centered:
                ins.then_inc(self.freed_dve.handle, 2)
            else:
                ins.then_inc(V, 1)
            dve.wait_ge(A, s.l * 3 + (a0 + 2))
            if centered:
                dve.tensor_tensor(CA[:, s.u, :], CA[:, s.u, :], CV[:, s.u, :], ALU.mult).then_inc(V, 1)
            else:
                dve.tensor_tensor(CA[:, s.u, :], CA[:, s.u, :], self.B[2 * s.u + 1][:, :],
                                  ALU.mult).then_inc(self.freed_dve.handle, 2)
            dve.wait_ge(A, s.l * 3 + (a0 + 3))
            low = GL[:, bass.ds(s.l, 1), :].rearrange("p a n -> p (a n)")
            high = GH[:, bass.ds(s.l, 1), :].rearrange("p a n -> p (a n)")
            dve.tensor_tensor(low, CA[:, s.u, :], high.bitcast(F32), ALU.subtract).then_inc(V, 1)

        def going(rd):
            return rd if rd is not None and rd.k < rd.n else None
        self.product(st, block, self.feature_tile(KT, self.HH, self.HL, ctx), 2, act_epi=act_epi,
                     dve_epi=dve_epi, freed=self.freed_dve, rider=going(rider))
        self.add_product(f"{name}down{g}", gate, GH, GL, ctx, going(rider), Ready(V, v0 + 2, 2), block)

    def pool_mixer(self):
        U, CS, DF, RC, ON, PH, PL = self.region("pool", [
            ("u", [P, KT, TX], F32), ("csum", [P, 2, TX], F32), ("pooled", [P, 2, TX], F32), ("edge", [P, 4, 16], F32),
            ("ones", [P, TX], F32), ("p_hi", [P, KT, TX], F32R), ("p_lo", [P, KT, TX], F32R)])
        ada = VC["ada_b"]
        mod = WC["mod1"]
        self.plain_product("pool_in", U, 0, rider=Rider("shift", "cond", 1, [(0, 4, mod + 24, ada + 24)]))
        a0, v0 = self.act_step.after(KT), self.dve_step.after(2 * KT)
        A, V = self.act_step.handle, self.dve_step.handle
        l0 = self.loaded.after(16)
        with self.nc.Block() as block:
            @block.sync
            def _(sync):
                sync.dma_start(RC[:, :, :], self.aps["pool_edge"]).then_inc(self.loaded.handle, 16)

            @block.vector
            def _(dve):
                dve.memset(ON[:, :], 1.0)
                dve.wait_ge(self.loaded.handle, l0 + 16)
                dve.drain()
                for k in range(KT):
                    w = 2 << (k // 2)
                    cs, df, u = CS[:, k % 2, :], DF[:, k % 2, :], U[:, k, :]
                    if k >= 2:
                        dve.wait_ge(A, a0 + k - 1)
                    dve.tensor_tensor_scan(cs, ON[:, :], u, 0.0, ALU.mult, ALU.add)
                    dve.drain()
                    dve.tensor_tensor(df[:, w:], cs[:, w:], cs[:, :-w], ALU.subtract)
                    dve.tensor_tensor(df[:, 0:w], cs[:, 0:w], RC[:, k // 2, 0:w], ALU.mult)
                    dve.drain()
                    dve.scalar_tensor_tensor(df[:, w:], df[:, w:], 1.0 / w, u[:, w:], ALU.mult, ALU.subtract)
                    dve.tensor_tensor(df[:, 0:w], df[:, 0:w], u[:, 0:w], ALU.subtract).then_inc(V, 1)
                    dve.wait_ge(A, a0 + k + 1)
                    dve.tensor_tensor(PL[:, k, :], df, PH[:, k, :].bitcast(F32), ALU.subtract).then_inc(V, 1)

            @block.scalar
            def _(act):
                for k in range(KT):
                    act.wait_ge(V, v0 + 2 * k + 1)
                    act.activation(PH[:, k, :], DF[:, k % 2, :], ACT.Copy).then_inc(A, 1)

        st = Stage(*self.take("grp"))
        TMP = CS

        def tile(pe, slot, s, t):
            T = 4 * s.u + t
            for k in range(2):
                c = (2 * t + k) * P
                mm = self.three(pe, self.B[t][:, :], (self.WH[:, slot, c:c + P], self.WL[:, slot, c:c + P]),
                                (PH[:, 2 * (T // 2) + k, :], PL[:, 2 * (T // 2) + k, :]), k == 0, k == 1)
            return mm

        a1, v1 = self.act_step.after(8), self.dve_step.after(8)

        def act_epi(act, s):
            for t in range(4):
                T = 4 * s.u + t
                act.wait_ge(self.tiles_done.handle, st.done0 + T + 1)
                if T >= 2:
                    act.wait_ge(V, v1 + T - 1)
                scale = self.vec("pool_scale", T)
                act.activation(self.HH[:, T, 0:TX], self.B[t][:, :], ACT.Copy, scale=scale).then_inc(A, 1)
                act.activation(TMP[:, T % 2, :], self.B[t][:, :], ACT.Copy, scale=scale).then_inc(self.freed_act.handle, 1)

        def dve_epi(dve, s):
            for t in range(4):
                T = 4 * s.u + t
                dve.wait_ge(A, a1 + T + 1)
                dve.wait_ge(self.freed_act.handle, st.free0 + T + 1)
                dve.tensor_tensor(self.HL[:, T, 0:TX], TMP[:, T % 2, :], self.HH[:, T, 0:TX].bitcast(F32),
                                  ALU.subtract).then_inc(V, 1)
        with self.nc.Block() as block:
            self.product(st, block, tile, 4, act_epi=act_epi, dve_epi=dve_epi, freed=self.freed_act)
        self.add_product("pool_out", [(mod + 16, 1)], rider=Rider("scale", "cond", 1, [(0, 4, mod + 32, ada + 32)]))

    def spill_product(self, name, dram, tokens=None, rider=None):
        st = Stage(*self.take(name))
        tpi = 2 if tokens is None else 4
        shape = [P, 2, 2, TX] if tokens is None else [P, 2, 4, 256]
        ST, = self.region(f"{name}_stage", [("out", shape, F32)], start=self.arena + 40960)
        s0 = [x.after(16 * ((st.n + 1 - k) // 2)) for k, x in enumerate(self.stored)]

        def epi(act, s):
            act.wait_ge(self.stored[s.u].handle, s.i * 16 + s0[s.u])
            for t in range(tpi):
                act.wait_ge(self.tiles_done.handle, s.l * tpi + (st.done0 + t + 1))
                src = self.B[2 * s.u + t][:, :] if tokens is None else self.B[t][:, 0:256]
                act.activation(ST[:, s.u, t, :], src, ACT.Copy).then_inc(self.freed_act.handle, 1)
            act.wait_ge(self.freed_act.handle, s.l * tpi + (st.free0 + tpi))
            if tokens is None:
                dst = dram[bass.ds(s.l * 2, 2), :, :].rearrange("t p n -> p t n")
            else:
                dst = dram[:, :, bass.ds(s.l * 256, 256)].rearrange("b p n -> p b n")
            act.dma_start(dst, ST[:, s.u, :, :]).then_inc(self.stored[s.u].handle, 16)

        tile = self.feature_tile(KT, self.HH, self.HL, False) if tokens is None else self.token_tile(tokens)
        with self.nc.Block() as block:
            self.product(st, block, tile, tpi, act_epi=epi, freed=self.freed_act, rider=rider)
            self.end_rides(block)

    def dilated_attention(self, shift1, kvshift):
        nc = self.nc
        dram = lambda n, shape: nc.dram_tensor(n, shape, F32, kind="Internal").ap()
        q_d, k_d = dram("q_scratch", (24, P, TX)), dram("k_scratch", (24, P, TX))
        v0_d, v1_d = dram("v0_scratch", (4, P, D)), dram("v1_scratch", (4, P, 2 * D))
        self.norm(("norm1_g", 8), [(shift1, shift1 + 8, 1)])
        self.spill_product("wq", q_d, rider=Rider("kvada", "cond", 1, [(0, 8, kvshift, VC["kv_ada_b"])]))
        self.norm(("kv_norm_g", 0), [(kvshift, kvshift + 8, 1)])
        self.spill_product("wk", k_d)
        self.spill_product("wv0", v0_d, [slice(P * b, P * b + P) for b in range(4)])
        self.spill_product("wv1", v1_d, [slice(b, TX, 4) for b in range(4)])

        D0, D12, SL, Q, K, V, SC, E, PT = self.region("att1", [
            ("dist0", [P, 4, TX], F32), ("dist12", [P, 2, P], F32), ("slopes", [P, NBR * NH1], F32),
            ("q", [P, 2, NBR, TX], F32), ("k", [P, 2, NBR, TX], F32), ("v", [P, 2, NBR, 4, P], F32),
            ("scores", [P, 2, TA], F32), ("exps", [P, 2, TA], F32), ("turned", [P, 2, TA], F32)])
        sem = lambda name: self.ctx.enter_context(nc.semaphore(name))
        qkv = [sem(f"qkv_loaded{k}") for k in range(2)]
        scored, turned, summed = sem("scored"), sem("turned"), sem("values_summed")
        biased, maxed, normed = sem("biased"), sem("maxed"), sem("normed")
        exped, copied = sem("exped"), sem("copied")
        o_hi, o_lo = sem("o_hi"), sem("o_lo")
        scale = HD ** -0.5
        UNITS = 8
        l0 = self.loaded.after(48)
        stored = [x.n for x in self.stored]
        q_v, k_v = (d.rearrange("(g t) p n -> t p g n", g=NBR) for d in (q_d, k_d))

        with nc.Block() as block:
            @block.sync
            def _(sync):
                for t, name in ((D0[:, :, :], "dist0"), (D12[:, :, :], "dist12"), (SL[:, :], "slopes")):
                    sync.dma_start(t, self.aps[name]).then_inc(self.loaded.handle, 16)
                for k in range(2):
                    sync.wait_ge(self.stored[k].handle, stored[k])

                def load(hp, u):
                    one = lambda a: a[bass.ds(hp, 1)].rearrange("a p g n -> p (a g) n")
                    sync.dma_start(Q[:, u, :, :], one(q_v)).then_inc(qkv[u], 16)
                    sync.dma_start(K[:, u, :, :], one(k_v)).then_inc(qkv[u], 16)
                    for g in range(NBR):
                        src = v0_d if g == 0 else v1_d
                        col = hp * P + (D if g == 2 else 0)
                        sync.dma_start(V[:, u, g, :, :],
                                       src[:, :, bass.ds(col, P)].rearrange("b p n -> p b n")).then_inc(qkv[u], 16)
                for u in range(2):
                    load(u, u)
                with sync.Fori(0, 3) as i:
                    for u in range(2):
                        sync.wait_ge(summed, i * (2 * UNITS) + UNITS * (u + 1))
                        load(i * 2 + (2 + u), u)

            def unit(x):
                return x // UNITS, x % UNITS // 4, x % 4

            @block.tensor
            def _(pe):
                def scores(i, x):
                    u, h, c = unit(x)
                    a, b = HD * h, HD * h + HD
                    if x % UNITS == 0:
                        pe.wait_ge(qkv[u], i * 80 + 80)
                    pe.wait_ge(biased, i * 16 + (x + 1))
                    own = slice(c, TX, 4)
                    pe.matmul(self.B[x % 2][:, :], Q[a:b, u, 0, own], K[a:b, u, 0, :], start=True, stop=True)
                    for g in (1, 2):
                        lo = (g - 1) * P
                        mm = pe.matmul(self.B[2 + x % 2][:, lo:lo + P], Q[a:b, u, g, own], K[a:b, u, g, own],
                                       start=True, stop=True)
                    mm.then_inc(scored, 1)

                def turn(i, x):
                    pe.wait_ge(normed, i * 16 + (x + 1))
                    pe.wait_ge(copied, i * 16 + (x + 2))
                    for j in range(6):
                        bank, lo = (self.B[4], j * P) if j < 4 else (self.B[5], (j - 4) * P)
                        mm = pe.transpose(bank[:, lo:lo + P], E[:, x % 2, j * P:j * P + P], self.IDENT[:, :])
                    mm.then_inc(turned, 1)

                def values(i, x):
                    u, h, c = unit(x)
                    pe.wait_ge(copied, i * 16 + (x + 3))
                    if x % UNITS == 0:
                        pe.wait_ge(o_lo, i * 2 + (u + 1))
                    out = self.B[6 + u][HD * h:HD * h + HD, c * P:c * P + P]
                    for j in range(6):
                        g, b = (0, j) if j < 4 else (j - 3, c)
                        mm = pe.matmul(out, V[:, u, g, b, HD * h:HD * h + HD], PT[:, x % 2, j * P:j * P + P],
                                       start=j == 0, stop=j == 5)
                    mm.then_inc(summed, 1)

                with pe.Fori(0, 4) as i:
                    for x in range(18):
                        if x < 16:
                            scores(i, x)
                        if 1 <= x < 17:
                            turn(i, x - 1)
                        if x >= 2:
                            values(i, x - 2)

            @block.vector
            def _(dve):
                dve.memset(self.wk("sum", 0, 1), 0.0).then_inc(biased, 2)
                dve.memset(self.wk("sum", 1, 1), 0.0).then_inc(o_lo, 2)
                dve.wait_ge(self.loaded.handle, l0 + 48)

                def bias_max(i, x):
                    u, h, c = unit(x)
                    sl = lambda g: SL[:, bass.ds(i * 4 + (2 * u + h + NH1 * g), 1)]
                    p = x % 2
                    dve.wait_ge(scored, i * 16 + (x + 1))
                    dve.wait_ge(exped, i * 16 + (x + 1))
                    dve.scalar_tensor_tensor(SC[:, p, 0:TX], D0[:, c, :], sl(0), self.B[p][:, :], ALU.mult, ALU.add)
                    for g in (1, 2):
                        lo = (g - 1) * P
                        ins = dve.scalar_tensor_tensor(SC[:, p, TX + lo:TX + lo + P], D12[:, g - 1, :], sl(g),
                                                       self.B[2 + p][:, lo:lo + P], ALU.mult, ALU.add)
                    ins.then_inc(biased, 1)
                    dve.drain()
                    dve.reduce_max(self.wk("mx", p), SC[:, p, :], AX)
                    dve.drain()
                    dve.tensor_scalar(self.wk("nb", p), self.wk("mx", p), -scale, None, ALU.mult).then_inc(maxed, 1)

                def normalise(i, x):
                    p = x % 2
                    dve.wait_ge(exped, i * 16 + (x + 3))
                    dve.reciprocal(self.wk("rs", p), self.wk("sum", p))
                    dve.drain()
                    dve.tensor_scalar(E[:, p, :], E[:, p, :], self.wk("rs", p), None, ALU.mult).then_inc(normed, 1)

                with dve.Fori(0, 4) as i:
                    for x in range(17):
                        if x < 16:
                            bias_max(i, x)
                        if x >= 1:
                            normalise(i, x - 1)
                    for u in range(2):
                        dve.wait_ge(o_hi, i * 2 + (u + 1))
                        src = self.B[6 + u][:, :].rearrange("p (c j) -> p c j", c=4)
                        one = lambda t: t[:, bass.ds(i * 2 + u, 1), 0:TX].rearrange("p a (j c) -> p c (a j)", c=4)
                        dve.tensor_tensor(one(self.HL), src, one(self.HH).bitcast(F32), ALU.subtract).then_inc(o_lo, 1)

            @block.scalar
            def _(act):
                act.activation(self.wk("rs", 2, 1), self.ONES[:, 0:1], ACT.Copy).then_inc(exped, 2)
                act.activation(self.wk("rs", 3, 1), self.ONES[:, 0:1], ACT.Copy).then_inc(copied, 2)

                def exp(i, x):
                    p = x % 2
                    act.wait_ge(maxed, i * 16 + (x + 1))
                    if x >= 2:
                        act.wait_ge(turned, i * 16 + (x - 1))
                    act.activation(E[:, p, :], SC[:, p, :], ACT.Exp, scale=scale, bias=self.wk("nb", p),
                                   accum_out=self.wk("sum", p)).then_inc(exped, 1)

                def copy(i, x):
                    p = x % 2
                    act.wait_ge(turned, i * 16 + (x + 1))
                    if x >= 2:
                        act.wait_ge(summed, i * 16 + (x - 1))
                    act.activation(PT[:, p, 0:TX], self.B[4][:, :], ACT.Copy)
                    act.activation(PT[:, p, TX:TA], self.B[5][:, 0:256], ACT.Copy).then_inc(copied, 1)

                with act.Fori(0, 4) as i:
                    for x in range(17):
                        if x < 16:
                            exp(i, x)
                        if x >= 1:
                            copy(i, x - 1)
                    for u in range(2):
                        act.wait_ge(summed, i * 16 + UNITS * (u + 1))
                        self.act_ready(act)
                        src = self.B[6 + u][:, :].rearrange("p (c j) -> p c j", c=4)
                        dst = self.HH[:, bass.ds(i * 2 + u, 1), 0:TX].rearrange("p a (j c) -> p c (a j)", c=4)
                        act.activation(dst, src, ACT.Copy).then_inc(o_hi, 1)

    def token_product(self, name, dest):
        st = Stage(*self.take(name))
        nb = TA // P

        def epi(act, s):
            for t in range(nb):
                act.wait_ge(self.tiles_done.handle, s.l * nb + (st.done0 + t + 1))
                self.act_ready(act)
                act.activation(dest[:, t, bass.ds(s.l * 256, 256)], self.B[t][:, 0:256],
                               ACT.Copy).then_inc(self.freed_act.handle, 1)
        with self.nc.Block() as block:
            self.product(st, block, self.token_tile([slice(P * b, P * b + P) for b in range(nb)]), nb,
                         act_epi=epi, freed=self.freed_act, distance=nb, post=False)

    def rope(self, F, li):
        CS, PM, T = self.region(f"rope{li}", [("cos_sin", [P, 2, TX], F32), ("perm", [P, P], F32),
                                              ("tmp", [P, 2, TX], F32)], self.split_at, self.split_end)
        tiles = list(range(8, 12)) + list(range(4))
        l0, p0, v0 = self.loaded.after(32), self.pe_step.after(8), self.dve_step.after(8)
        with self.nc.Block() as block:
            @block.sync
            def _(sync):
                sync.dma_start(CS[:, :, :], self.aps["rope_cs"]).then_inc(self.loaded.handle, 16)
                sync.dma_start(PM[:, :], self.aps["rope_perm"]).then_inc(self.loaded.handle, 16)

            @block.tensor
            def _(pe):
                pe.wait_ge(self.loaded.handle, l0 + 32)
                for x, t in enumerate(tiles):
                    if x >= 4:
                        pe.wait_ge(self.dve_step.handle, v0 + x - 3)
                    pe.matmul(self.B[x % 4][:, :], PM[:, :], F[:, t, 0:TX], start=True,
                              stop=True).then_inc(self.pe_step.handle, 1)

            @block.vector
            def _(dve):
                dve.wait_ge(self.loaded.handle, l0 + 32)
                for x, t in enumerate(tiles):
                    dve.wait_ge(self.pe_step.handle, p0 + x + 1)
                    dve.tensor_tensor(T[:, x % 2, :], CS[:, 1, :], self.B[x % 4][:, :],
                                      ALU.mult).then_inc(self.dve_step.handle, 1)
                    dve.tensor_tensor(F[:, t, 0:TX], F[:, t, 0:TX], CS[:, 0, :], ALU.mult)
                    dve.drain()
                    dve.tensor_tensor(F[:, t, 0:TX], F[:, t, 0:TX], T[:, x % 2, :], ALU.add)

    def lambdas(self):
        pr, = self.region("lam", [("prod", [P, 16], F32)])
        V, A, E = (x.handle for x in (self.dve_step, self.act_step, self.pe_step))
        v0, a0, p0 = self.dve_step.after(3), self.act_step.after(3), self.pe_step.after(1)
        lam, lb = self.vec("lam", 0, 8), self.vec("lb", 0, 8)
        with self.nc.Block() as block:
            @block.vector
            def _(dve):
                dve.tensor_tensor(pr[:, 0:4], lam[:, 0:8:2], lam[:, 1:8:2], ALU.mult).then_inc(V, 1)
                dve.tensor_tensor(pr[:, 4:8], lb[:, 4:8], lb[:, 0:4], ALU.subtract)
                dve.drain()
                dve.scalar_tensor_tensor(pr[:, 8:12], pr[:, 4:8], -1.0, pr[:, 4:8], ALU.mult, ALU.min).then_inc(V, 1)
                dve.wait_ge(A, a0 + 2)
                dve.scalar_tensor_tensor(self.wk("lb", 0, 4), pr[:, 4:8], 0.0, pr[:, 12:16], ALU.min, ALU.subtract)
                dve.tensor_scalar(pr[:, 4:8], pr[:, 4:8], -1.0, 0.0, ALU.mult, ALU.min)
                dve.drain()
                dve.tensor_tensor(self.wk("lb", 4, 4), pr[:, 4:8], pr[:, 12:16], ALU.subtract)
                dve.drain()
                dve.tensor_tensor(self.wk("lb", 8, 4), self.wk("lb", 4, 4), self.wk("lb", 0, 4), ALU.subtract).then_inc(V, 1)
                dve.wait_ge(A, a0 + 3)
                dve.tensor_tensor(self.wk("lam", 2, 2), self.wk("lam", 4, 4)[:, 0:4:2], self.wk("lam", 4, 4)[:, 1:4:2],
                                  ALU.subtract)
                dve.drain()
                for li in range(2):
                    dve.tensor_scalar(self.wk("lam", li), self.wk("lam", 2 + li), LAM0[li], None, ALU.add)
                for li in range(2):
                    dve.tensor_scalar(self.vec("subln", li), self.vec("subln", li), 1.0 - LAM0[li], None, ALU.mult)

            @block.tensor
            def _(pe):
                pe.wait_ge(V, v0 + 1)
                pe.matmul(self.B[0][:, 0:4], self.ONES[:, :], pr[:, 0:4], start=True, stop=True).then_inc(E, 1)

            @block.scalar
            def _(act):
                act.wait_ge(V, v0 + 2)
                act.activation(pr[:, 12:16], pr[:, 8:12], ACT.Exp).then_inc(A, 1)
                act.wait_ge(A, a0 + 1)
                act.activation(pr[:, 12:16], pr[:, 12:16], ACT.Ln, bias=1.0).then_inc(A, 1)
                act.wait_ge(E, p0 + 1)
                act.activation(self.wk("lam", 4, 4), self.B[0][:, 0:4], ACT.Exp).then_inc(A, 1)

    def diff_attention(self, F, VT, li):
        nc = self.nc
        E, PT = self.region(f"att2_{li}", [("exps", [P, 2, 2, TA], F32), ("turned", [P, 2, TA], F32)],
                            self.split_at, self.split_end)
        units = [(h, b) for h in range(4) for b in range(4 if li else 6)]
        N = len(units)
        per = N // 4
        if li == 0:
            self.att2 = {n: Signal(self.ctx.enter_context(nc.semaphore(n))) for n in
                         ("d_scored", "d_turned", "d_summed", "d_maxed", "d_combined", "d_exped", "d_copied", "d_out")}
        q = self.att2
        S = {n: (x.handle, x.after({"d_scored": 2, "d_maxed": 2, "d_exped": 2}.get(n, 1) * (4 if n == "d_out" else N)))
             for n, x in q.items()}
        scale = HD ** -0.5

        def wait(eng, name, count):
            if count > 0:
                eng.wait_ge(S[name][0], S[name][1] + count)

        def parts(x):
            return ([(0, TX)] if units[x][1] < 4 else []) + [(TX, TA)]

        def blocks(x):
            return range(6) if units[x][1] < 4 else range(4, 6)

        with nc.Block() as block:
            @block.tensor
            def _(pe):
                def scores(x, c):
                    h, b = units[x]
                    wait(pe, "d_exped", 2 * (x - 1) + c + 1)
                    rows = slice(HD * c, HD * c + HD)
                    for lo, hi in parts(x):
                        bank = self.B[c] if lo == 0 else self.B[2 + c]
                        mm = pe.matmul(bank[:, 0:hi - lo], F[rows, 8 + h, b * P:b * P + P], F[rows, h, lo:hi],
                                       start=True, stop=True)
                    mm.then_inc(S["d_scored"][0], 1)

                def turn(x):
                    wait(pe, "d_combined", x + 1)
                    wait(pe, "d_copied", x)
                    for j in blocks(x):
                        bank, lo = (self.B[4], j * P) if j < 4 else (self.B[5], (j - 4) * P)
                        mm = pe.transpose(bank[:, lo:lo + P], E[:, x % 2, 0, j * P:j * P + P], self.IDENT[:, :])
                    mm.then_inc(S["d_turned"][0], 1)

                def values(x):
                    h, b = units[x]
                    wait(pe, "d_copied", x + 1)
                    if b == 0:
                        wait(pe, "d_out", h)
                    out = self.B[6][:, b * P:b * P + P] if b < 4 else self.B[7][:, (b - 4) * P:(b - 4) * P + P]
                    js = list(blocks(x))
                    for j in js:
                        mm = pe.matmul(out, VT[:, j, h * P:h * P + P], PT[:, x % 2, j * P:j * P + P],
                                       start=j == js[0], stop=j == js[-1])
                    mm.then_inc(S["d_summed"][0], 1)

                for x in range(N + 2):
                    if x < N:
                        scores(x, 0)
                        scores(x, 1)
                    if 1 <= x <= N:
                        turn(x - 1)
                    if x >= 2:
                        values(x - 2)

            @block.vector
            def _(dve):
                def maxima(x, c):
                    wait(dve, "d_scored", 2 * x + c + 1)
                    m = self.wk("mx", 2 * c, 2)
                    if len(parts(x)) == 2:
                        dve.reduce_max(m[:, 0:1], self.B[c][:, :], AX)
                        dve.reduce_max(m[:, 1:2], self.B[2 + c][:, 0:TC], AX)
                        dve.drain()
                        dve.tensor_tensor(m[:, 0:1], m[:, 0:1], m[:, 1:2], ALU.max)
                    else:
                        dve.reduce_max(m[:, 0:1], self.B[2 + c][:, 0:TC], AX)
                    dve.drain()
                    dve.tensor_scalar(self.wk("nb", 2 * (x % 2) + c), m[:, 0:1], -scale, None,
                                      ALU.mult).then_inc(S["d_maxed"][0], 1)

                def combine(x):
                    p = x % 2
                    wait(dve, "d_exped", 2 * x + 2)
                    sums = self.wk("sum", 4 * p, 4)
                    rs = self.wk("rs", 2 * p, 2)
                    if len(parts(x)) == 2:
                        dve.tensor_tensor(sums[:, 0:4:2], sums[:, 0:4:2], sums[:, 1:4:2], ALU.add)
                        dve.drain()
                        dve.reciprocal(rs, sums[:, 0:4:2])
                    else:
                        dve.reciprocal(rs, sums[:, 1:4:2])
                    dve.drain()
                    a, b = parts(x)[0][0], TA
                    dve.tensor_scalar(E[:, p, 1, a:b], E[:, p, 1, a:b], rs[:, 1:2], self.wk("lam", li),
                                      ALU.mult, ALU.mult)
                    dve.drain()
                    dve.scalar_tensor_tensor(E[:, p, 0, a:b], E[:, p, 0, a:b], rs[:, 0:1], E[:, p, 1, a:b],
                                             ALU.mult, ALU.subtract).then_inc(S["d_combined"][0], 1)
                for x in range(N + 1):
                    if x < N:
                        maxima(x, 0)
                        maxima(x, 1)
                    if x >= 1:
                        combine(x - 1)

            @block.scalar
            def _(act):
                def exps(x, c):
                    p = x % 2
                    wait(act, "d_maxed", 2 * x + c + 1)
                    wait(act, "d_turned", x - 1)
                    for lo, hi in parts(x):
                        bank = self.B[c] if lo == 0 else self.B[2 + c]
                        ins = act.activation(E[:, p, c, lo:hi], bank[:, 0:hi - lo], ACT.Exp, scale=scale,
                                             bias=self.wk("nb", 2 * p + c),
                                             accum_out=self.wk("sum", 4 * p + 2 * c + (lo > 0)))
                    ins.then_inc(S["d_exped"][0], 1)

                def copy(x):
                    wait(act, "d_turned", x + 1)
                    wait(act, "d_summed", x - 1)
                    for lo, hi in parts(x):
                        ins = act.activation(PT[:, x % 2, lo:hi], self.B[4 if lo == 0 else 5][:, 0:hi - lo], ACT.Copy)
                    ins.then_inc(S["d_copied"][0], 1)

                def head(h):
                    wait(act, "d_summed", per * (h + 1))
                    ins = act.activation(F[:, 8 + h, 0:TX], self.B[6][:, :], ACT.Copy)
                    if li == 0:
                        ins = act.activation(F[:, 8 + h, TX:TA], self.B[7][:, 0:TC], ACT.Copy)
                    ins.then_inc(S["d_out"][0], 1)

                for x in range(N + 2):
                    if x < N:
                        exps(x, 0)
                        exps(x, 1)
                    if 1 <= x <= N:
                        copy(x - 1)
                    if x >= 2 and (x - 2) % per == per - 1:
                        head((x - 2) // per)

    def head_norms(self, name, src, tiles, ones, inverse, weight, dest, W, gates=None):
        T1, RS = self.region(f"{name}_hn", [("a", [P, 2, TA], F32), ("r", [P, 2, TA], F32)],
                             self.split_at, self.split_end)
        G = None if gates is None else self.region(f"{name}_g", [("g", [P, 2, TA], F32)],
                                                   self.split_at + 16 * TA, self.split_end)[0]
        V, A, E = (x.handle for x in (self.dve_step, self.act_step, self.pe_step))
        n = len(tiles)
        v0, a0, p0 = self.dve_step.after(3 * n), self.act_step.after(4 * n), self.pe_step.after(n)
        spans = [(0, TX)] + ([(TX, TA)] if W == TA else [])
        with self.nc.Block() as block:
            @block.scalar
            def _(act):
                for x, t in enumerate(tiles):
                    p = x % 2
                    if x >= 2:
                        act.wait_ge(V, v0 + 3 * (x - 2) + 3)
                    act.activation(T1[:, p, 0:W], src[:, t, 0:W], ACT.Square).then_inc(A, 1)
                    act.wait_ge(V, v0 + 3 * x + 1)
                    act.activation(RS[:, p, 0:W], RS[:, p, 0:W], ACT.Sqrt).then_inc(A, 1)
                    if gates is not None:
                        act.activation(G[:, p, 0:W], gates[:, x, 0:W], ACT.Silu).then_inc(A, 1)
                    else:
                        act.activation(T1[:, p, 0:1], T1[:, p, 0:1], ACT.Copy).then_inc(A, 1)
                    act.wait_ge(V, v0 + 3 * x + 2)
                    act.activation(self.HH[:, dest + x, 0:W], T1[:, p, 0:W], ACT.Copy).then_inc(A, 1)

            @block.tensor
            def _(pe):
                for x in range(n):
                    pe.wait_ge(A, a0 + 4 * x + 1)
                    if x >= 2:
                        pe.wait_ge(V, v0 + 3 * (x - 2) + 1)
                    for b, (s, e) in enumerate(spans):
                        mm = pe.matmul(self.B[2 * (x % 2) + b][:, 0:e - s], ones, T1[:, x % 2, s:e],
                                       start=True, stop=True)
                    mm.then_inc(E, 1)

            @block.vector
            def _(dve):
                for x, t in enumerate(tiles):
                    p = x % 2
                    dve.wait_ge(E, p0 + x + 1)
                    for b, (s, e) in enumerate(spans):
                        dve.tensor_scalar(RS[:, p, s:e], self.B[2 * p + b][:, 0:e - s], inverse, EPS, ALU.mult, ALU.add)
                    dve.drain()
                    dve.reciprocal(RS[:, p, 0:W], RS[:, p, 0:W]).then_inc(V, 1)
                    dve.wait_ge(A, a0 + 4 * x + 3)
                    dve.scalar_tensor_tensor(T1[:, p, 0:W], src[:, t, 0:W], weight, RS[:, p, 0:W], ALU.mult, ALU.mult)
                    dve.drain()
                    if gates is not None:
                        dve.tensor_tensor(T1[:, p, 0:W], T1[:, p, 0:W], G[:, p, 0:W], ALU.mult).then_inc(V, 1)
                    else:
                        dve.memset(self.wk("sum", 15), 0.0).then_inc(V, 1)
                    dve.wait_ge(A, a0 + 4 * x + 4)
                    dve.tensor_tensor(self.HL[:, dest + x, 0:W], T1[:, p, 0:W], self.HH[:, dest + x, 0:W].bitcast(F32),
                                      ALU.subtract).then_inc(V, 1)

    def fourier(self, F, li):
        nb = 4 if li else 6
        CL, F64, WF, AB = self.region(f"four{li}", [
            ("dft", [P, 2, 4, TX], F32), ("dft64", [P, 2 * P], F32), ("w", [P, 2, 256], F32), ("ab", [P, nb, 2, 256], F32)],
            self.split_at, self.split_end)
        V, A, E = (x.handle for x in (self.dve_step, self.act_step, self.pe_step))
        segs = [(0, TX, [0, 1, 2, 3], 1)] + ([(TX, TA, [4, 5], 2)] if li == 0 else [])
        ns = len(segs)
        n_act = nb + 2 * ns + 2
        l0, p0, a0, v0 = self.loaded.after(48), self.pe_step.after(nb + 2 * ns + 2), self.act_step.after(n_act), self.dve_step.after(2)
        W = segs[-1][1]
        TMP, = self.region(f"four{li}t", [("t", [P, 1, TA], F32)], self.arena_tail, self.end)
        with self.nc.Block() as block:
            @block.sync
            def _(sync):
                sync.dma_start(CL[:, :, :, :], self.aps["dft"]).then_inc(self.loaded.handle, 16)
                sync.dma_start(F64[:, :], self.aps["dft64"]).then_inc(self.loaded.handle, 16)
                sync.dma_start(WF[:, :, :], self.aps["w_fnet"][li]).then_inc(self.loaded.handle, 16)

            @block.tensor
            def _(pe):
                pe.wait_ge(self.loaded.handle, l0 + 48)
                for b in range(nb):
                    if b >= 4:
                        pe.wait_ge(A, a0 + b - 3)
                    for j in range(2):
                        mm = pe.matmul(self.B[b % 4][:, 256 * j:256 * j + 256], F[:, 16 + j, b * P:b * P + P],
                                       F64[:, :], start=True, stop=True)
                    mm.then_inc(E, 1)
                for x, (s, e, bl, step) in enumerate(segs):
                    pe.wait_ge(A, a0 + nb)
                    for j in range(2):
                        for y, b in enumerate(bl):
                            for z in range(2):
                                mm = pe.matmul(self.B[4 + 2 * x + j][:, 0:e - s], AB[:, b, j, z * P:z * P + P],
                                               CL[:, z, y, 0:TX:step], start=(y, z) == (0, 0),
                                               stop=(y, z) == (len(bl) - 1, 1))
                        mm.then_inc(E, 1)
                pe.wait_ge(A, a0 + nb + 2 * ns)
                for m in range(2):
                    for x, (s, e, _, _) in enumerate(segs):
                        for j in range(2):
                            mm = pe.matmul(self.B[2 * m + x][:, 0:e - s], WF[:, j, m * P:m * P + P], F[:, 16 + j, s:e],
                                           start=j == 0, stop=j == 1)
                    mm.then_inc(E, 1)

            @block.scalar
            def _(act):
                for b in range(nb):
                    act.wait_ge(E, p0 + b + 1)
                    act.activation(AB[:, b, :, :].rearrange("p a n -> p (a n)"), self.B[b % 4][:, :], ACT.Copy).then_inc(A, 1)
                for x, (s, e, _, _) in enumerate(segs):
                    for j in range(2):
                        act.wait_ge(E, p0 + nb + 2 * x + j + 1)
                        act.activation(F[:, 16 + j, s:e], self.B[4 + 2 * x + j][:, 0:e - s], ACT.Copy,
                                       scale=((e - s) * 64.0) ** -0.5).then_inc(A, 1)
                for m in range(2):
                    act.wait_ge(E, p0 + nb + 2 * ns + m + 1)
                    if m == 1:
                        act.wait_ge(V, v0 + 1)
                    for x, (s, e, _, _) in enumerate(segs):
                        act.activation(self.HH[:, 6 + m, s:e], self.B[2 * m + x][:, 0:e - s], ACT.Copy)
                    for x, (s, e, _, _) in enumerate(segs):
                        ins = act.activation(TMP[:, 0, s:e], self.B[2 * m + x][:, 0:e - s], ACT.Copy)
                    ins.then_inc(A, 1)

            @block.vector
            def _(dve):
                for m in range(2):
                    dve.wait_ge(A, a0 + nb + 2 * ns + m + 1)
                    dve.tensor_tensor(self.HL[:, 6 + m, 0:W], TMP[:, 0, 0:W], self.HH[:, 6 + m, 0:W].bitcast(F32),
                                      ALU.subtract).then_inc(V, 1)

    def recurrence(self, F, VT, li):
        lat = li == 1
        nb = 4 if lat else 6
        W = nb * P
        NB = TA // P
        KS, T2, ST, TOT, ET = self.region(f"rec{li}", [
            ("ks", [P, 4, TA], F32), ("t2", [P, 4, TA], F32), ("states", [P, 2 * NB, 2, HD], F32),
            ("total", [P, 4, NB], F32), ("exptotal", [P, 4, NB], F32)], self.split_at, self.split_end)
        KTT, ACC = self.region(f"rec{li}k", [("kt", [P, NB, 2, 256], F32)], self.split_at + 16 * TA, self.split_end) + \
            self.region(f"rec{li}a", [("acc", [P, 2, nb // 2, 4, P], F32)], self.split_at + 16 * TA, self.split_end)
        DB, = self.region(f"rec{li}d", [("d", [P, 2, 2, TA], F32)], self.split_at, self.split_end)
        MK, = self.region(f"rec{li}m", [("masks", [P, 2 * LEVELS, P], mybir.dt.int32)], self.arena_tail, self.end)
        RM = KS[:, 0, :]
        Z, K, T1, Q = F[:, 4:8, :], F[:, 0:4, :], F[:, 8:12, :], F[:, 12:14, :]
        l0 = self.loaded.after(32)
        V, A, E, G = (x.handle for x in (self.dve_step, self.act_step, self.pe_step, self.pool_step))
        v0, a0, p0 = self.dve_step.n, self.act_step.n, self.pe_step.n
        second = 1 if li else 0
        a, c, ca = self.wk("lb", 0, 4), self.wk("lb", 4, 4), self.wk("lb", 8, 4)
        with self.nc.Block() as block:
            @block.sync
            def _(sync):
                sync.dma_start(MK[:, :, :], self.aps["level_masks"]).then_inc(self.loaded.handle, 16)
                sync.dma_start(RM, self.aps["block_reset"]).then_inc(self.loaded.handle, 16)

            @block.vector
            def _(dve):
                for t in range(4):
                    dve.scalar_tensor_tensor(T1[:, t, :], Z[:, t, :], -1.0, Z[:, t, :], ALU.mult, ALU.min).then_inc(V, 1)
                for t in range(4):
                    dve.wait_ge(A, a0 + 2 * t + 2)
                    dve.scalar_tensor_tensor(T1[:, t, :], Z[:, t, :], 0.0, T1[:, t, :], ALU.min, ALU.subtract)
                    dve.drain()
                    dve.tensor_tensor(K[:, t, :], T1[:, t, :], Z[:, t, :], ALU.subtract).then_inc(V, 1)
                if second:
                    for t in range(4):
                        dve.drain()
                        dve.tensor_scalar(Z[:, t, :], T1[:, t, :], ca[:, t:t + 1], None, ALU.add)
                        dve.drain()
                        dve.scalar_tensor_tensor(Z[:, t, :], Z[:, t, :], -1.0, Z[:, t, :], ALU.mult, ALU.min).then_inc(V, 1)
                        dve.tensor_scalar(T1[:, t, :], T1[:, t, :], c[:, t:t + 1], a[:, t:t + 1], ALU.add, ALU.max)
                dve.wait_ge(self.loaded.handle, l0 + 32)
                for t in range(4):
                    if second:
                        dve.wait_ge(A, a0 + 12 + 2 * t + 2)
                        dve.tensor_tensor(T1[:, t, :], T1[:, t, :], Z[:, t, :], ALU.add)
                    dve.drain()
                    dve.tensor_tensor_scan(Z[:, t, :], RM, T1[:, t, :], 0.0, ALU.mult, ALU.add)
                dve.drain()
                last = Z.rearrange("p t (b n) -> p t b n", n=P)[:, :, :, P - 1:P]
                dve.tensor_copy(TOT[:, :, :], last.rearrange("p t b n -> p t (b n)"))
                dve.drain()
                dve.tensor_tensor(Z[:, 2:4, :], Z[:, 2:4, :], T1[:, 2:4, :], ALU.subtract)
                dve.drain()
                for t in range(4):
                    view = lambda x: x[:, t, :].rearrange("p (b n) -> p b n", n=P)
                    dve.tensor_tensor(view(T2), TOT[:, t, :].rearrange("p (b n) -> p b n", n=1).to_broadcast([P, NB, P]),
                                      view(Z), ALU.subtract).then_inc(V, 1)
                n = v0 + 12 + 4 * second
                done = a0 + 12 + 8 * second
                dve.wait_ge(A, done + 9)
                dve.tensor_tensor(KS[:, 0:2, :], K[:, 0:2, :], T2[:, 0:2, :], ALU.mult).then_inc(V, 1)
                dve.tensor_tensor(KS[:, 2:4, :], K[:, 2:4, :], T1[:, 2:4, :], ALU.mult).then_inc(V, 1)
                dve.drain()
                dve.tensor_tensor(T1[:, 0:2, 0:W], Q[:, :, 0:W], T1[:, 0:2, 0:W], ALU.mult)
                dve.tensor_tensor(T1[:, 2:4, 0:W], Q[:, :, 0:W], T2[:, 2:4, 0:W], ALU.mult).then_inc(V, 1)
                for d in range(2):
                    dve.memset(ST[:, d * NB, :, :], 0.0)
                dve.wait_ge(E, p0 + 2 * NB)
                order = [[4, 5, 0, 1, 2, 3], [5, 4, 3, 2, 1, 0]]
                for pos in range(NB - 1):
                    dve.drain()
                    for d in range(2):
                        b = order[d][pos]
                        x = d * NB + b
                        for j in range(2):
                            u = self.B[x // 4][:, (x % 4) * P + j * HD:(x % 4) * P + j * HD + HD]
                            dve.scalar_tensor_tensor(ST[:, d * NB + pos + 1, j, :], ST[:, d * NB + pos, j, :],
                                                     ET[:, 2 * d + j, b:b + 1], u, ALU.mult, ALU.add)

            @block.scalar
            def _(act):
                for t in range(4):
                    act.wait_ge(V, v0 + t + 1)
                    act.activation(T1[:, t, :], T1[:, t, :], ACT.Exp).then_inc(A, 1)
                    act.wait_ge(A, a0 + 2 * t + 1)
                    act.activation(T1[:, t, :], T1[:, t, :], ACT.Ln, bias=1.0).then_inc(A, 1)
                for t in range(4):
                    act.wait_ge(V, v0 + 4 + t + 1)
                    act.activation(K[:, t, :], K[:, t, :], ACT.Exp, bias=c[:, t:t + 1] if second else 0.0).then_inc(A, 1)
                if second:
                    for t in range(4):
                        act.wait_ge(V, v0 + 8 + t + 1)
                        act.activation(Z[:, t, :], Z[:, t, :], ACT.Exp).then_inc(A, 1)
                        act.wait_ge(A, a0 + 12 + 2 * t + 1)
                        act.activation(Z[:, t, :], Z[:, t, :], ACT.Ln, bias=1.0).then_inc(A, 1)
                n = v0 + 8 + 4 * second
                for t in range(4):
                    act.wait_ge(V, n + t + 1)
                    act.activation(T2[:, t, :], T2[:, t, :], ACT.Exp).then_inc(A, 1)
                    act.activation(T1[:, t, :], Z[:, t, :], ACT.Exp).then_inc(A, 1)
                act.activation(ET[:, :, :], TOT[:, :, :], ACT.Exp).then_inc(A, 1)
                done = a0 + 12 + 8 * second + 9
                for b in range(NB):
                    act.wait_ge(E, p0 + b + 1)
                    if b == 0:
                        act.wait_ge(V, n + 4 + 3)
                    act.activation(KTT[:, b, :, :].rearrange("p a n -> p (a n)"), self.B[4 + b % 4][:, :],
                                   ACT.Copy).then_inc(A, 1)

            @block.tensor
            def _(pe):
                n = v0 + 12 + 4 * second
                done = a0 + 12 + 8 * second + 9
                pe.wait_ge(V, n + 2)
                for b in range(NB):
                    if b >= 4:
                        pe.wait_ge(A, done + b - 3)
                    for t in range(4):
                        mm = pe.transpose(self.B[4 + b % 4][:, t * P:t * P + P], KS[:, t, b * P:b * P + P], self.IDENT[:, :])
                    mm.then_inc(E, 1)
                for b in range(NB):
                    pe.wait_ge(A, done + b + 1)
                    for d in range(2):
                        x = d * NB + b
                        for h in range(4):
                            r, j = h % 2, h // 2
                            lo = (x % 4) * P + j * HD
                            mm = pe.matmul(self.B[x // 4][HD * r:HD * r + HD, lo:lo + HD], KTT[:, b, d, h * HD:h * HD + HD],
                                           VT[:, b, 2 * 256 + h * HD:2 * 256 + h * HD + HD], start=True, stop=True)
                    mm.then_inc(E, 1)
        self.dve_step.after(12 + 4 * second + 3)
        self.act_step.after(12 + 8 * second + 9 + NB)
        self.pe_step.after(2 * NB)

        jobs = [None] + [(lv, d) for lv in range(LEVELS) for d in range(2)]
        J = len(jobs)
        v0, a0, p0, g0 = self.dve_step.n, self.act_step.n, self.pe_step.n, self.pool_step.n
        if li == 0:
            self.read_out = Signal(self.ctx.enter_context(self.nc.semaphore("pairs_read_out")))
            self.paired = Signal(self.ctx.enter_context(self.nc.semaphore("pairs_done")))
        c0, s0 = self.read_out.after(J * nb), self.paired.after(J * nb)

        def halves(x, lv, tiles=None):
            m = 1 << lv
            v = x.rearrange("p t (n m) -> p t n m", m=2 * m)
            return v[:, :, :, 0:m], v[:, :, :, m:2 * m], v

        with self.nc.Block() as block:
            @block.gpsimd
            def _(pool):
                for n, job in enumerate(jobs):
                    if n >= 2:
                        pool.wait_ge(self.paired.handle, s0 + (n - 1) * nb)
                    if job is None:
                        pool.tensor_tensor(DB[:, 0, :, 0:W], K[:, 0:2, 0:W], K[:, 2:4, 0:W], ALU.add).then_inc(G, 1)
                        continue
                    lv, d = job
                    m = 1 << lv
                    cl, cr, cv = halves(Z[:, 2 * d:2 * d + 2, 0:W], lv)
                    dl, dr, _ = halves(DB[:, n % 2, :, 0:W], lv)
                    at = m - 1 if d == 0 else m
                    mid = cv[:, :, :, at:at + 1].to_broadcast([P, 2, W // (2 * m), m])
                    pool.tensor_tensor(dl, mid, cl, ALU.subtract)
                    pool.tensor_tensor(dr, cr, mid, ALU.subtract).then_inc(G, 1)

            @block.scalar
            def _(act):
                for n, job in enumerate(jobs):
                    if job is None:
                        continue
                    act.wait_ge(G, g0 + n + 1)
                    act.activation(DB[:, n % 2, :, 0:W], DB[:, n % 2, :, 0:W], ACT.Exp).then_inc(A, 1)

            @block.vector
            def _(dve):
                def decay(n):
                    lv, d = jobs[n]
                    dve.wait_ge(A, a0 + n)
                    xl, xr, _ = halves(DB[:, n % 2, :, 0:W], lv)
                    ql, qr, _ = halves(Q[:, :, 0:W], lv)
                    kl, kr, _ = halves(K[:, 2 * d:2 * d + 2, 0:W], lv)
                    dve.tensor_tensor(xl, xl, kl if d == 0 else ql, ALU.mult)
                    dve.tensor_tensor(xr, xr, qr if d == 0 else kr, ALU.mult).then_inc(V, 1)

                for n, job in enumerate(jobs):
                    if n + 1 < J:
                        decay(n + 1)
                    for y in range(nb):
                        dve.wait_ge(self.paired.handle, s0 + n * nb + y + 1)
                        acc = ACC[:, y % 2, y // 2, :, :]
                        bank = self.B[(n * nb + y) % 8][:, :].rearrange("p (a n) -> p a n", a=4)
                        if job is None:
                            every = self.IDENT[:, :].rearrange("p (a n) -> p a n", a=1).to_broadcast([P, 4, P])
                            ins = dve.tensor_tensor(acc, every, bank, ALU.mult)
                        else:
                            mask = MK[:, n - 1:n, :].to_broadcast([P, 4, P])
                            ins = dve.copy_predicated(acc, mask, bank)
                        ins.then_inc(self.read_out.handle, 1)
                    dve.drain()

            @block.tensor
            def _(pe):
                for n, job in enumerate(jobs):
                    if job is None:
                        pe.wait_ge(G, g0 + 1)
                    else:
                        pe.wait_ge(V, v0 + n)
                    for y in range(nb):
                        if n * nb + y >= 8:
                            pe.wait_ge(self.read_out.handle, c0 + n * nb + y - 7)
                        r, pair = y % 2, y // 2
                        rows = slice(HD * r, HD * r + HD)
                        for q in range(4):
                            b, j = 2 * pair + q // 2, q % 2
                            x = DB[rows, n % 2, j, b * P:b * P + P]
                            other = Q[rows, j, b * P:b * P + P] if job is None else x
                            mm = pe.matmul(self.B[(n * nb + y) % 8][:, q * P:q * P + P], x, other, start=True, stop=True)
                        mm.then_inc(self.paired.handle, 1)
        self.pool_step.after(J)
        self.act_step.after(J - 1)
        self.dve_step.after(J - 1)

        p0, a0 = self.pe_step.after(nb), self.act_step.after(nb)
        order = [[4, 5, 0, 1, 2, 3], [5, 4, 3, 2, 1, 0]]
        with self.nc.Block() as block:
            @block.tensor
            def _(pe):
                for b in range(nb):
                    if b >= 4:
                        pe.wait_ge(A, a0 + b - 3)
                    for h in range(4):
                        r, j = h % 2, h // 2
                        rows = slice(HD * r, HD * r + HD)
                        out = self.B[2 * (b % 4) + r][rows, j * P:j * P + P]
                        pe.matmul(out, VT[:, b, 512 + h * HD:512 + h * HD + HD], ACC[:, r, b // 2, 2 * (b % 2) + j, :],
                                  start=True, stop=False)
                        for d in range(2):
                            mm = pe.matmul(out, ST[rows, d * NB + order[d].index(b), j, :],
                                           T1[rows, 2 * d + j, b * P:b * P + P], start=False, stop=d == 1)
                    mm.then_inc(E, 1)

            @block.scalar
            def _(act):
                for b in range(nb):
                    act.wait_ge(E, p0 + b + 1)
                    for r in range(2):
                        rows = slice(HD * r, HD * r + HD)
                        src = self.B[2 * (b % 4) + r][rows, 0:256].rearrange("p (j n) -> p j n", j=2)
                        ins = act.activation(F[rows, 4:6, b * P:b * P + P], src, ACT.Copy)
                    ins.then_inc(A, 1)

    def mod2_rider(self, li):
        return Rider(f"ada2_{li}", "condc", 2, [(0, 24, WC["mod2b" if li else "mod2"], VC["b_ada"] + 48 * li)])

    def second_block(self):
        self.lambdas()
        for li in range(2):
            m2 = WC["mod2b" if li else "mod2"]
            ctx = li == 0

            def segs(q, scale=True):
                return [(m2 + 16 * q + j, m2 + 16 * q + 16 + j, 2) for j in range(2)]

            def gate(q):
                return [(m2 + 16 * q + j, 2) for j in range(2)]
            self.norm(("norm1_w", 8 * li), segs(0), ctx=True)
            F, VT = self.region(f"proj{li}", [("f", [P, 18, TA], F32), ("v", [P, TA // P, TA], F32)])
            self.arena_tail = self.arena + 18 * TA * 4 + TA // P * TA * 4
            self.plain_product(f"in_{li}a", F, 0, True)
            self.plain_product(f"in_{li}b", F, 8, ctx)
            self.token_product(f"in_{li}v", VT)
            self.rope(F, li)
            self.diff_attention(F, VT, li)
            W = TA if ctx else TX
            self.head_norms(f"a{li}", F, [8, 9, 10, 11], self.ONES[:, :], 1.0 / (2 * HD), self.vec("subln", li), 0, W)
            self.fourier(F, li)
            self.recurrence(F, VT, li)
            self.head_norms(f"r{li}", F, [4, 5], self.HALF[:, :], 1.0 / HD, self.vec("hgrn_w", li), 4, W,
                            gates=F[:, 14:16, :])
            if self.upto == f"cat{li}":
                return
            self.add_product(f"out_{li}", gate(2), ctx=ctx)
            if self.upto == f"mix{li}":
                return
            self.norm(("norm2_w", 8 * li), segs(3), ctx=ctx)
            self.ffn(f"g{li}", gate(5), VC["conv2_w"] + 132 * li, VC["conv2_b"] + 44 * li, True,
                     None if li else self.mod2_rider(1))
            if self.upto == f"b2_{li}":
                return
        self.norm(("final_w", 0), final=True)

    def finish(self):
        n = self.out_stored.after(16)
        with self.nc.Block() as block:
            @block.sync
            def _(sync):
                sync.dma_start(self.out, self.X[:, :, 0:TX]).then_inc(self.out_stored.handle, 16)
                sync.wait_ge(self.out_stored.handle, n + 16)

    def build(self):
        m1 = WC["mod1"]
        def stop(name):
            return self.upto == name
        self.begin()
        self.norm(("norm1_g", 0), [(m1, m1 + 8, 1)])
        self.pool_mixer()
        if stop("pool"): return self.finish()
        self.norm(("norm2_g", 0), [(m1 + 24, m1 + 32, 1)])
        self.ffn("f0", [(m1 + 40, 1)], VC["conv1_w"], VC["conv1_b"], False,
                 Rider("ada1", "cond", 1, [(0, 24, WC["mod1b"], VC["ada_b"] + 48)]))
        if stop("ffn0"): return self.finish()
        m1 = WC["mod1b"]
        self.dilated_attention(m1, WC["kvmod"])
        self.add_product("wo", [(m1 + 16, 1)])
        if stop("attn"): return self.finish()
        self.norm(("norm2_g", 8), [(m1 + 24, m1 + 32, 1)])
        self.ffn("f1", [(m1 + 40, 1)], VC["conv1_w"] + 66, VC["conv1_b"] + 22, False,
                 self.mod2_rider(0))
        self.norm(("final_g", 0), final=True)
        if stop("first"): return self.finish()
        self.second_block()
        self.finish()


def program(nc, aps, out, upto=None):
    with ExitStack() as ctx:
        Program(nc, ctx, aps, out, upto).build()


def cols(v):
    v = np.asarray(v)
    return v.reshape(-1, P).T


def items(w, order=None):
    w = np.asarray(w)
    K, N = w.shape
    kt = K // P
    if order is not None:
        w = w.reshape(K, N // P, P)[:, order].reshape(K, -1)
        N = w.shape[1]
    out = w.reshape(kt, P, N // 256, 256).transpose(2, 1, 0, 3).reshape(N // 256, P, kt * 256)
    if kt < KT:
        out = np.concatenate([out, np.zeros((N // 256, P, ITEM - kt * 256), w.dtype)], axis=2)
    return out


def ffn_items(up, down):
    out = []
    pairs = [t for j in range(FT) for t in (j, FT + j)]
    both = items(up, pairs)
    for first, n in FGROUPS:
        out += [both[first:first + n], items(down[first * P:(first + n) * P])]
    return out


def group_items(w):
    w = np.asarray(w).reshape(4, 2, P, 2, P)
    w = w.transpose(0, 3, 2, 1, 4).reshape(2, 4, P, 2 * P)
    w = w.transpose(0, 2, 1, 3).reshape(2, P, 8 * P)
    return np.concatenate([w, np.zeros((2, P, ITEM - 8 * P), w.dtype)], axis=2)


def weight_array(g):
    w = [items(g["pool_w_in"][0]), group_items(g["pool_w_grp"][0]), items(g["pool_w_out"][0])]
    w += ffn_items(g["ffn_w_up"][0], g["ffn_w_down"][0])
    kv = items(g["w_kv"])
    w += [items(g["attn_w_q"][0]), kv[:12], kv[12:16], kv[16:24],
          items(g["attn_w_o"][0])]
    w += ffn_items(g["ffn_w_up"][1], g["ffn_w_down"][1])
    for li in range(2):
        w += [items(g["w_in_2"][li], [4, 5, 6, 7, 14, 15, 16, 17, 0, 1, 2, 3, 12, 13, 20, 21, 22, 23, 8, 9, 10, 11, 18, 19]),
              items(g["w_out_2"][li])]
        w += ffn_items(g["w_up_2"][li], g["w_down_2"][li])
    out = np.concatenate(w)
    assert out.shape == (N_ITEMS, P, ITEM), (out.shape, N_ITEMS)
    return out


def mod_array(g):
    a = items(g["ada_w"][0])
    w = [a[0:12], a[20:24], a[12:16], a[16:20], items(g["ada_w"][1]), items(g["kv_ada_w"])]
    return np.concatenate(w + [items(g["w_ada_2"][li]) for li in range(2)])


def vector_array(g):
    out = np.zeros((P, NVEC), np.float32)

    def put(name, a):
        at, n = VC.at[name]
        assert a.shape == (P, n), (name, a.shape, n)
        out[:, at:at + n] = a
    put("c", cols(g["c"]))
    put("cc", np.stack([cols(g["c_2"]), cols(g["c_ctx_2"])], axis=2).reshape(P, 16))
    for name, key in (("ada_b", "ada_b"), ("kv_ada_b", "kv_ada_b"), ("b_ada", "b_ada_2"), ("norm1_g", "norm1_g"),
                      ("norm2_g", "norm2_g"), ("kv_norm_g", "kv_norm_g"), ("final_g", "final_g"),
                      ("pool_scale", "pool_scale"), ("norm1_w", "norm1_w_2"), ("norm2_w", "norm2_w_2"),
                      ("final_w", "final_norm_w_2"), ("conv1_b", "ffn_conv_b"), ("conv1_w", "ffn_conv_w"),
                      ("conv2_b", "conv_b_2"), ("conv2_w", "conv_w_2"), ("subln", "subln_w_2"),
                      ("lb", "lb_param_2")):
        put(name, cols(g[key]))
    put("hgrn_w", np.concatenate([g["hgrn_norm_w_2"].T, g["hgrn_norm_w_2"].T]))
    lam = g["lam_qk_2"].transpose(2, 0, 1).reshape(64, 8)
    put("lam", np.concatenate([lam, np.zeros_like(lam)]))
    return out


def alibi_slopes(n):
    def pow2(m):
        start = 2.0 ** (-(2.0 ** -(math.log2(m) - 3)))
        return [start ** (i + 1) for i in range(m)]
    c = 2 ** math.floor(math.log2(n))
    s = pow2(c) if c == n else pow2(c) + pow2(2 * c)[0::2][: n - c]
    return -np.sort(-np.asarray(s, np.float32))


def constants():
    out = {"ident": np.eye(P, dtype=np.float32)}
    edge = np.zeros((4, 16), np.float32)
    for g in range(4):
        w = 2 << g
        edge[g] = 1.0 / np.minimum(np.arange(16) + 1, w)
    key = np.arange(TX)
    dist = np.full((P, 4, TX), BIG, np.float32)
    for c in range(4):
        back = (4 * np.arange(P) + c)[:, None] - key[None]
        ok = (back >= 0) & (back <= 128)
        dist[:, c][ok] = back[ok]
    back = np.arange(P)[:, None] - np.arange(P)[None]
    near = np.full((P, 2, P), BIG, np.float32)
    near[:, 0][back >= 0] = 4.0 * back[back >= 0]
    ok = (back >= 0) & (back % 4 == 0)
    near[:, 1][ok] = 4.0 * back[ok]
    out["dist0"], out["dist12"] = dist, near
    out["slopes"] = np.broadcast_to(-alibi_slopes(NBR * NH1) * HD ** 0.5, (P, NBR * NH1)).astype(np.float32)
    masks = np.zeros((P, 2 * LEVELS, P), np.int32)
    a, b = np.arange(P)[:, None], np.arange(P)[None]
    for lv in range(LEVELS):
        same = a >> (lv + 1) == b >> (lv + 1)
        for d in range(2):
            masks[:, 2 * lv + d] = same & ((a >> lv & 1) == d) & ((b >> lv & 1) == 1 - d)
    out["level_masks"] = masks
    out["block_reset"] = np.broadcast_to((np.arange(TA) % P != 0).astype(np.float32), (P, TA)).copy()
    out["half"] = np.kron(np.eye(2), np.ones((HD, HD))).astype(np.float32)
    inv = 10000.0 ** (-np.arange(0, 32, 2, dtype=np.float32) / np.float32(32))
    t = np.arange(TX)
    ang_r = (t // 64).astype(np.float32)[:, None] * inv.astype(np.float32)
    ang_c = (t % 64).astype(np.float32)[:, None] * inv.astype(np.float32)
    ang = np.concatenate([ang_r, ang_r, ang_c, ang_c] * 2, axis=1).T
    out["rope_cs"] = np.stack([np.cos(ang), np.sin(ang)], axis=1).astype(np.float32)
    perm = np.zeros((P, P), np.float32)
    for lo in range(0, P, 32):
        for i in range(16):
            perm[lo + i + 16, lo + i] = -1.0
            perm[lo + i, lo + i + 16] = 1.0
    out["rope_perm"] = perm
    n = np.arange(TX)
    ang = 2 * np.pi * (np.outer(n, n) % TX) / TX
    out["dft"] = np.stack([np.cos(ang), -np.sin(ang)]).reshape(2, 4, P, TX).transpose(2, 0, 1, 3).astype(np.float32)
    n = np.arange(64)
    ang = 2 * np.pi * (np.outer(n, n) % 64) / 64
    out["dft64"] = np.concatenate([np.kron(np.eye(2), np.cos(ang)), np.kron(np.eye(2), np.sin(ang))], axis=1).astype(np.float32)
    out["pool_edge"] = np.broadcast_to(edge, (P, 4, 16)).copy()
    return out


def host_inputs(g):
    g = {k: np.asarray(v) for k, v in g.items()}
    return {
        "weights": weight_array(g), "mods": mod_array(g), "vectors": vector_array(g),
        "xT": np.ascontiguousarray(g["x"][0].T.reshape(KT, P, TX).transpose(1, 0, 2)),
        "ctxT": np.ascontiguousarray(g["ctx_2"][0].T.reshape(KT, P, TC).transpose(1, 0, 2)),
        "w_fnet": np.ascontiguousarray(g["w_fnet_2"].reshape(2, 2, P, 256).transpose(0, 2, 1, 3)),
        **constants(),
    }


def kernel(**inputs):
    import concourse.bacc as bacc
    from concourse.bass_utils import run_bass_kernel_spmd

    nc = bacc.Bacc("TRN2", target_bir_lowering=False, num_devices=1)
    arrays = host_inputs(inputs)
    aps = {n: nc.dram_tensor(n, a.shape, mybir.dt.from_np(a.dtype), kind="ExternalInput").ap()
           for n, a in arrays.items()}
    out = nc.dram_tensor("out", (P, KT, TX), F32, kind="ExternalOutput").ap()
    program(nc, aps, out)
    r = run_bass_kernel_spmd(nc, [arrays], core_ids=[0])
    y = r.results[0]["out"]
    return np.ascontiguousarray(y.transpose(1, 0, 2).reshape(D, TX).T)[None]
```

```python
import math
from contextlib import ExitStack

import numpy as np
import concourse.bass as bass
from concourse import mybir

F32 = mybir.dt.float32
F32R = mybir.dt.float32r
ALU = mybir.AluOpType
ACT = mybir.ActivationFunctionType
AX = mybir.AxisListType.X

P = 128
D = 1024
KT = D // P
TX, TC = 512, 256
TA = TX + TC
FF = 2816
FT = FF // P
NBR, NH1, HD = 3, 16, 64
EPS = 1e-6
ITEM = KT * 2 * P
FGROUPS = [(0, 8), (8, 8), (16, 6)]
BIG = 1.0e30
LAM0 = [0.8 - 0.6 * math.exp(-0.3 * li) for li in range(2)]
LEVELS = 7


class Columns:
    def __init__(self):
        self.at, self.n = {}, 0

    def add(self, name, n):
        self.at[name] = (self.n, n)
        self.n += n

    def __getitem__(self, name):
        return self.at[name][0]


def vector_columns():
    c = Columns()
    for name, n in (("c", 8), ("cc", 16), ("ada_b", 96), ("kv_ada_b", 16), ("b_ada", 96),
                    ("norm1_g", 16), ("norm2_g", 16), ("kv_norm_g", 8), ("final_g", 8), ("pool_scale", 8),
                    ("norm1_w", 16), ("norm2_w", 16), ("final_w", 8), ("conv1_b", 44), ("conv1_w", 132),
                    ("conv2_b", 88), ("conv2_w", 264), ("subln", 2), ("hgrn_w", 2), ("lam", 8), ("lb", 8)):
        c.add(name, n)
    return c


VC = vector_columns()
NVEC = VC.n


def work_columns():
    c = Columns()
    for name, n in (("cond", 8), ("condc", 16), ("mod1", 48), ("mod1b", 48), ("kvmod", 16), ("mod2", 96), ("mod2b", 96), ("gs", 16), ("gs2", 16),
                    ("lam", 8), ("lb", 24), ("mx", 16), ("nb", 16), ("sum", 16), ("rs", 16), ("eps", 1)):
        c.add(name, n)
    return c


WC = work_columns()


def weight_plan():
    plan = [("pool_in", 4, 8), ("grp", 2, 4), ("pool_out", 4, 8)]
    plan += ffn_plan("f0")
    plan += [("wq", 12, 8), ("wk", 12, 8), ("wv0", 4, 8), ("wv1", 8, 8), ("wo", 4, 8)]
    plan += ffn_plan("f1")
    for li in range(2):
        plan += [(f"in_{li}a", 4, 8), (f"in_{li}b", 5, 8), (f"in_{li}v", 3, 8),
                 (f"out_{li}", 4, 8)]
        plan += ffn_plan(f"g{li}")
    return plan


def ffn_plan(name):
    out = []
    for g, (_, n) in enumerate(FGROUPS):
        out += [(f"{name}up{g}", n, 8), (f"{name}down{g}", 4, n)]
    return out


PLAN = weight_plan()
N_ITEMS = sum(n for _, n, _ in PLAN)
MODS = [("first", 16), ("shift", 4), ("scale", 4), ("ada1", 24), ("kvada", 8), ("ada2_0", 24), ("ada2_1", 24)]
MOD_BASE = {name: sum(n for _, n in MODS[:k]) for k, (name, _) in enumerate(MODS)}
N_MODS = sum(n for _, n in MODS)


class Signal:

    def __init__(self, handle):
        self.handle, self.n = handle, 0

    def after(self, count):
        was, self.n = self.n, self.n + count
        return was


class Step:

    def __init__(self, i, u):
        self.i, self.u = i, u
        self.l = i * 2 + u


class Ready:

    def __init__(self, handle, first, step):
        self.handle, self.first, self.step = handle, first, step

    def at(self, k):
        return self.first + self.step * k


class Stage:

    def __init__(self, base, n, kt):
        self.base, self.n, self.kt = base, n, kt


class Rider:

    def __init__(self, name, cond, ncol, runs, apart=False):
        self.apart = apart
        self.name, self.cond, self.ncol, self.runs = name, cond, ncol, runs
        self.base, self.n = MOD_BASE[name], dict(MODS)[name]
        self.k = 0


class Next:

    def __init__(self, s):
        self.i, self.u, self.l = s.i + s.u, 1 - s.u, s.l + 1


class Ahead:

    def __init__(self, s):
        self.i, self.u, self.l = s.i + 1, s.u, s.l + 2


def steps(eng, first, last, body):
    n = last - first
    if n >= 4:
        with eng.Fori(first // 2, last // 2) as i:
            for u in range(2):
                body(Step(i, u))
    else:
        for l in range(first, last - n % 2):
            body(Step(l // 2, l % 2))
    if n % 2:
        body(Step(last // 2, 0))


class Program:
    def __init__(self, nc, ctx, aps, out, upto=None):
        self.nc, self.ctx, self.aps, self.out, self.upto = nc, ctx, aps, out, upto
        self.pre = 0
        self.riders_done = []
        self.item = 0
        self.kt_of = [kt for _, n, kt in PLAN for _ in range(n)]
        self.plan = list(PLAN)
        self.freed = {}
        self.place_memory()
        s = lambda name: Signal(ctx.enter_context(nc.semaphore(name)))
        self.landed = [ctx.enter_context(nc.semaphore(f"weights_landed{k}")) for k in range(2)]
        self.hi_split = s("hi_split")
        self.lo_split = s("lo_split")
        self.raw_used = s("raw_used")
        self.mods_landed = [ctx.enter_context(nc.semaphore(f"mods_landed{k}")) for k in range(4)]
        self.ride_landed = [s(f"ride_landed{k}") for k in range(2)]
        self.ride_shared = s("ride_shared")
        self.ride_added = s("ride_added")
        self.ride_summed = s("ride_summed")
        self.tiles_done = s("tiles_done")
        self.freed_act = s("freed_by_scalar")
        self.freed_dve = s("freed_by_vector")
        self.act_step = s("act_step")
        self.dve_step = s("dve_step")
        self.pe_step = s("pe_step")
        self.pool_step = s("pool_step")
        self.loaded = s("loaded")
        self.stored = [s(f"stored{k}") for k in range(2)]
        self.normed = s("normed_tiles")
        self.started = s("started")
        self.out_stored = s("out_stored")

    def place_memory(self):
        nc = self.nc
        self.cursor = (nc.sbuf_base + 31) // 32 * 32
        self.end = nc.sbuf_top // 32 * 32

        def sb(name, shape, dt=F32):
            at = self.cursor
            self.cursor += (int(np.prod(shape[1:])) * 4 + 31) // 32 * 32
            return nc.alloc_sbuf_tensor_at(name, shape, dt, offset=at)

        self.X = sb("x_res", [P, KT, TA])
        self.HH = sb("h_hi", [P, KT, TA], F32R)
        self.HL = sb("h_lo", [P, KT, TA], F32R)
        self.RAW = sb("w_raw", [P, 2, ITEM])
        self.split_at = self.cursor
        self.WH = sb("w_hi", [P, 2, ITEM], F32R)
        self.WL = sb("w_lo", [P, 2, ITEM], F32R)
        self.split_end = self.cursor
        self.VEC = sb("vec", [P, NVEC])
        self.WK = sb("work_vec", [P, WC.n])
        self.ONES = sb("ones", [P, P])
        self.IDENT = sb("ident", [P, P])
        self.HALF = sb("ones_by_half", [P, P])
        self.arena = self.cursor
        self.ride_at = self.end - 2 * ITEM * 4 - 4 * 256 * 4
        self.RIDE = nc.alloc_sbuf_tensor_at("ride_raw", [P, 2, ITEM], F32, offset=self.ride_at)
        self.RTMP = nc.alloc_sbuf_tensor_at("ride_tmp", [P, ITEM], F32, offset=self.ride_at - ITEM * 4)
        self.RACC = nc.alloc_sbuf_tensor_at("ride_acc", [P, 2, 2, 256], F32, offset=self.ride_at + 2 * ITEM * 4)
        self.B = [self.ctx.enter_context(nc.psum_tensor(f"bank{k}", [P, 512], F32)) for k in range(8)]

    def region(self, stage, spec, start=None, end=None):
        at = self.arena if start is None else start
        end = self.end if end is None else end
        out = []
        for name, shape, dt in spec:
            size = int(np.prod(shape[1:])) * mybir.dt.size(dt)
            out.append(self.nc.alloc_sbuf_tensor_at(f"{stage}_{name}", shape, dt, offset=at))
            at += (size + 31) // 32 * 32
            assert at <= end, (stage, name, at - end)
        return out

    def vec(self, name, k=0, n=1):
        return self.VEC[:, VC[name] + k:VC[name] + k + n]

    def wk(self, name, k=0, n=1):
        return self.WK[:, WC[name] + k:WC[name] + k + n]

    def fetch(self, sync, m, kt, slot, wait=None):
        if wait is not None:
            sync.wait_ge(wait[0], wait[1])
        src = self.aps["weights"][bass.ds(m, 1), :, 0:kt * 256].rearrange("a p n -> p (a n)")
        sync.dma_start(self.RAW[:, slot, 0:kt * 256], src).then_inc(self.landed[slot], 16)

    def take(self, name):
        got, n, kt = self.plan.pop(0)
        assert got == name, (got, name)
        base = self.item
        self.item += n
        return base, n, kt

    def stream(self, sync, st, rider, ride):
        lo, n = self.lo_split.handle, st.n

        def one(s):
            self.fetch(sync, s.l + (st.base + 2), st.kt, (st.base + s.u) % 2, (lo, s.l + (st.lo0 + 1)))

        def both(s):
            one(s)
            self.ride_fetch(sync, rider, s, 2)
        first, last = st.pre, max(st.pre, n - 2)
        if ride:
            if rider.k == 0:
                for l in range(2):
                    self.ride_fetch(sync, rider, Step(0, l), 0)
            for l in range(0, first):
                self.ride_fetch(sync, rider, Step(0, l), 2)
            mid = ride - 2
            if first == 1:
                both(Step(0, 1))
                first = 2
            steps(sync, first, mid, both)
            if mid < last:
                steps(sync, mid, last, one)
            first = last
        else:
            if first == 1:
                one(Step(0, 1))
                first = 2
            steps(sync, first, last, one)
        for l in range(last, n + st.post):
            m = st.base + l + 2
            if m < N_ITEMS:
                self.fetch(sync, m, self.kt_of[m], m % 2, (lo, st.lo0 + l + 1))
            if ride == n and l < n and rider.k + l + 2 < rider.n:
                self.ride_fetch(sync, rider, Step(l // 2, l % 2), 2)

    def split_hi(self, act, st, s, kt=None):
        slot = (st.base + s.u) % 2
        act.wait_ge(self.landed[slot], s.i * 16 + 16 * ((st.base + s.u) // 2 + 1))
        if not (isinstance(s.l, int) and s.l < 2):
            act.wait_ge(self.tiles_done.handle, s.l * st.tpi + (st.done0 - st.tpi))
        n = (kt or st.kt) * 256
        act.activation(self.WH[:, slot, 0:n], self.RAW[:, slot, 0:n], ACT.Copy).then_inc(self.hi_split.handle, 1)

    def split_lo(self, dve, st, s, kt=None):
        slot = (st.base + s.u) % 2
        dve.wait_ge(self.hi_split.handle, s.l + (st.hi0 + 1))
        n = (kt or st.kt) * 256
        dve.tensor_tensor(self.WL[:, slot, 0:n], self.RAW[:, slot, 0:n], self.WH[:, slot, 0:n].bitcast(F32),
                          ALU.subtract).then_inc(self.lo_split.handle, 1)

    def ride_fetch(self, sync, rd, s, ahead):
        slot = s.u
        if ahead:
            if rd.apart:
                sync.wait_ge(self.ride_summed.handle, s.l + (self.ride0 + 3))
            else:
                sync.wait_ge(self.ride_added.handle, s.l + (self.ride0 + 1))
        src = self.aps["mods"][bass.ds(s.l + (rd.base + rd.k + ahead), 1), :, :].rearrange("a p n -> p (a n)")
        sync.dma_start(self.RIDE[:, slot, :], src).then_inc(self.ride_landed[slot].handle, 16)

    def weigh_by_vector(self, dve, item, acc, cond, stride=1):
        for k in range(KT):
            w, c = item[:, k * 256:k * 256 + 256], cond[:, k * stride:k * stride + 1]
            if k == 0:
                ins = dve.tensor_scalar(acc, w, c, None, ALU.mult)
            else:
                dve.drain()
                ins = dve.scalar_tensor_tensor(acc, w, c, acc, ALU.mult, ALU.add)
        return ins

    def weigh_by_pool(self, pool, item, acc, cond, stride=1, tmp=None):
        rows = item.rearrange("p (k n) -> p k n", k=KT)
        c = cond[:, 0:(KT - 1) * stride + 1:stride].rearrange("p (k a) -> p k a", a=1)
        if tmp is not None:
            item = tmp
        pool.tensor_tensor(item.rearrange("p (k n) -> p k n", k=KT), rows, c.broadcast_to([P, KT, 256]), ALU.mult)
        half = KT // 2
        while half >= 1:
            pool.drain()
            dst = item[:, 0:half * 256] if half > 1 else acc
            ins = pool.tensor_tensor(dst, item[:, 0:half * 256], item[:, half * 256:2 * half * 256], ALU.add)
            half //= 2
        return ins

    def ride_add(self, pool, rd, s):
        if rd.apart:
            pool.drain()
        if rd.ncol == 1 or rd.apart:
            pool.wait_ge(self.ride_landed[s.u].handle, s.i * 16 + (self.ride_landed[s.u].n + 16))
        else:
            pool.wait_ge(self.ride_shared.handle, s.l + (self.ride_shared.n + 1))
        pool.wait_ge(self.ride_summed.handle, s.l + (self.ride0 + 1))
        cond = self.wk(rd.cond, rd.ncol - 1, KT * rd.ncol - rd.ncol + 1)
        ins = self.weigh_by_pool(pool, self.RIDE[:, s.u, :], self.RACC[:, s.u, rd.ncol - 1, :], cond, rd.ncol,
                                 self.RTMP[:, :] if rd.apart else None)
        ins.then_inc(self.ride_added.handle, 1)

    def ride_share(self, dve, rd, s):
        dve.wait_ge(self.ride_landed[s.u].handle, s.i * 16 + (self.ride_landed[s.u].n + 16))
        dve.wait_ge(self.ride_summed.handle, s.l + (self.ride0 + 1))
        ins = self.weigh_by_vector(dve, self.RIDE[:, s.u, :], self.RACC[:, s.u, 0, :], self.wk(rd.cond, 0, 15), 2)
        ins.then_inc(self.ride_shared.handle, 1)

    def ride_sum(self, pe, rd, s):
        pe.wait_ge(self.ride_added.handle, s.l + (self.ride0 + 1))
        if rd.ncol == 2:
            pe.wait_ge(self.ride_shared.handle, s.l + (self.ride_shared.n + 1))
        for t in range(2):
            for j in range(rd.ncol):
                col = s.i * (2 * rd.ncol) + (256 + rd.k * rd.ncol + t * rd.ncol + j)
                mm = pe.matmul(self.B[5 + 2 * s.u][:, bass.ds(col, 1)], self.RACC[:, s.u, j, t * P:t * P + P],
                               self.ONES[:, 0:1], start=True, stop=True)
        mm.then_inc(self.ride_summed.handle, 1)

    def ride_finish(self, dve, rd):
        dve.wait_ge(self.ride_summed.handle, self.ride_summed.n)
        nc_ = rd.ncol
        for first, n, dest, bias in rd.runs:
            for u in range(2):
                src = self.B[5 + 2 * u][:, 256 + first * nc_:256 + (first + n) * nc_].rearrange(
                    "p (i t j) -> p i t j", t=2, j=nc_)
                out = self.WK[:, dest:dest + 2 * n * nc_].rearrange("p (i u t j) -> p i u t j", u=2, t=2, j=nc_)
                b = self.VEC[:, bias:bias + 2 * n].rearrange("p (i u t) -> p i u t", u=2, t=2)
                for j in range(nc_):
                    dve.tensor_tensor(out[:, :, u, :, j], src[:, :, :, j], b[:, :, u, :], ALU.add)

    def product(self, st, block, pe_tile, tpi, act_epi=None, dve_epi=None, freed=None, distance=4,
                post=2, rider=None, ready=None, inside=False):
        st.tpi, st.done0 = tpi, self.tiles_done.after(tpi * st.n)
        st.pre, st.post = self.pre, int(post) if st.base + st.n < N_ITEMS else 0
        self.pre = st.post
        st.hi0, st.lo0 = (x.after(st.n - st.pre + st.post) - st.pre for x in (self.hi_split, self.lo_split))
        st.free0 = freed.after(tpi * st.n)
        done, n = self.tiles_done.handle, st.n
        ride = 0 if rider is None else min(n, rider.n - rider.k)
        self.ride0 = self.ride_added.n
        assert ride in (0, n) or rider.ncol == 1

        @block.sync
        def _(sync):
            self.stream(sync, st, rider, ride)

        def program(eng, epilogue, split, share=False):
            if share and rider.k == 0:
                self.ride_share(eng, rider, Step(0, 0))
            for l in range(st.pre, 2):
                split(eng, st, Step(0, l))

            def both(s):
                if share:
                    self.ride_share(eng, rider, Next(s))
                if inside:
                    epilogue(eng, s, lambda: split(eng, st, Ahead(s)))
                    return
                if epilogue is not None:
                    epilogue(eng, s)
                split(eng, st, Ahead(s))
            steps(eng, 0, n - 2, both)
            for l in (n - 2, n - 1):
                if share and rider.k + l + 1 < rider.n:
                    self.ride_share(eng, rider, Next(Step(l // 2, l % 2)))
                following = lambda: split(eng, st, Step((l + 2) // 2, l % 2), self.kt_of[st.base + l + 2])
                if inside:
                    epilogue(eng, Step(l // 2, l % 2), following if l + 2 < n + st.post else lambda: None)
                    continue
                if epilogue is not None:
                    epilogue(eng, Step(l // 2, l % 2))
                if l + 2 < n + st.post:
                    following()

        @block.scalar
        def _(act):
            program(act, act_epi, self.split_hi)

        @block.vector
        def _(dve):
            program(dve, dve_epi, self.split_lo, share=ride > 0 and rider.ncol == 2)

        @block.tensor
        def _(pe):
            def item(s, riding=False):
                slot = (st.base + s.u) % 2
                pe.wait_ge(self.lo_split.handle, s.l + (st.lo0 + 1))
                for t in range(tpi):
                    pe.wait_ge(freed.handle, s.l * tpi + (st.free0 + t + 1 - distance))
                    if riding and t == 1:
                        self.ride_sum(pe, rider, s)
                    pe_tile(pe, slot, s, t).then_inc(done, 1)
            first = 0
            if ready is not None:
                s = Step(0, 0)
                slot = st.base % 2
                pe.wait_ge(self.lo_split.handle, st.lo0 + 1)
                pe.wait_ge(freed.handle, st.free0 + 2 - distance)
                for k in range(pe_tile.kt):
                    pe.wait_ge(ready.handle, ready.at(k))
                    for t in range(2):
                        last = k == pe_tile.kt - 1
                        riding = ride > 0 and last and t == 1
                        mm = pe_tile.part(pe, slot, s, t, k, (lambda: self.ride_sum(pe, rider, s)) if riding else None)
                        if last:
                            mm.then_inc(done, 1)
                item(Step(0, 1), ride > 0)
                first = 2
            if ride:
                steps(pe, first, ride, lambda s: item(s, True))
                first = ride
            if first < n:
                steps(pe, first, n, item)

        if ride:
            @block.gpsimd
            def _(pool):
                steps(pool, 0, ride, lambda s: self.ride_add(pool, rider, s))
            if rider.ncol == 2:
                self.ride_shared.after(ride)
            self.ride_added.after(ride)
            self.ride_summed.after(ride)
            for x in self.ride_landed:
                x.after(8 * ride)
            rider.k += ride
            if rider.k == rider.n:
                self.riders_done.append(rider)

    def end_rides(self, block):
        @block.vector
        def _(dve):
            for rd in self.riders_done:
                self.ride_finish(dve, rd)
        self.riders_done = []

    def three(self, pe, out, w, x, start, stop):
        (wh, wl), (xh, xl) = w, x
        pe.matmul(out, wh, xh, start=start, stop=False)
        pe.matmul(out, wh, xl, start=False, stop=False)
        return pe.matmul(out, wl, xh, start=False, stop=stop)

    def feature_tile(self, kt, hi, lo, ctx):
        def part(pe, slot, s, t, k, between=None):
            outs = [(self.B[4 + 2 * s.u + t][:, 0:TC], TX, TA)] if ctx else []
            outs.append((self.B[2 * s.u + t][:, :], 0, TX))
            c = k * 256 + t * P
            for out, a, b in outs:
                if a == 0 and between is not None:
                    between()
                mm = self.three(pe, out, (self.WH[:, slot, c:c + P], self.WL[:, slot, c:c + P]),
                                (hi[:, k, a:b], lo[:, k, a:b]), k == 0, k == kt - 1)
            return mm

        def tile(pe, slot, s, t):
            for k in range(kt):
                mm = part(pe, slot, s, t, k)
            return mm
        tile.part, tile.kt = part, kt
        return tile

    def token_tile(self, blocks):
        def tile(pe, slot, s, t):
            for k in range(KT):
                c = k * 256
                x = (self.HH[:, k, blocks[t]], self.HL[:, k, blocks[t]])
                w = (self.WH[:, slot, c:c + 256], self.WL[:, slot, c:c + 256])
                (wh, wl), (xh, xl) = w, x
                pe.matmul(self.B[t][:, 0:256], xh, wh, start=k == 0, stop=False)
                pe.matmul(self.B[t][:, 0:256], xl, wh, start=False, stop=False)
                mm = pe.matmul(self.B[t][:, 0:256], xh, wl, start=False, stop=k == KT - 1)
            return mm
        return tile

    def act_ready(self, act):
        act.wait_ge(self.started.handle, 1)

    def begin(self):
        nc, a = self.nc, self.aps
        n_mods, turn = dict(MODS)["first"], 4
        land = self.mods_landed

        FIRST, = self.region("first", [("mods", [P, turn, ITEM], F32)], self.split_at, self.split_end)

        def acc(k):
            return self.RACC[:, k // 2, k % 2, :]
        added = [(self.dve_step, 3, k) for k in range(3)] + [(self.pool_step, 1, 0)]
        self.dve_step.after(n_mods // turn * 3)
        self.pool_step.after(n_mods // turn)

        def weighed(eng, i, k):
            signal, per, place = added[k]
            eng.wait_ge(signal.handle, i * per + (place + 1))

        def weigh_item(eng, i, k):
            eng.wait_ge(land[k], i * 16 + 16)
            eng.wait_ge(self.raw_used.handle, i * turn + (k + 1))
            by = self.weigh_by_pool if k == turn - 1 else self.weigh_by_vector
            by(eng, FIRST[:, k, :], acc(k), self.wk("cond", 0, KT)).then_inc(added[k][0].handle, 1)
        with nc.Block() as block:
            @block.sync
            def _(sync):
                sync.dma_start(self.VEC[:, :], a["vectors"]).then_inc(self.loaded.handle, 16)

                def mod(m, k):
                    sync.dma_start(FIRST[:, k, :], a["mods"][bass.ds(m, 1), :, :].rearrange("a p n -> p (a n)")
                                   ).then_inc(land[k], 16)
                for k in range(turn):
                    mod(k, k)
                with sync.Fori(0, n_mods // turn - 1) as i:
                    for k in range(turn):
                        weighed(sync, i, k)
                        mod(i * turn + (k + turn), k)
                for m in range(2):
                    self.fetch(sync, m, self.kt_of[m], m)

            @block.gpsimd
            def _(pool):
                pool.memset(self.ONES[:, :], 1.0).then_inc(self.raw_used.handle, 4)
                pool.wait_ge(self.started.handle, 1)
                pool.drain()
                with pool.Fori(0, n_mods // turn) as i:
                    weigh_item(pool, i, turn - 1)

            @block.vector
            def _(dve):
                dve.memset(self.wk("eps"), EPS)
                dve.memset(self.wk("mx", 0, 16), 0.0).then_inc(self.freed_dve.handle, 8)
                dve.wait_ge(self.started.handle, 1)
                with dve.Fori(0, n_mods // turn) as i:
                    for k in range(turn - 1):
                        weigh_item(dve, i, k)
                dve.wait_ge(self.raw_used.handle, n_mods + 4)
                half, quarter = n_mods, n_mods // 2
                for dest, src, n in ((0, 0, half), (half, half, quarter), (half + 3 * quarter, half + quarter, quarter)):
                    dve.tensor_tensor(self.wk("mod1", dest, n), self.B[0][:, src:src + n], self.vec("ada_b", dest, n),
                                      ALU.add)

            @block.scalar
            def _(act):
                act.dma_start(self.X[:, :, 0:TX], a["xT"]).then_inc(self.loaded.handle, 16)
                act.wait_ge(self.loaded.handle, 32)
                act.activation(self.wk("cond", 0, 8), self.vec("c", 0, 8), ACT.Silu).then_inc(self.freed_act.handle, 8)
                act.activation(self.wk("condc", 0, 16), self.vec("cc", 0, 16), ACT.Silu).then_inc(self.started.handle, 1)
                act.activation(self.wk("nb", 0, 2), self.vec("c", 0, 2), ACT.Copy).then_inc(self.ride_summed.handle, 2)
                for k in range(2):
                    act.activation(self.wk("rs", k), self.vec("c", k), ACT.Copy).then_inc(self.stored[k].handle, 16)
                for t, src in ((self.IDENT[:, :], a["ident"]), (self.HALF[:, :], a["half"]),
                               (self.X[:, :, TX:TA], a["ctxT"])):
                    act.dma_start(t, src).then_inc(self.loaded.handle, 16)
                act.wait_ge(self.loaded.handle, 80)

            @block.tensor
            def _(pe):
                with pe.Fori(0, n_mods // turn) as i:
                    for k in range(turn):
                        weighed(pe, i, k)
                        for t in range(2):
                            out = self.B[0][:, bass.ds(i * (2 * turn) + (2 * k + t), 1)]
                            mm = pe.matmul(out, acc(k)[:, t * P:t * P + P], self.ONES[:, 0:1], start=True, stop=True)
                        mm.then_inc(self.raw_used.handle, 1)
        self.loaded.after(80)
        self.ride_summed.after(2)
        self.freed_dve.after(8)
        self.freed_act.after(8)
        self.started.after(1)
        for k in range(2):
            self.stored[k].after(16)

    def norm(self, block, g, mods=None, ctx=False, final=False, start=None):
        W = TA if ctx else TX
        spans = [(0, TX)] + ([(TX, TA)] if ctx else [])
        tag = f"norm{self.item}_{g[0]}"
        SQ, R = self.region(tag, [("sq", [P, KT, W], F32), ("rstd", [P, W], F32)], start)
        a0, d0, p0 = (x.n for x in (self.act_step, self.dve_step, self.pe_step))
        A, V, E = (x.handle for x in (self.act_step, self.dve_step, self.pe_step))
        gs = [self.wk("gs", 0, 8), self.wk("gs2", 0, 8)]

        def mod(j, kind, k):
            col, stride = mods[j][kind], mods[j][2]
            return self.WK[:, col + stride * k:col + stride * k + 1]

        @block.scalar
        def _(act):
            for q in range(4):
                act.activation(SQ[:, 2 * q:2 * q + 2, :], self.X[:, 2 * q:2 * q + 2, 0:W], ACT.Square,
                               scale=D ** -0.5).then_inc(A, 1)
            act.activation(self.wk("rs", 12), self.wk("eps"), ACT.Sqrt)
            act.wait_ge(E, p0 + 1)
            for b, (s, e) in enumerate(spans):
                ins = act.activation(R[:, s:e], self.B[b][:, 0:e - s], ACT.Sqrt, bias=self.wk("eps"))
            ins.then_inc(A, 1)
            for k in range(KT):
                act.wait_ge(V, d0 + 2 + k)
                if final:
                    act.activation(self.X[:, k, 0:W], SQ[:, k, :], ACT.Copy, scale=self.vec(g[0], g[1] + k)).then_inc(A, 1)
                    continue
                for dst in (self.HH, SQ):
                    for j, (s, e) in enumerate(spans):
                        ins = act.activation(dst[:, k, s:e], SQ[:, k, s:e], ACT.Identity,
                                             scale=gs[j][:, k:k + 1], bias=mod(j, 0, k))
                ins.then_inc(A, 1)

        @block.vector
        def _(dve):
            if not final:
                for j in range(len(spans)):
                    col, stride = mods[j][1], mods[j][2]
                    dve.scalar_tensor_tensor(gs[j], self.WK[:, col:col + 8 * stride:stride], 1.0,
                                             self.vec(g[0], g[1], 8), ALU.add, ALU.mult)
            for q in range(1, 4):
                dve.wait_ge(A, a0 + q + 1)
                dve.tensor_tensor(SQ[:, 0:2, :], SQ[:, 0:2, :], SQ[:, 2 * q:2 * q + 2, :], ALU.add)
                dve.drain()
            dve.tensor_tensor(SQ[:, 0, :], SQ[:, 0, :], SQ[:, 1, :], ALU.add).then_inc(V, 1)
            dve.wait_ge(A, a0 + 5)
            dve.reciprocal(R[:, :], R[:, :])
            dve.drain()

            def scale(k):
                dve.tensor_tensor(SQ[:, k, :], self.X[:, k, 0:W], R[:, :], ALU.mult).then_inc(V, 1)

            def low(k):
                dve.wait_ge(A, a0 + 6 + k)
                dve.tensor_tensor(self.HL[:, k, 0:W], SQ[:, k, :], self.HH[:, k, 0:W].bitcast(F32),
                                  ALU.subtract).then_inc(self.normed.handle, 1)
            for k in range(KT):
                scale(k)
                if not final and k >= 2:
                    low(k - 2)
            if not final:
                low(KT - 2)
                low(KT - 1)

        @block.tensor
        def _(pe):
            pe.wait_ge(V, d0 + 1)
            for b, (s, e) in enumerate(spans):
                mm = pe.matmul(self.B[b][:, 0:e - s], self.ONES[:, :], SQ[:, 0, s:e], start=True, stop=True)
            mm.then_inc(E, 1)

        self.act_step.after(5 + KT)
        self.dve_step.after(1 + KT)
        self.pe_step.after(1)
        if not final:
            return Ready(self.normed.handle, self.normed.after(KT) + 1, 1)

    def residual_epilogue(self, st, gate, ctx):
        def epi(dve, s):
            for t in range(2):
                dve.wait_ge(self.tiles_done.handle, s.l * 2 + (st.done0 + t + 1))
                m = s.l * 2 + t
                outs = [(self.B[2 * s.u + t][:, :], 0, TX, gate[0])]
                if ctx:
                    outs.append((self.B[4 + 2 * s.u + t][:, 0:TC], TX, TA, gate[1]))
                for bank, a, b, (col, stride) in outs:
                    x = self.X[:, bass.ds(m, 1), a:b].rearrange("p a n -> p (a n)")
                    ins = dve.scalar_tensor_tensor(x, bank, self.WK[:, bass.ds(m * stride + col, 1)], x,
                                                   ALU.mult, ALU.add)
                ins.then_inc(self.freed_dve.handle, 1)
        return epi

    def add_product(self, name, gate, hi=None, lo=None, ctx=False, rider=None, ready=None, block=None, post=1):
        st = Stage(*self.take(name))
        hi, lo = (self.HH, self.HL) if hi is None else (hi, lo)

        def body(block):
            self.product(st, block, self.feature_tile(st.kt, hi, lo, ctx), 2,
                         dve_epi=self.residual_epilogue(st, gate, ctx), freed=self.freed_dve, rider=rider,
                         ready=ready, post=post)
        if block is not None:
            return body(block)
        with self.nc.Block() as block:
            body(block)
            self.end_rides(block)

    def plain_product(self, name, dest, first, ctx=False, rider=None, norm=None):
        st = Stage(*self.take(name))

        def epi(act, s):
            for t in range(2):
                act.wait_ge(self.tiles_done.handle, s.l * 2 + (st.done0 + t + 1))
                self.act_ready(act)
                d = dest[:, bass.ds(s.l * 2 + (first + t), 1), :].rearrange("p a n -> p (a n)")
                ins = act.activation(d[:, 0:TX], self.B[2 * s.u + t][:, :], ACT.Copy)
                if ctx:
                    ins = act.activation(d[:, TX:TA], self.B[4 + 2 * s.u + t][:, 0:TC], ACT.Copy)
                ins.then_inc(self.freed_act.handle, 1)
        with self.nc.Block() as block:
            ready = None if norm is None else norm(block)
            self.product(st, block, self.feature_tile(st.kt, self.HH, self.HL, ctx), 2, act_epi=epi,
                         freed=self.freed_act, rider=rider, ready=ready)
            self.end_rides(block)

    def ffn(self, name, norm, gate, wcol, bcol, centered, rider=None):
        ctx = centered and name == "g0"
        W = TA if ctx else TX
        GH, GL, CA, CV = self.region(name, [("g_hi", [P, 8, W], F32R), ("g_lo", [P, 8, W], F32R),
                                            ("conv_a", [P, 2, W], F32), ("conv_v", [P, 2, W], F32)],
                                     end=self.ride_at - (0 if ctx else ITEM * 4))
        with self.nc.Block() as block:
            ready = norm(block)
            for g in range(len(FGROUPS)):
                self.ffn_group(block, name, g, gate, wcol, bcol, centered, rider, (GH, GL, CA, CV),
                               ready if g == 0 else None)
            self.end_rides(block)

    def ffn_group(self, block, name, g, gate, wcol, bcol, centered, rider, tensors, ready):
        GH, GL, CA, CV = tensors
        first = FGROUPS[g][0]
        ctx = centered and name == "g0"
        W = TA if ctx else TX
        taps = 2 * FT if centered else FT
        st = Stage(*self.take(f"{name}up{g}"))
        a0, v0 = self.act_step.after(3 * st.n), self.dve_step.after(2 * st.n)
        A, V = self.act_step.handle, self.dve_step.handle

        def col(base, tap, s, half):
            return self.VEC[:, bass.ds(s.l + (base + taps * tap + half * FT + first), 1)]

        def banks(s, t):
            out = [(self.B[2 * s.u + t][:, :], 0, TX)]
            if ctx:
                out.append((self.B[4 + 2 * s.u + t][:, 0:TC], TX, TA))
            return out

        def act_epi(act, s, split):
            act.wait_ge(self.tiles_done.handle, s.l * 2 + (st.done0 + 2))
            act.wait_ge(V, s.l * 2 + (v0 - 2))
            self.act_ready(act)
            here = 1 if centered else 2
            for t, dst in enumerate((CA, CV) if centered else (CA,)):
                for bank, a, b in banks(s, t):
                    ins = act.activation(dst[:, s.u, a:b], bank, ACT.Identity, scale=col(wcol, here, s, t),
                                         bias=col(bcol, 0, s, t))
            ins.then_inc(A, 1)
            split()
            act.wait_ge(*((self.freed_dve.handle, s.l * 2 + (st.free0 + 2)) if centered else
                          (V, s.l * 2 + (v0 + 1))))
            act.activation(CA[:, s.u, :], CA[:, s.u, :], ACT.Silu).then_inc(A, 1)
            act.wait_ge(*((V, s.l * 2 + (v0 + 1)) if centered else
                          (self.freed_dve.handle, s.l * 2 + (st.free0 + 2))))
            self.act_ready(act)
            act.activation(GH[:, bass.ds(s.l, 1), :].rearrange("p a n -> p (a n)"), CA[:, s.u, :],
                           ACT.Copy).then_inc(A, 1)

        def dve_epi(dve, s, split):
            dve.wait_ge(A, s.l * 3 + (a0 + 1))
            for tap, back in (((0, 1), (2, -1)) if centered else ((1, 1), (0, 2))):
                for t, dst in enumerate((CA, CV) if centered else (CA,)):
                    for bank, a, b in banks(s, t):
                        n = b - a
                        to = dst[:, s.u, a + max(back, 0):b + min(back, 0)]
                        ins = dve.scalar_tensor_tensor(to, bank[:, max(-back, 0):n - max(back, 0)],
                                                       col(wcol, tap, s, t), to, ALU.mult, ALU.add)
                if back > 0 and not (back == 2):
                    dve.drain()
            if centered:
                ins.then_inc(self.freed_dve.handle, 2)
            else:
                ins.then_inc(V, 1)
            split()
            dve.wait_ge(A, s.l * 3 + (a0 + 2))
            if centered:
                dve.tensor_tensor(CA[:, s.u, :], CA[:, s.u, :], CV[:, s.u, :], ALU.mult).then_inc(V, 1)
            else:
                dve.tensor_tensor(CA[:, s.u, :], CA[:, s.u, :], self.B[2 * s.u + 1][:, :],
                                  ALU.mult).then_inc(self.freed_dve.handle, 2)
            dve.wait_ge(A, s.l * 3 + (a0 + 3))
            low = GL[:, bass.ds(s.l, 1), :].rearrange("p a n -> p (a n)")
            high = GH[:, bass.ds(s.l, 1), :].rearrange("p a n -> p (a n)")
            dve.tensor_tensor(low, CA[:, s.u, :], high.bitcast(F32), ALU.subtract).then_inc(V, 1)

        def going(rd):
            return rd if rd is not None and rd.k < rd.n else None
        self.product(st, block, self.feature_tile(KT, self.HH, self.HL, ctx), 2, act_epi=act_epi,
                     dve_epi=dve_epi, freed=self.freed_dve, rider=going(rider), ready=ready,
                     inside=True)
        self.add_product(f"{name}down{g}", gate, GH, GL, ctx, going(rider), Ready(V, v0 + 2, 2), block,
                         post=1 if g == len(FGROUPS) - 1 else 2)

    def pool_mixer(self):
        U, CS, DF, RC, ON = self.region("pool", [
            ("u", [P, KT, TX], F32), ("csum", [P, 2, TX], F32), ("pooled", [P, 2, TX], F32), ("edge", [P, 4, 16], F32),
            ("ones", [P, TX], F32)])
        self.pooled_at = self.arena + (KT + 5) * TX * 4 + 256
        PH, PL = self.region("pool2", [("p_hi", [P, KT, TX], F32R), ("p_lo", [P, KT, TX], F32R)], self.pooled_at)
        ada = VC["ada_b"]
        mod = WC["mod1"]
        A, V = self.act_step.handle, self.dve_step.handle
        l0 = self.loaded.after(16)
        st = Stage(*self.take("pool_in"))

        def pooled(k):
            return self.pool_a0 + k, self.pool_v0 + 2 * k

        def act_in(act, s, split):
            for t in range(2):
                k = s.l * 2 + t
                act.wait_ge(self.tiles_done.handle, st.done0 + k + 1)
                act.activation(U[:, k, :], self.B[2 * s.u + t][:, :], ACT.Copy).then_inc(self.freed_act.handle, 1)
            split()
            for t in range(2):
                k = s.l * 2 + t
                act.wait_ge(V, pooled(k)[1] + 1)
                act.activation(PH[:, k, :], DF[:, k % 2, :], ACT.Copy).then_inc(A, 1)

        def dve_in(dve, s, split):
            if s.l == 0:
                dve.wait_ge(self.loaded.handle, l0 + 16)
            for t in range(2):
                k = s.l * 2 + t
                w = 2 << (k // 2)
                cs, df, u = CS[:, k % 2, :], DF[:, k % 2, :], U[:, k, :]
                dve.wait_ge(self.freed_act.handle, st.free0 + k + 1)
                if k >= 2:
                    dve.wait_ge(A, pooled(k)[0] - 1)
                    dve.drain()
                dve.tensor_tensor_scan(cs, ON[:, :], u, 0.0, ALU.mult, ALU.add)
                dve.drain()
                dve.tensor_tensor(df[:, w:], cs[:, w:], cs[:, :-w], ALU.subtract)
                dve.tensor_tensor(df[:, 0:w], cs[:, 0:w], RC[:, k // 2, 0:w], ALU.mult)
                dve.drain()
                dve.scalar_tensor_tensor(df[:, w:], df[:, w:], 1.0 / w, u[:, w:], ALU.mult, ALU.subtract)
                dve.tensor_tensor(df[:, 0:w], df[:, 0:w], u[:, 0:w], ALU.subtract).then_inc(V, 1)
                if t == 0:
                    split()
                dve.wait_ge(A, pooled(k)[0] + 1)
                dve.tensor_tensor(PL[:, k, :], df, PH[:, k, :].bitcast(F32), ALU.subtract).then_inc(V, 1)

        with self.nc.Block() as block:
            @block.scalar
            def _(act):
                act.dma_start(RC[:, :, :], self.aps["pool_edge"]).then_inc(self.loaded.handle, 16)

            ready = self.norm(block, ("norm1_g", 0), [(mod, mod + 8, 1)], start=self.pooled_at)
            self.pool_a0, self.pool_v0 = self.act_step.after(KT), self.dve_step.after(2 * KT)

            @block.vector
            def _(dve):
                dve.memset(ON[:, :], 1.0)

            self.product(st, block, self.feature_tile(st.kt, self.HH, self.HL, False), 2, act_epi=act_in, dve_epi=dve_in,
                         freed=self.freed_act, ready=ready, inside=True,
                         rider=Rider("shift", "cond", 1, [(0, 4, mod + 24, ada + 24)]))
            self.end_rides(block)

        st = Stage(*self.take("grp"))
        TMP = CS

        def tile(pe, slot, s, t):
            T = 4 * s.u + t
            for k in range(2):
                c = (2 * t + k) * P
                mm = self.three(pe, self.B[t][:, :], (self.WH[:, slot, c:c + P], self.WL[:, slot, c:c + P]),
                                (PH[:, 2 * (T // 2) + k, :], PL[:, 2 * (T // 2) + k, :]), k == 0, k == 1)
            return mm

        a1, v1 = self.act_step.after(8), self.dve_step.after(8)

        def act_epi(act, s):
            for t in range(4):
                T = 4 * s.u + t
                act.wait_ge(self.tiles_done.handle, st.done0 + T + 1)
                if T >= 2:
                    act.wait_ge(V, v1 + T - 1)
                scale = self.vec("pool_scale", T)
                act.activation(self.HH[:, T, 0:TX], self.B[t][:, :], ACT.Copy, scale=scale).then_inc(A, 1)
                act.activation(TMP[:, T % 2, :], self.B[t][:, :], ACT.Copy, scale=scale).then_inc(self.freed_act.handle, 1)

        def dve_epi(dve, s):
            for t in range(4):
                T = 4 * s.u + t
                dve.wait_ge(A, a1 + T + 1)
                dve.wait_ge(self.freed_act.handle, st.free0 + T + 1)
                dve.tensor_tensor(self.HL[:, T, 0:TX], TMP[:, T % 2, :], self.HH[:, T, 0:TX].bitcast(F32),
                                  ALU.subtract).then_inc(V, 1)
        with self.nc.Block() as block:
            self.product(st, block, tile, 4, act_epi=act_epi, dve_epi=dve_epi, freed=self.freed_act)
        self.add_product("pool_out", [(mod + 16, 1)], rider=Rider("scale", "cond", 1, [(0, 4, mod + 32, ada + 32)]))

    def spill_product(self, name, dram, tokens=None, rider=None, norm=None):
        st = Stage(*self.take(name))
        tpi = 2 if tokens is None else 4
        shape = [P, 2, 2, TX] if tokens is None else [P, 2, 4, 256]
        ST, = self.region(f"{name}_stage", [("out", shape, F32)], start=self.arena + 40960)
        s0 = [x.after(16 * ((st.n + 1 - k) // 2)) for k, x in enumerate(self.stored)]

        def epi(act, s):
            act.wait_ge(self.stored[s.u].handle, s.i * 16 + s0[s.u])
            for t in range(tpi):
                act.wait_ge(self.tiles_done.handle, s.l * tpi + (st.done0 + t + 1))
                src = self.B[2 * s.u + t][:, :] if tokens is None else self.B[t][:, 0:256]
                act.activation(ST[:, s.u, t, :], src, ACT.Copy).then_inc(self.freed_act.handle, 1)
            act.wait_ge(self.freed_act.handle, s.l * tpi + (st.free0 + tpi))
            if tokens is None:
                dst = dram[bass.ds(s.l * 2, 2), :, :].rearrange("t p n -> p t n")
            else:
                dst = dram[:, :, bass.ds(s.l * 256, 256)].rearrange("b p n -> p b n")
            act.dma_start(dst, ST[:, s.u, :, :]).then_inc(self.stored[s.u].handle, 16)

        with self.nc.Block() as block:
            ready = None if norm is None else norm(block)
            tile = self.feature_tile(KT, self.HH, self.HL, False) if tokens is None else self.token_tile(tokens)
            self.product(st, block, tile, tpi, act_epi=epi, freed=self.freed_act, rider=rider,
                         ready=ready, post=1 if name == "wq" else 2)
            self.end_rides(block)

    def dilated_attention(self, shift1, kvshift):
        nc = self.nc
        dram = lambda n, shape: nc.dram_tensor(n, shape, F32, kind="Internal").ap()
        q_d, k_d = dram("q_scratch", (24, P, TX)), dram("k_scratch", (24, P, TX))
        v0_d, v1_d = dram("v0_scratch", (4, P, D)), dram("v1_scratch", (4, P, 2 * D))
        self.spill_product("wq", q_d, norm=lambda block: self.norm(block, ("norm1_g", 8), [(shift1, shift1 + 8, 1)]),
                           rider=Rider("kvada", "cond", 1, [(0, 8, kvshift, VC["kv_ada_b"])]))
        self.spill_product("wk", k_d, norm=lambda block: self.norm(block, ("kv_norm_g", 0), [(kvshift, kvshift + 8, 1)]))
        self.spill_product("wv0", v0_d, [slice(P * b, P * b + P) for b in range(4)])
        self.spill_product("wv1", v1_d, [slice(b, TX, 4) for b in range(4)])

        D0, D12, SL, Q, K, V, SC, E, PT = self.region("att1", [
            ("dist0", [P, 4, TX], F32), ("dist12", [P, 2, P], F32), ("slopes", [P, NBR * NH1], F32),
            ("q", [P, 2, NBR, TX], F32), ("k", [P, 2, NBR, TX], F32), ("v", [P, 2, NBR, 4, P], F32),
            ("scores", [P, 2, TA], F32), ("exps", [P, 4, TA], F32), ("turned", [P, 2, TA], F32)])
        sem = lambda name: self.ctx.enter_context(nc.semaphore(name))
        qkv = [sem(f"qkv_loaded{k}") for k in range(2)]
        scored, turned, summed = sem("scored"), sem("turned"), sem("values_summed")
        biased, maxed, normed = sem("biased"), sem("maxed"), sem("normed")
        exped, copied = sem("exped"), sem("copied")
        o_hi, o_lo = sem("o_hi"), sem("o_lo")
        scale = HD ** -0.5
        UNITS = 8
        l0 = self.loaded.after(48)
        stored = [x.n for x in self.stored]
        q_v, k_v = (d.rearrange("(g t) p n -> t p g n", g=NBR) for d in (q_d, k_d))

        with nc.Block() as block:
            @block.sync
            def _(sync):
                for t, name in ((D0[:, :, :], "dist0"), (D12[:, :, :], "dist12"), (SL[:, :], "slopes")):
                    sync.dma_start(t, self.aps[name]).then_inc(self.loaded.handle, 16)
                for k in range(2):
                    sync.wait_ge(self.stored[k].handle, stored[k])

                def load(hp, u):
                    one = lambda a: a[bass.ds(hp, 1)].rearrange("a p g n -> p (a g) n")
                    sync.dma_start(Q[:, u, :, :], one(q_v)).then_inc(qkv[u], 16)
                    sync.dma_start(K[:, u, :, :], one(k_v)).then_inc(qkv[u], 16)
                    for g in range(NBR):
                        src = v0_d if g == 0 else v1_d
                        col = hp * P + (D if g == 2 else 0)
                        sync.dma_start(V[:, u, g, :, :],
                                       src[:, :, bass.ds(col, P)].rearrange("b p n -> p b n")).then_inc(qkv[u], 16)
                for u in range(2):
                    load(u, u)
                with sync.Fori(0, 3) as i:
                    for u in range(2):
                        sync.wait_ge(summed, i * (2 * UNITS) + UNITS * (u + 1))
                        load(i * 2 + (2 + u), u)

            def unit(x):
                return x // UNITS % 2, x % UNITS // 4, x % 4

            def drive(eng, stages, pair_done=None):
                turns, skew = 4, 5

                def step(i, x, last):
                    for lag, f in stages:
                        if x >= lag and not (last and x - lag >= 2 * UNITS):
                            f(i, x - lag)
                    if pair_done is not None and x in (12, 20):
                        pair_done(i, x // 16)
                for x in range(skew):
                    step(0, x, False)
                with eng.Fori(0, turns - 1) as i:
                    for x in range(skew, skew + 2 * UNITS):
                        step(i, x, False)
                for x in range(skew, skew + 2 * UNITS):
                    step(turns - 1, x, True)

            @block.tensor
            def _(pe):
                def scores(i, x):
                    u, h, c = unit(x)
                    a, b = HD * h, HD * h + HD
                    if x % UNITS == 0:
                        pe.wait_ge(qkv[u], i * 80 + 80 * (1 + x // (2 * UNITS)))
                    pe.wait_ge(biased, i * 16 + (x + 1))
                    own = slice(c, TX, 4)
                    pe.matmul(self.B[x % 2][:, :], Q[a:b, u, 0, own], K[a:b, u, 0, :], start=True, stop=True)
                    for g in (1, 2):
                        lo = (g - 1) * P
                        mm = pe.matmul(self.B[2 + x % 2][:, lo:lo + P], Q[a:b, u, g, own], K[a:b, u, g, own],
                                       start=True, stop=True)
                    mm.then_inc(scored, 1)

                def turn(i, x):
                    pe.wait_ge(normed, i * 16 + (x + 1))
                    pe.wait_ge(copied, i * 16 + (x + 2))
                    for j in range(6):
                        bank, lo = (self.B[4], j * P) if j < 4 else (self.B[5], (j - 4) * P)
                        mm = pe.transpose(bank[:, lo:lo + P], E[:, x % 4, j * P:j * P + P], self.IDENT[:, :])
                    mm.then_inc(turned, 1)

                def values(i, x):
                    u, h, c = unit(x)
                    pe.wait_ge(copied, i * 16 + (x + 3))
                    if x % UNITS == 0:
                        pe.wait_ge(o_lo, i * 2 + (x // UNITS + 1))
                    out = self.B[6 + u][HD * h:HD * h + HD, c * P:c * P + P]
                    for j in range(6):
                        g, b = (0, j) if j < 4 else (j - 3, c)
                        mm = pe.matmul(out, V[:, u, g, b, HD * h:HD * h + HD], PT[:, x % 2, j * P:j * P + P],
                                       start=j == 0, stop=j == 5)
                    mm.then_inc(summed, 1)

                drive(pe, [(0, scores), (3, turn), (4, values)])

            @block.vector
            def _(dve):
                dve.memset(self.wk("sum", 0, 1), 0.0).then_inc(biased, 2)
                dve.memset(self.wk("sum", 1, 1), 0.0).then_inc(o_lo, 2)
                dve.wait_ge(self.loaded.handle, l0 + 48)

                def bias_max(i, x):
                    u, h, c = unit(x)
                    sl = lambda g: SL[:, bass.ds(i * 4 + (2 * (x // UNITS) + h + NH1 * g), 1)]
                    p = x % 2
                    dve.wait_ge(scored, i * 16 + (x + 1))
                    dve.wait_ge(exped, i * 16 + (x + 1))
                    dve.scalar_tensor_tensor(SC[:, p, 0:TX], D0[:, c, :], sl(0), self.B[p][:, :], ALU.mult, ALU.add)
                    for g in (1, 2):
                        lo = (g - 1) * P
                        ins = dve.scalar_tensor_tensor(SC[:, p, TX + lo:TX + lo + P], D12[:, g - 1, :], sl(g),
                                                       self.B[2 + p][:, lo:lo + P], ALU.mult, ALU.add)
                    ins.then_inc(biased, 1)
                    dve.drain()
                    dve.reduce_max(self.wk("mx", p), SC[:, p, :], AX)
                    dve.drain()
                    dve.tensor_scalar(self.wk("nb", p), self.wk("mx", p), -scale, None, ALU.mult).then_inc(maxed, 1)

                def normalise(i, x):
                    p = x % 4
                    dve.wait_ge(exped, i * 16 + (x + 3))
                    dve.reciprocal(self.wk("rs", p), self.wk("sum", p))
                    dve.drain()
                    dve.tensor_scalar(E[:, p, :], E[:, p, :], self.wk("rs", p), None, ALU.mult).then_inc(normed, 1)

                def pair_done(i, u):
                    dve.wait_ge(o_hi, i * 2 + (u + 1))
                    src = self.B[6 + u][:, :].rearrange("p (c j) -> p c j", c=4)
                    one = lambda t: t[:, bass.ds(i * 2 + u, 1), 0:TX].rearrange("p a (j c) -> p c (a j)", c=4)
                    dve.tensor_tensor(one(self.HL), src, one(self.HH).bitcast(F32), ALU.subtract).then_inc(o_lo, 1)
                drive(dve, [(0, bias_max), (2, normalise)], pair_done)

            @block.scalar
            def _(act):
                act.activation(self.wk("rs", 8, 1), self.ONES[:, 0:1], ACT.Copy).then_inc(exped, 2)
                act.activation(self.wk("rs", 9, 1), self.ONES[:, 0:1], ACT.Copy).then_inc(copied, 2)

                def exp(i, x):
                    act.wait_ge(maxed, i * 16 + (x + 1))
                    if x >= 4:
                        act.wait_ge(turned, i * 16 + (x - 3))
                    act.activation(E[:, x % 4, :], SC[:, x % 2, :], ACT.Exp, scale=scale, bias=self.wk("nb", x % 2),
                                   accum_out=self.wk("sum", x % 4)).then_inc(exped, 1)

                def copy(i, x):
                    p = x % 2
                    act.wait_ge(turned, i * 16 + (x + 1))
                    if x >= 2:
                        act.wait_ge(summed, i * 16 + (x - 1))
                    act.activation(PT[:, p, 0:TX], self.B[4][:, :], ACT.Copy)
                    act.activation(PT[:, p, TX:TA], self.B[5][:, 0:256], ACT.Copy).then_inc(copied, 1)

                def pair_done(i, u):
                    act.wait_ge(summed, i * 16 + UNITS * (u + 1))
                    self.act_ready(act)
                    src = self.B[6 + u][:, :].rearrange("p (c j) -> p c j", c=4)
                    dst = self.HH[:, bass.ds(i * 2 + u, 1), 0:TX].rearrange("p a (j c) -> p c (a j)", c=4)
                    act.activation(dst, src, ACT.Copy).then_inc(o_hi, 1)
                drive(act, [(0, exp), (3, copy)], pair_done)

    def token_product(self, name, dest, load):
        st = Stage(*self.take(name))
        nb = TA // P

        def epi(act, s):
            for t in range(nb):
                act.wait_ge(self.tiles_done.handle, s.l * nb + (st.done0 + t + 1))
                self.act_ready(act)
                act.activation(dest[:, t, bass.ds(s.l * 256, 256)], self.B[t][:, 0:256],
                               ACT.Copy).then_inc(self.freed_act.handle, 1)
        with self.nc.Block() as block:
            load(block)
            self.product(st, block, self.token_tile([slice(P * b, P * b + P) for b in range(nb)]), nb,
                         act_epi=epi, freed=self.freed_act, distance=nb, post=False)

    def rope(self, F, li, values_product):
        CS, PM, T = self.region(f"rope{li}", [("cos_sin", [P, 2, TX], F32), ("perm", [P, P], F32),
                                              ("tmp", [P, 2, TX], F32)], self.arena_tail, self.end)
        tiles = list(range(8, 12)) + list(range(4))
        p0, v0 = self.pe_step.after(8), self.dve_step.after(8)

        def load(block):
            @block.sync
            def _(sync):
                sync.dma_start(CS[:, :, :], self.aps["rope_cs"]).then_inc(self.loaded.handle, 16)
                sync.dma_start(PM[:, :], self.aps["rope_perm"]).then_inc(self.loaded.handle, 16)
        l0 = self.loaded.after(32)
        values_product(load)
        with self.nc.Block() as block:
            @block.tensor
            def _(pe):
                pe.wait_ge(self.loaded.handle, l0 + 32)
                for x, t in enumerate(tiles):
                    if x >= 4:
                        pe.wait_ge(self.dve_step.handle, v0 + x - 3)
                    pe.matmul(self.B[x % 4][:, :], PM[:, :], F[:, t, 0:TX], start=True,
                              stop=True).then_inc(self.pe_step.handle, 1)

            @block.vector
            def _(dve):
                dve.wait_ge(self.loaded.handle, l0 + 32)
                for x, t in enumerate(tiles):
                    dve.wait_ge(self.pe_step.handle, p0 + x + 1)
                    dve.tensor_tensor(T[:, x % 2, :], CS[:, 1, :], self.B[x % 4][:, :],
                                      ALU.mult).then_inc(self.dve_step.handle, 1)
                    dve.tensor_tensor(F[:, t, 0:TX], F[:, t, 0:TX], CS[:, 0, :], ALU.mult)
                    dve.drain()
                    dve.tensor_tensor(F[:, t, 0:TX], F[:, t, 0:TX], T[:, x % 2, :], ALU.add)

    def lambdas(self, block):
        pr, = self.region("lam", [("prod", [P, 16], F32)], self.ride_at)
        V, A, E = (x.handle for x in (self.dve_step, self.act_step, self.pe_step))
        v0, a0, p0 = self.dve_step.after(3), self.act_step.after(3), self.pe_step.after(1)
        lam, lb = self.vec("lam", 0, 8), self.vec("lb", 0, 8)
        @block.vector
        def _(dve):
            dve.tensor_tensor(pr[:, 0:4], lam[:, 0:8:2], lam[:, 1:8:2], ALU.mult).then_inc(V, 1)
            dve.tensor_tensor(pr[:, 4:8], lb[:, 4:8], lb[:, 0:4], ALU.subtract)
            dve.drain()
            dve.scalar_tensor_tensor(pr[:, 8:12], pr[:, 4:8], -1.0, pr[:, 4:8], ALU.mult, ALU.min).then_inc(V, 1)
            dve.wait_ge(A, a0 + 2)
            dve.scalar_tensor_tensor(self.wk("lb", 0, 4), pr[:, 4:8], 0.0, pr[:, 12:16], ALU.min, ALU.subtract)
            dve.tensor_scalar(pr[:, 4:8], pr[:, 4:8], -1.0, 0.0, ALU.mult, ALU.min)
            dve.drain()
            dve.tensor_tensor(self.wk("lb", 4, 4), pr[:, 4:8], pr[:, 12:16], ALU.subtract)
            dve.drain()
            dve.tensor_tensor(self.wk("lb", 8, 4), self.wk("lb", 4, 4), self.wk("lb", 0, 4), ALU.subtract).then_inc(V, 1)
            dve.wait_ge(A, a0 + 3)
            dve.tensor_tensor(self.wk("lam", 2, 2), self.wk("lam", 4, 4)[:, 0:4:2], self.wk("lam", 4, 4)[:, 1:4:2],
                              ALU.subtract)
            dve.drain()
            for li in range(2):
                dve.tensor_scalar(self.wk("lam", li), self.wk("lam", 2 + li), LAM0[li], None, ALU.add)
            for li in range(2):
                dve.tensor_scalar(self.vec("subln", li), self.vec("subln", li), 1.0 - LAM0[li], None, ALU.mult)

        @block.tensor
        def _(pe):
            pe.wait_ge(V, v0 + 1)
            pe.matmul(self.B[7][:, 0:4], self.ONES[:, :], pr[:, 0:4], start=True, stop=True).then_inc(E, 1)

        @block.scalar
        def _(act):
            act.wait_ge(V, v0 + 2)
            act.activation(pr[:, 12:16], pr[:, 8:12], ACT.Exp).then_inc(A, 1)
            act.wait_ge(A, a0 + 1)
            act.activation(pr[:, 12:16], pr[:, 12:16], ACT.Ln, bias=1.0).then_inc(A, 1)
            act.wait_ge(E, p0 + 1)
            act.activation(self.wk("lam", 4, 4), self.B[7][:, 0:4], ACT.Exp).then_inc(A, 1)

    def diff_attention(self, F, VT, li):
        nc = self.nc
        E, PT = self.region(f"att2_{li}", [("exps", [P, 3, 2, TA], F32), ("turned", [P, 2, TA], F32)],
                            self.split_at, self.split_end)
        units = [(h, b) for h in range(4) for b in range(4 if li else 6)]
        N = len(units)
        per = N // 4
        if li == 0:
            self.att2 = {n: Signal(self.ctx.enter_context(nc.semaphore(n))) for n in
                         ("d_scored", "d_turned", "d_summed", "d_maxed", "d_combined", "d_exped", "d_copied", "d_out")}
        q = self.att2
        S = {n: (x.handle, x.after({"d_scored": 2, "d_maxed": 2, "d_exped": 2}.get(n, 1) * (4 if n == "d_out" else N)))
             for n, x in q.items()}
        scale = HD ** -0.5

        def wait(eng, name, count):
            if count > 0:
                eng.wait_ge(S[name][0], S[name][1] + count)

        def parts(x):
            return ([(0, TX)] if units[x][1] < 4 else []) + [(TX, TA)]

        def blocks(x):
            return range(6) if units[x][1] < 4 else range(4, 6)

        with nc.Block() as block:
            @block.tensor
            def _(pe):
                def scores(x, c):
                    h, b = units[x]
                    wait(pe, "d_exped", 2 * (x - 1) + c + 1)
                    rows = slice(HD * c, HD * c + HD)
                    for lo, hi in parts(x):
                        bank = self.B[c] if lo == 0 else self.B[2 + c]
                        mm = pe.matmul(bank[:, 0:hi - lo], F[rows, 8 + h, b * P:b * P + P], F[rows, h, lo:hi],
                                       start=True, stop=True)
                    mm.then_inc(S["d_scored"][0], 1)

                def turn(x):
                    wait(pe, "d_combined", x + 1)
                    wait(pe, "d_copied", x)
                    for j in blocks(x):
                        bank, lo = (self.B[4], j * P) if j < 4 else (self.B[5], (j - 4) * P)
                        mm = pe.transpose(bank[:, lo:lo + P], E[:, x % 3, 0, j * P:j * P + P], self.IDENT[:, :])
                    mm.then_inc(S["d_turned"][0], 1)

                def values(x):
                    h, b = units[x]
                    wait(pe, "d_copied", x + 1)
                    if b == 0:
                        wait(pe, "d_out", h)
                    out = self.B[6][:, b * P:b * P + P] if b < 4 else self.B[7][:, (b - 4) * P:(b - 4) * P + P]
                    js = list(blocks(x))
                    for j in js:
                        mm = pe.matmul(out, VT[:, j, h * P:h * P + P], PT[:, x % 2, j * P:j * P + P],
                                       start=j == js[0], stop=j == js[-1])
                    mm.then_inc(S["d_summed"][0], 1)

                for x in range(N + 3):
                    if x < N:
                        scores(x, 0)
                        scores(x, 1)
                    if 2 <= x < N + 2:
                        turn(x - 2)
                    if x >= 3:
                        values(x - 3)

            @block.vector
            def _(dve):
                def maxima(x, c):
                    wait(dve, "d_scored", 2 * x + c + 1)
                    m = self.wk("mx", 2 * c, 2)
                    if len(parts(x)) == 2:
                        dve.reduce_max(m[:, 0:1], self.B[c][:, :], AX)
                        dve.reduce_max(m[:, 1:2], self.B[2 + c][:, 0:TC], AX)
                        dve.drain()
                        dve.tensor_tensor(m[:, 0:1], m[:, 0:1], m[:, 1:2], ALU.max)
                    else:
                        dve.reduce_max(m[:, 0:1], self.B[2 + c][:, 0:TC], AX)
                    dve.drain()
                    dve.tensor_scalar(self.wk("nb", 2 * (x % 3) + c), m[:, 0:1], -scale, None,
                                      ALU.mult).then_inc(S["d_maxed"][0], 1)

                def combine(x):
                    p = x % 3
                    wait(dve, "d_exped", 2 * x + 2)
                    sums = self.wk("sum", 4 * p, 4)
                    rs = self.wk("rs", 2 * p, 2)
                    if len(parts(x)) == 2:
                        dve.tensor_tensor(sums[:, 0:4:2], sums[:, 0:4:2], sums[:, 1:4:2], ALU.add)
                        dve.drain()
                        dve.reciprocal(rs, sums[:, 0:4:2])
                    else:
                        dve.reciprocal(rs, sums[:, 1:4:2])
                    dve.drain()
                    a, b = parts(x)[0][0], TA
                    dve.tensor_scalar(E[:, p, 1, a:b], E[:, p, 1, a:b], rs[:, 1:2], self.wk("lam", li),
                                      ALU.mult, ALU.mult)
                    dve.drain()
                    dve.scalar_tensor_tensor(E[:, p, 0, a:b], E[:, p, 0, a:b], rs[:, 0:1], E[:, p, 1, a:b],
                                             ALU.mult, ALU.subtract).then_inc(S["d_combined"][0], 1)
                for x in range(N + 1):
                    if x < N:
                        maxima(x, 0)
                        maxima(x, 1)
                    if x >= 1:
                        combine(x - 1)

            @block.scalar
            def _(act):
                def exps(x, c):
                    p = x % 3
                    wait(act, "d_maxed", 2 * x + c + 1)
                    wait(act, "d_turned", x - 2)
                    for lo, hi in parts(x):
                        bank = self.B[c] if lo == 0 else self.B[2 + c]
                        ins = act.activation(E[:, p, c, lo:hi], bank[:, 0:hi - lo], ACT.Exp, scale=scale,
                                             bias=self.wk("nb", 2 * p + c),
                                             accum_out=self.wk("sum", 4 * p + 2 * c + (lo > 0)))
                    ins.then_inc(S["d_exped"][0], 1)

                def copy(x):
                    wait(act, "d_turned", x + 1)
                    wait(act, "d_summed", x - 1)
                    for lo, hi in parts(x):
                        ins = act.activation(PT[:, x % 2, lo:hi], self.B[4 if lo == 0 else 5][:, 0:hi - lo], ACT.Copy)
                    ins.then_inc(S["d_copied"][0], 1)

                def head(h):
                    wait(act, "d_summed", per * (h + 1))
                    ins = act.activation(F[:, 8 + h, 0:TX], self.B[6][:, :], ACT.Copy)
                    if li == 0:
                        ins = act.activation(F[:, 8 + h, TX:TA], self.B[7][:, 0:TC], ACT.Copy)
                    ins.then_inc(S["d_out"][0], 1)

                for x in range(N + 3):
                    if x < N:
                        exps(x, 0)
                        exps(x, 1)
                    if 2 <= x < N + 2:
                        copy(x - 2)
                    if x >= 3 and (x - 3) % per == per - 1:
                        head((x - 3) // per)

    def head_norms(self, name, src, tiles, ones, inverse, weight, dest, W, gates=None, loads=None):
        T1, RS = self.region(f"{name}_hn", [("a", [P, 2, TA], F32), ("r", [P, 2, TA], F32)],
                             self.split_at, self.split_end)
        G = None if gates is None else self.region(f"{name}_g", [("g", [P, 2, TA], F32)],
                                                   self.split_at + 16 * TA, self.split_end)[0]
        V, A, E = (x.handle for x in (self.dve_step, self.act_step, self.pe_step))
        n = len(tiles)
        spans = [(0, TX)] + ([(TX, TA)] if W == TA else [])
        act_order = [("gate", x) for x in range(n if gates is not None else 0)] + [("square", 0), ("square", 1)]
        dve_order = [("inverse", 0)]
        for x in range(n):
            act_order += [("root", x), ("high", x)] + ([("square", x + 2)] if x + 2 < n else [])
            dve_order += [("normed", x)] + ([("inverse", x + 1)] if x + 1 < n else []) + [("low", x)]
        v0, a0, p0 = self.dve_step.after(len(dve_order)), self.act_step.after(len(act_order)), self.pe_step.after(n)
        at_act = {step: a0 + k + 1 for k, step in enumerate(act_order)}
        at_dve = {step: v0 + k + 1 for k, step in enumerate(dve_order)}
        with self.nc.Block() as block:
            if loads is not None:
                loads(block)

            @block.scalar
            def _(act):
                for step, x in act_order:
                    p = x % 2
                    if step == "gate":
                        ins = act.activation(G[:, p, 0:W], gates[:, x, 0:W], ACT.Silu)
                    elif step == "square":
                        if x >= 2:
                            act.wait_ge(V, at_dve["normed", x - 2])
                        ins = act.activation(RS[:, p, 0:W], src[:, tiles[x], 0:W], ACT.Square)
                    elif step == "root":
                        act.wait_ge(V, at_dve["inverse", x])
                        ins = act.activation(RS[:, p, 0:W], RS[:, p, 0:W], ACT.Sqrt)
                    else:
                        act.wait_ge(V, at_dve["normed", x])
                        ins = act.activation(self.HH[:, dest + x, 0:W], T1[:, p, 0:W], ACT.Copy)
                    ins.then_inc(A, 1)

            @block.tensor
            def _(pe):
                for x in range(n):
                    pe.wait_ge(A, at_act["square", x])
                    if x >= 2:
                        pe.wait_ge(V, at_dve["inverse", x - 2])
                    for b, (s, e) in enumerate(spans):
                        mm = pe.matmul(self.B[2 * (x % 2) + b][:, 0:e - s], ones, RS[:, x % 2, s:e],
                                       start=True, stop=True)
                    mm.then_inc(E, 1)

            @block.vector
            def _(dve):
                for step, x in dve_order:
                    p = x % 2
                    if step == "inverse":
                        dve.wait_ge(E, p0 + x + 1)
                        for b, (s, e) in enumerate(spans):
                            dve.tensor_scalar(RS[:, p, s:e], self.B[2 * p + b][:, 0:e - s], inverse, EPS,
                                              ALU.mult, ALU.add)
                        dve.drain()
                        ins = dve.reciprocal(RS[:, p, 0:W], RS[:, p, 0:W])
                    elif step == "normed":
                        dve.wait_ge(A, at_act["root", x])
                        ins = dve.scalar_tensor_tensor(T1[:, p, 0:W], src[:, tiles[x], 0:W], weight, RS[:, p, 0:W],
                                                       ALU.mult, ALU.mult)
                        if gates is not None:
                            dve.drain()
                            ins = dve.tensor_tensor(T1[:, p, 0:W], T1[:, p, 0:W], G[:, p, 0:W], ALU.mult)
                    else:
                        dve.wait_ge(A, at_act["high", x])
                        ins = dve.tensor_tensor(self.HL[:, dest + x, 0:W], T1[:, p, 0:W],
                                                self.HH[:, dest + x, 0:W].bitcast(F32), ALU.subtract)
                    ins.then_inc(V, 1)

    def fourier_loads(self, block, li):
        self.four_at = self.split_at + 16 * TA
        self.four = self.region(f"four{li}c", [
            ("dft", [P, 2, 4, TX], F32), ("dft64", [P, 2 * P], F32), ("w", [P, 2, 256], F32)], self.four_at, self.split_end)
        self.four_l0 = self.loaded.after(48)

        @block.sync
        def _(sync):
            CL, F64, WF = self.four
            sync.dma_start(CL[:, :, :, :], self.aps["dft"]).then_inc(self.loaded.handle, 16)
            sync.dma_start(F64[:, :], self.aps["dft64"]).then_inc(self.loaded.handle, 16)
            sync.dma_start(WF[:, :, :], self.aps["w_fnet"][li]).then_inc(self.loaded.handle, 16)

    def fourier(self, F, li):
        nb = 4 if li else 6
        AB, = self.region(f"four{li}", [("ab", [P, nb, 2, 256], F32)], self.split_at, self.four_at)
        CL, F64, WF = self.four
        V, A, E = (x.handle for x in (self.dve_step, self.act_step, self.pe_step))
        segs = [(0, TX, [0, 1, 2, 3], 1)] + ([(TX, TA, [4, 5], 2)] if li == 0 else [])
        ns = len(segs)
        n_act = nb + 2 * ns + 2
        l0, p0, a0, v0 = self.four_l0, self.pe_step.after(nb + 2 * ns + 2), self.act_step.after(n_act), self.dve_step.after(2)
        W = segs[-1][1]
        TMP, = self.region(f"four{li}t", [("t", [P, 1, TA], F32)], self.arena_tail, self.end)
        with self.nc.Block() as block:
            @block.tensor
            def _(pe):
                pe.wait_ge(self.loaded.handle, l0 + 48)
                for b in range(nb):
                    if b >= 4:
                        pe.wait_ge(A, a0 + b - 3)
                    for j in range(2):
                        mm = pe.matmul(self.B[b % 4][:, 256 * j:256 * j + 256], F[:, 16 + j, b * P:b * P + P],
                                       F64[:, :], start=True, stop=True)
                    mm.then_inc(E, 1)
                for x, (s, e, bl, step) in enumerate(segs):
                    pe.wait_ge(A, a0 + nb)
                    for j in range(2):
                        for y, b in enumerate(bl):
                            for z in range(2):
                                mm = pe.matmul(self.B[4 + 2 * x + j][:, 0:e - s], AB[:, b, j, z * P:z * P + P],
                                               CL[:, z, y, 0:TX:step], start=(y, z) == (0, 0),
                                               stop=(y, z) == (len(bl) - 1, 1))
                        mm.then_inc(E, 1)
                pe.wait_ge(A, a0 + nb + 2 * ns)
                for m in range(2):
                    for x, (s, e, _, _) in enumerate(segs):
                        for j in range(2):
                            mm = pe.matmul(self.B[2 * m + x][:, 0:e - s], WF[:, j, m * P:m * P + P], F[:, 16 + j, s:e],
                                           start=j == 0, stop=j == 1)
                    mm.then_inc(E, 1)

            @block.scalar
            def _(act):
                for b in range(nb):
                    act.wait_ge(E, p0 + b + 1)
                    act.activation(AB[:, b, :, :].rearrange("p a n -> p (a n)"), self.B[b % 4][:, :], ACT.Copy).then_inc(A, 1)
                for x, (s, e, _, _) in enumerate(segs):
                    for j in range(2):
                        act.wait_ge(E, p0 + nb + 2 * x + j + 1)
                        act.activation(F[:, 16 + j, s:e], self.B[4 + 2 * x + j][:, 0:e - s], ACT.Copy,
                                       scale=((e - s) * 64.0) ** -0.5).then_inc(A, 1)
                for m in range(2):
                    act.wait_ge(E, p0 + nb + 2 * ns + m + 1)
                    if m == 1:
                        act.wait_ge(V, v0 + 1)
                    for x, (s, e, _, _) in enumerate(segs):
                        act.activation(self.HH[:, 6 + m, s:e], self.B[2 * m + x][:, 0:e - s], ACT.Copy)
                    for x, (s, e, _, _) in enumerate(segs):
                        ins = act.activation(TMP[:, 0, s:e], self.B[2 * m + x][:, 0:e - s], ACT.Copy)
                    ins.then_inc(A, 1)

            @block.vector
            def _(dve):
                for m in range(2):
                    dve.wait_ge(A, a0 + nb + 2 * ns + m + 1)
                    dve.tensor_tensor(self.HL[:, 6 + m, 0:W], TMP[:, 0, 0:W], self.HH[:, 6 + m, 0:W].bitcast(F32),
                                      ALU.subtract).then_inc(V, 1)

    def recurrence(self, F, VT, li):
        lat = li == 1
        nb = 4 if lat else 6
        W = nb * P
        NB = TA // P
        KS, T2, ST, TOT, ET = self.region(f"rec{li}", [
            ("ks", [P, 4, TA], F32), ("t2", [P, 4, TA], F32), ("states", [P, 2 * NB, 2, HD], F32),
            ("total", [P, 4, NB], F32), ("exptotal", [P, 4, NB], F32)], self.split_at, self.split_end)
        KTT, ACC = self.region(f"rec{li}k", [("kt", [P, NB, 2, 256], F32)], self.split_at + 16 * TA, self.split_end) + \
            self.region(f"rec{li}a", [("acc", [P, 2, nb // 2, 4, P], F32)], self.split_at + 16 * TA, self.split_end)
        DB, = self.region(f"rec{li}d", [("d", [P, 2, 2, TA], F32)], self.split_at, self.split_end)
        MK, = self.region(f"rec{li}m", [("masks", [P, 2 * LEVELS, P], mybir.dt.int32)], self.arena_tail, self.end)
        RM = KS[:, 0, :]
        Z, K, T1, Q = F[:, 4:8, :], F[:, 0:4, :], F[:, 8:12, :], F[:, 12:14, :]
        l0 = self.loaded.after(32)
        V, A, E, G = (x.handle for x in (self.dve_step, self.act_step, self.pe_step, self.pool_step))
        v0, a0, p0 = self.dve_step.n, self.act_step.n, self.pe_step.n
        second = 1 if li else 0
        a, c, ca = self.wk("lb", 0, 4), self.wk("lb", 4, 4), self.wk("lb", 8, 4)
        with self.nc.Block() as block:
            @block.sync
            def _(sync):
                sync.dma_start(MK[:, :, :], self.aps["level_masks"]).then_inc(self.loaded.handle, 16)
                sync.dma_start(RM, self.aps["block_reset"]).then_inc(self.loaded.handle, 16)

            @block.vector
            def _(dve):
                for t in range(4):
                    dve.scalar_tensor_tensor(T1[:, t, :], Z[:, t, :], -1.0, Z[:, t, :], ALU.mult, ALU.min).then_inc(V, 1)
                for t in range(4):
                    dve.wait_ge(A, a0 + 4 + t + 1)
                    dve.scalar_tensor_tensor(T1[:, t, :], Z[:, t, :], 0.0, T1[:, t, :], ALU.min, ALU.subtract)
                    dve.drain()
                    dve.tensor_tensor(K[:, t, :], T1[:, t, :], Z[:, t, :], ALU.subtract).then_inc(V, 1)
                if second:
                    for t in range(4):
                        dve.drain()
                        dve.tensor_scalar(Z[:, t, :], T1[:, t, :], ca[:, t:t + 1], None, ALU.add)
                        dve.drain()
                        dve.scalar_tensor_tensor(Z[:, t, :], Z[:, t, :], -1.0, Z[:, t, :], ALU.mult, ALU.min).then_inc(V, 1)
                        dve.tensor_scalar(T1[:, t, :], T1[:, t, :], c[:, t:t + 1], a[:, t:t + 1], ALU.add, ALU.max)
                dve.wait_ge(self.loaded.handle, l0 + 32)
                for t in range(4):
                    if second:
                        dve.wait_ge(A, a0 + 12 + 4 + t + 1)
                        dve.tensor_tensor(T1[:, t, :], T1[:, t, :], Z[:, t, :], ALU.add)
                    dve.drain()
                    dve.tensor_tensor_scan(Z[:, t, :], RM, T1[:, t, :], 0.0, ALU.mult, ALU.add)
                dve.drain()
                last = Z.rearrange("p t (b n) -> p t b n", n=P)[:, :, :, P - 1:P]
                dve.tensor_copy(TOT[:, :, :], last.rearrange("p t b n -> p t (b n)"))
                dve.drain()
                dve.tensor_tensor(Z[:, 2:4, :], Z[:, 2:4, :], T1[:, 2:4, :], ALU.subtract)
                dve.drain()
                for t in range(4):
                    view = lambda x: x[:, t, :].rearrange("p (b n) -> p b n", n=P)
                    dve.tensor_tensor(view(T2), TOT[:, t, :].rearrange("p (b n) -> p b n", n=1).to_broadcast([P, NB, P]),
                                      view(Z), ALU.subtract).then_inc(V, 1)
                n = v0 + 12 + 4 * second
                done = a0 + 12 + 8 * second
                dve.wait_ge(A, done + 9)
                dve.tensor_tensor(KS[:, 0:2, :], K[:, 0:2, :], T2[:, 0:2, :], ALU.mult).then_inc(V, 1)
                dve.tensor_tensor(KS[:, 2:4, :], K[:, 2:4, :], T1[:, 2:4, :], ALU.mult).then_inc(V, 1)
                dve.drain()
                dve.tensor_tensor(T1[:, 0:2, 0:W], Q[:, :, 0:W], T1[:, 0:2, 0:W], ALU.mult)
                dve.tensor_tensor(T1[:, 2:4, 0:W], Q[:, :, 0:W], T2[:, 2:4, 0:W], ALU.mult).then_inc(V, 1)
                for d in range(2):
                    dve.memset(ST[:, d * NB, :, :], 0.0)
                dve.wait_ge(E, p0 + 2 * NB)
                order = [[4, 5, 0, 1, 2, 3], [5, 4, 3, 2, 1, 0]]
                for pos in range(NB - 1):
                    dve.drain()
                    for d in range(2):
                        b = order[d][pos]
                        x = d * NB + b
                        for j in range(2):
                            u = self.B[x // 4][:, (x % 4) * P + j * HD:(x % 4) * P + j * HD + HD]
                            dve.scalar_tensor_tensor(ST[:, d * NB + pos + 1, j, :], ST[:, d * NB + pos, j, :],
                                                     ET[:, 2 * d + j, b:b + 1], u, ALU.mult, ALU.add)

            @block.scalar
            def _(act):
                for t in range(4):
                    act.wait_ge(V, v0 + t + 1)
                    act.activation(T1[:, t, :], T1[:, t, :], ACT.Exp).then_inc(A, 1)
                for t in range(4):
                    act.wait_ge(A, a0 + t + 1)
                    act.activation(T1[:, t, :], T1[:, t, :], ACT.Ln, bias=1.0).then_inc(A, 1)
                for t in range(4):
                    act.wait_ge(V, v0 + 4 + t + 1)
                    act.activation(K[:, t, :], K[:, t, :], ACT.Exp, bias=c[:, t:t + 1] if second else 0.0).then_inc(A, 1)
                if second:
                    for t in range(4):
                        act.wait_ge(V, v0 + 8 + t + 1)
                        act.activation(Z[:, t, :], Z[:, t, :], ACT.Exp).then_inc(A, 1)
                    for t in range(4):
                        act.wait_ge(A, a0 + 12 + t + 1)
                        act.activation(Z[:, t, :], Z[:, t, :], ACT.Ln, bias=1.0).then_inc(A, 1)
                n = v0 + 8 + 4 * second
                for t in range(4):
                    act.wait_ge(V, n + t + 1)
                    act.activation(T2[:, t, :], T2[:, t, :], ACT.Exp).then_inc(A, 1)
                    act.activation(T1[:, t, :], Z[:, t, :], ACT.Exp).then_inc(A, 1)
                act.activation(ET[:, :, :], TOT[:, :, :], ACT.Exp).then_inc(A, 1)
                done = a0 + 12 + 8 * second + 9
                for b in range(NB):
                    act.wait_ge(E, p0 + b + 1)
                    if b == 0:
                        act.wait_ge(V, n + 4 + 3)
                    act.activation(KTT[:, b, :, :].rearrange("p a n -> p (a n)"), self.B[4 + b % 4][:, :],
                                   ACT.Copy).then_inc(A, 1)

            @block.tensor
            def _(pe):
                n = v0 + 12 + 4 * second
                done = a0 + 12 + 8 * second + 9
                pe.wait_ge(V, n + 2)
                for b in range(NB):
                    if b >= 4:
                        pe.wait_ge(A, done + b - 3)
                    for t in range(4):
                        mm = pe.transpose(self.B[4 + b % 4][:, t * P:t * P + P], KS[:, t, b * P:b * P + P], self.IDENT[:, :])
                    mm.then_inc(E, 1)
                for b in range(NB):
                    pe.wait_ge(A, done + b + 1)
                    for d in range(2):
                        x = d * NB + b
                        for h in range(4):
                            r, j = h % 2, h // 2
                            lo = (x % 4) * P + j * HD
                            mm = pe.matmul(self.B[x // 4][HD * r:HD * r + HD, lo:lo + HD], KTT[:, b, d, h * HD:h * HD + HD],
                                           VT[:, b, 2 * 256 + h * HD:2 * 256 + h * HD + HD], start=True, stop=True)
                    mm.then_inc(E, 1)
        self.dve_step.after(12 + 4 * second + 3)
        self.act_step.after(12 + 8 * second + 9 + NB)
        self.pe_step.after(2 * NB)

        jobs = [None] + [(lv, d) for lv in range(LEVELS) for d in range(2)]
        J = len(jobs)
        v0, a0, p0, g0 = self.dve_step.n, self.act_step.n, self.pe_step.n, self.pool_step.n
        if li == 0:
            self.read_out = Signal(self.ctx.enter_context(self.nc.semaphore("pairs_read_out")))
            self.paired = Signal(self.ctx.enter_context(self.nc.semaphore("pairs_done")))
        c0, s0 = self.read_out.after(J * nb), self.paired.after(J * nb)

        def halves(x, lv, tiles=None):
            m = 1 << lv
            v = x.rearrange("p t (n m) -> p t n m", m=2 * m)
            return v[:, :, :, 0:m], v[:, :, :, m:2 * m], v

        with self.nc.Block() as block:
            @block.gpsimd
            def _(pool):
                for n, job in enumerate(jobs):
                    if n >= 2:
                        pool.wait_ge(self.paired.handle, s0 + (n - 1) * nb)
                    if job is None:
                        pool.tensor_tensor(DB[:, 0, :, 0:W], K[:, 0:2, 0:W], K[:, 2:4, 0:W], ALU.add).then_inc(G, 1)
                        continue
                    lv, d = job
                    m = 1 << lv
                    cl, cr, cv = halves(Z[:, 2 * d:2 * d + 2, 0:W], lv)
                    dl, dr, _ = halves(DB[:, n % 2, :, 0:W], lv)
                    at = m - 1 if d == 0 else m
                    mid = cv[:, :, :, at:at + 1].to_broadcast([P, 2, W // (2 * m), m])
                    pool.tensor_tensor(dl, mid, cl, ALU.subtract)
                    pool.tensor_tensor(dr, cr, mid, ALU.subtract).then_inc(G, 1)

            @block.scalar
            def _(act):
                for n, job in enumerate(jobs):
                    if job is None:
                        continue
                    act.wait_ge(G, g0 + n + 1)
                    act.activation(DB[:, n % 2, :, 0:W], DB[:, n % 2, :, 0:W], ACT.Exp).then_inc(A, 1)

            @block.vector
            def _(dve):
                def decay(n):
                    lv, d = jobs[n]
                    dve.wait_ge(A, a0 + n)
                    xl, xr, _ = halves(DB[:, n % 2, :, 0:W], lv)
                    ql, qr, _ = halves(Q[:, :, 0:W], lv)
                    kl, kr, _ = halves(K[:, 2 * d:2 * d + 2, 0:W], lv)
                    dve.tensor_tensor(xl, xl, kl if d == 0 else ql, ALU.mult)
                    dve.tensor_tensor(xr, xr, qr if d == 0 else kr, ALU.mult).then_inc(V, 1)

                for n, job in enumerate(jobs):
                    if n + 1 < J:
                        decay(n + 1)
                    for y in range(nb):
                        dve.wait_ge(self.paired.handle, s0 + n * nb + y + 1)
                        acc = ACC[:, y % 2, y // 2, :, :]
                        bank = self.B[(n * nb + y) % 8][:, :].rearrange("p (a n) -> p a n", a=4)
                        if job is None:
                            every = self.IDENT[:, :].rearrange("p (a n) -> p a n", a=1).to_broadcast([P, 4, P])
                            ins = dve.tensor_tensor(acc, every, bank, ALU.mult)
                        else:
                            mask = MK[:, n - 1:n, :].to_broadcast([P, 4, P])
                            ins = dve.copy_predicated(acc, mask, bank)
                        ins.then_inc(self.read_out.handle, 1)
                    dve.drain()

            @block.tensor
            def _(pe):
                for n, job in enumerate(jobs):
                    if job is None:
                        pe.wait_ge(G, g0 + 1)
                    else:
                        pe.wait_ge(V, v0 + n)
                    for y in range(nb):
                        if n * nb + y >= 8:
                            pe.wait_ge(self.read_out.handle, c0 + n * nb + y - 7)
                        r, pair = y % 2, y // 2
                        rows = slice(HD * r, HD * r + HD)
                        for q in range(4):
                            b, j = 2 * pair + q // 2, q % 2
                            x = DB[rows, n % 2, j, b * P:b * P + P]
                            other = Q[rows, j, b * P:b * P + P] if job is None else x
                            mm = pe.matmul(self.B[(n * nb + y) % 8][:, q * P:q * P + P], x, other, start=True, stop=True)
                        mm.then_inc(self.paired.handle, 1)
        self.pool_step.after(J)
        self.act_step.after(J - 1)
        self.dve_step.after(J - 1)

        p0, a0 = self.pe_step.after(nb), self.act_step.after(nb)
        order = [[4, 5, 0, 1, 2, 3], [5, 4, 3, 2, 1, 0]]
        with self.nc.Block() as block:
            @block.tensor
            def _(pe):
                for b in range(nb):
                    if b >= 4:
                        pe.wait_ge(A, a0 + b - 3)
                    for h in range(4):
                        r, j = h % 2, h // 2
                        rows = slice(HD * r, HD * r + HD)
                        out = self.B[2 * (b % 4) + r][rows, j * P:j * P + P]
                        pe.matmul(out, VT[:, b, 512 + h * HD:512 + h * HD + HD], ACC[:, r, b // 2, 2 * (b % 2) + j, :],
                                  start=True, stop=False)
                        for d in range(2):
                            mm = pe.matmul(out, ST[rows, d * NB + order[d].index(b), j, :],
                                           T1[rows, 2 * d + j, b * P:b * P + P], start=False, stop=d == 1)
                    mm.then_inc(E, 1)

            @block.scalar
            def _(act):
                for b in range(nb):
                    act.wait_ge(E, p0 + b + 1)
                    for r in range(2):
                        rows = slice(HD * r, HD * r + HD)
                        src = self.B[2 * (b % 4) + r][rows, 0:256].rearrange("p (j n) -> p j n", j=2)
                        ins = act.activation(F[rows, 4:6, b * P:b * P + P], src, ACT.Copy)
                    ins.then_inc(A, 1)

    def mod2_rider(self, li):
        return Rider(f"ada2_{li}", "condc", 2, [(0, 24, WC["mod2b" if li else "mod2"], VC["b_ada"] + 48 * li)],
                     apart=li == 0)

    def second_block(self):
        for li in range(2):
            m2 = WC["mod2b" if li else "mod2"]
            ctx = li == 0

            def segs(q, scale=True):
                return [(m2 + 16 * q + j, m2 + 16 * q + 16 + j, 2) for j in range(2)]

            def gate(q):
                return [(m2 + 16 * q + j, 2) for j in range(2)]
            F, VT = self.region(f"proj{li}", [("f", [P, 18, TA], F32), ("v", [P, TA // P, TA], F32)])
            self.arena_tail = self.arena + 18 * TA * 4 + TA // P * TA * 4
            self.plain_product(f"in_{li}a", F, 0, True,
                               norm=lambda block: self.norm(block, ("norm1_w", 8 * li), segs(0), ctx=True))
            self.plain_product(f"in_{li}b", F, 8, ctx)
            self.rope(F, li, lambda load: self.token_product(f"in_{li}v", VT, load))
            self.diff_attention(F, VT, li)
            W = TA if ctx else TX
            self.head_norms(f"a{li}", F, [8, 9, 10, 11], self.ONES[:, :], 1.0 / (2 * HD), self.vec("subln", li), 0, W,
                            loads=lambda block: self.fourier_loads(block, li))
            self.fourier(F, li)
            self.recurrence(F, VT, li)
            self.head_norms(f"r{li}", F, [4, 5], self.HALF[:, :], 1.0 / HD, self.vec("hgrn_w", li), 4, W,
                            gates=F[:, 14:16, :])
            if self.upto == f"cat{li}":
                return
            self.add_product(f"out_{li}", gate(2), ctx=ctx)
            if self.upto == f"mix{li}":
                return
            norm = lambda block: self.norm(block, ("norm2_w", 8 * li), segs(3), ctx=ctx)
            self.ffn(f"g{li}", norm, gate(5), VC["conv2_w"] + 132 * li, VC["conv2_b"] + 44 * li, True,
                     None if li else self.mod2_rider(1))
            if self.upto == f"b2_{li}":
                return
        with self.nc.Block() as block:
            self.norm(block, ("final_w", 0), final=True)

    def finish(self):
        n = self.out_stored.after(16)
        with self.nc.Block() as block:
            @block.sync
            def _(sync):
                sync.dma_start(self.out, self.X[:, :, 0:TX]).then_inc(self.out_stored.handle, 16)
                sync.wait_ge(self.out_stored.handle, n + 16)

    def build(self):
        m1 = WC["mod1"]
        def stop(name):
            return self.upto == name
        self.begin()
        self.pool_mixer()
        if stop("pool"): return self.finish()
        self.ffn("f0", lambda block: self.norm(block, ("norm2_g", 0), [(WC["mod1"] + 24, WC["mod1"] + 32, 1)]),
                 [(m1 + 40, 1)], VC["conv1_w"], VC["conv1_b"], False,
                 Rider("ada1", "cond", 1, [(0, 24, WC["mod1b"], VC["ada_b"] + 48)]))
        if stop("ffn0"): return self.finish()
        m1 = WC["mod1b"]
        self.dilated_attention(m1, WC["kvmod"])
        self.add_product("wo", [(m1 + 16, 1)])
        if stop("attn"): return self.finish()
        self.ffn("f1", lambda block: self.norm(block, ("norm2_g", 8), [(m1 + 24, m1 + 32, 1)]), [(m1 + 40, 1)], VC["conv1_w"] + 66, VC["conv1_b"] + 22, False,
                 self.mod2_rider(0))
        with self.nc.Block() as block:
            self.norm(block, ("final_g", 0), final=True)
            self.lambdas(block)
        if stop("first"): return self.finish()
        self.second_block()
        self.finish()


def program(nc, aps, out, upto=None):
    with ExitStack() as ctx:
        Program(nc, ctx, aps, out, upto).build()


def cols(v):
    v = np.asarray(v)
    return v.reshape(-1, P).T


def items(w, order=None):
    w = np.asarray(w)
    K, N = w.shape
    kt = K // P
    if order is not None:
        w = w.reshape(K, N // P, P)[:, order].reshape(K, -1)
        N = w.shape[1]
    out = w.reshape(kt, P, N // 256, 256).transpose(2, 1, 0, 3).reshape(N // 256, P, kt * 256)
    if kt < KT:
        out = np.concatenate([out, np.zeros((N // 256, P, ITEM - kt * 256), w.dtype)], axis=2)
    return out


def ffn_items(up, down):
    out = []
    pairs = [t for j in range(FT) for t in (j, FT + j)]
    both = items(up, pairs)
    for first, n in FGROUPS:
        out += [both[first:first + n], items(down[first * P:(first + n) * P])]
    return out


def group_items(w):
    w = np.asarray(w).reshape(4, 2, P, 2, P)
    w = w.transpose(0, 3, 2, 1, 4).reshape(2, 4, P, 2 * P)
    w = w.transpose(0, 2, 1, 3).reshape(2, P, 8 * P)
    return np.concatenate([w, np.zeros((2, P, ITEM - 8 * P), w.dtype)], axis=2)


def weight_array(g):
    w = [items(g["pool_w_in"][0]), group_items(g["pool_w_grp"][0]), items(g["pool_w_out"][0])]
    w += ffn_items(g["ffn_w_up"][0], g["ffn_w_down"][0])
    kv = items(g["w_kv"])
    w += [items(g["attn_w_q"][0]), kv[:12], kv[12:16], kv[16:24],
          items(g["attn_w_o"][0])]
    w += ffn_items(g["ffn_w_up"][1], g["ffn_w_down"][1])
    for li in range(2):
        w += [items(g["w_in_2"][li], [4, 5, 6, 7, 14, 15, 16, 17, 0, 1, 2, 3, 12, 13, 20, 21, 22, 23, 8, 9, 10, 11, 18, 19]),
              items(g["w_out_2"][li])]
        w += ffn_items(g["w_up_2"][li], g["w_down_2"][li])
    out = np.concatenate(w)
    assert out.shape == (N_ITEMS, P, ITEM), (out.shape, N_ITEMS)
    return out


def mod_array(g):
    a = items(g["ada_w"][0])
    w = [a[0:12], a[20:24], a[12:16], a[16:20], items(g["ada_w"][1]), items(g["kv_ada_w"])]
    return np.concatenate(w + [items(g["w_ada_2"][li]) for li in range(2)])


def vector_array(g):
    out = np.zeros((P, NVEC), np.float32)

    def put(name, a):
        at, n = VC.at[name]
        assert a.shape == (P, n), (name, a.shape, n)
        out[:, at:at + n] = a
    put("c", cols(g["c"]))
    put("cc", np.stack([cols(g["c_2"]), cols(g["c_ctx_2"])], axis=2).reshape(P, 16))
    for name, key in (("ada_b", "ada_b"), ("kv_ada_b", "kv_ada_b"), ("b_ada", "b_ada_2"), ("norm1_g", "norm1_g"),
                      ("norm2_g", "norm2_g"), ("kv_norm_g", "kv_norm_g"), ("final_g", "final_g"),
                      ("pool_scale", "pool_scale"), ("norm1_w", "norm1_w_2"), ("norm2_w", "norm2_w_2"),
                      ("final_w", "final_norm_w_2"), ("conv1_b", "ffn_conv_b"), ("conv1_w", "ffn_conv_w"),
                      ("conv2_b", "conv_b_2"), ("conv2_w", "conv_w_2"), ("subln", "subln_w_2"),
                      ("lb", "lb_param_2")):
        put(name, cols(g[key]))
    put("hgrn_w", np.concatenate([g["hgrn_norm_w_2"].T, g["hgrn_norm_w_2"].T]))
    lam = g["lam_qk_2"].transpose(2, 0, 1).reshape(64, 8)
    put("lam", np.concatenate([lam, np.zeros_like(lam)]))
    return out


def alibi_slopes(n):
    def pow2(m):
        start = 2.0 ** (-(2.0 ** -(math.log2(m) - 3)))
        return [start ** (i + 1) for i in range(m)]
    c = 2 ** math.floor(math.log2(n))
    s = pow2(c) if c == n else pow2(c) + pow2(2 * c)[0::2][: n - c]
    return -np.sort(-np.asarray(s, np.float32))


def constants():
    out = {"ident": np.eye(P, dtype=np.float32)}
    edge = np.zeros((4, 16), np.float32)
    for g in range(4):
        w = 2 << g
        edge[g] = 1.0 / np.minimum(np.arange(16) + 1, w)
    key = np.arange(TX)
    dist = np.full((P, 4, TX), BIG, np.float32)
    for c in range(4):
        back = (4 * np.arange(P) + c)[:, None] - key[None]
        ok = (back >= 0) & (back <= 128)
        dist[:, c][ok] = back[ok]
    back = np.arange(P)[:, None] - np.arange(P)[None]
    near = np.full((P, 2, P), BIG, np.float32)
    near[:, 0][back >= 0] = 4.0 * back[back >= 0]
    ok = (back >= 0) & (back % 4 == 0)
    near[:, 1][ok] = 4.0 * back[ok]
    out["dist0"], out["dist12"] = dist, near
    out["slopes"] = np.broadcast_to(-alibi_slopes(NBR * NH1) * HD ** 0.5, (P, NBR * NH1)).astype(np.float32)
    masks = np.zeros((P, 2 * LEVELS, P), np.int32)
    a, b = np.arange(P)[:, None], np.arange(P)[None]
    for lv in range(LEVELS):
        same = a >> (lv + 1) == b >> (lv + 1)
        for d in range(2):
            masks[:, 2 * lv + d] = same & ((a >> lv & 1) == d) & ((b >> lv & 1) == 1 - d)
    out["level_masks"] = masks
    out["block_reset"] = np.broadcast_to((np.arange(TA) % P != 0).astype(np.float32), (P, TA)).copy()
    out["half"] = np.kron(np.eye(2), np.ones((HD, HD))).astype(np.float32)
    inv = 10000.0 ** (-np.arange(0, 32, 2, dtype=np.float32) / np.float32(32))
    t = np.arange(TX)
    ang_r = (t // 64).astype(np.float32)[:, None] * inv.astype(np.float32)
    ang_c = (t % 64).astype(np.float32)[:, None] * inv.astype(np.float32)
    ang = np.concatenate([ang_r, ang_r, ang_c, ang_c] * 2, axis=1).T
    out["rope_cs"] = np.stack([np.cos(ang), np.sin(ang)], axis=1).astype(np.float32)
    perm = np.zeros((P, P), np.float32)
    for lo in range(0, P, 32):
        for i in range(16):
            perm[lo + i + 16, lo + i] = -1.0
            perm[lo + i, lo + i + 16] = 1.0
    out["rope_perm"] = perm
    n = np.arange(TX)
    ang = 2 * np.pi * (np.outer(n, n) % TX) / TX
    out["dft"] = np.stack([np.cos(ang), -np.sin(ang)]).reshape(2, 4, P, TX).transpose(2, 0, 1, 3).astype(np.float32)
    n = np.arange(64)
    ang = 2 * np.pi * (np.outer(n, n) % 64) / 64
    out["dft64"] = np.concatenate([np.kron(np.eye(2), np.cos(ang)), np.kron(np.eye(2), np.sin(ang))], axis=1).astype(np.float32)
    out["pool_edge"] = np.broadcast_to(edge, (P, 4, 16)).copy()
    return out


def host_inputs(g):
    g = {k: np.asarray(v) for k, v in g.items()}
    return {
        "weights": weight_array(g), "mods": mod_array(g), "vectors": vector_array(g),
        "xT": np.ascontiguousarray(g["x"][0].T.reshape(KT, P, TX).transpose(1, 0, 2)),
        "ctxT": np.ascontiguousarray(g["ctx_2"][0].T.reshape(KT, P, TC).transpose(1, 0, 2)),
        "w_fnet": np.ascontiguousarray(g["w_fnet_2"].reshape(2, 2, P, 256).transpose(0, 2, 1, 3)),
        **constants(),
    }


def kernel(**inputs):
    import concourse.bacc as bacc
    from concourse.bass_utils import run_bass_kernel_spmd

    nc = bacc.Bacc("TRN2", target_bir_lowering=False, num_devices=1)
    arrays = host_inputs(inputs)
    aps = {n: nc.dram_tensor(n, a.shape, mybir.dt.from_np(a.dtype), kind="ExternalInput").ap()
           for n, a in arrays.items()}
    out = nc.dram_tensor("out", (P, KT, TX), F32, kind="ExternalOutput").ap()
    program(nc, aps, out)
    r = run_bass_kernel_spmd(nc, [arrays], core_ids=[0])
    y = r.results[0]["out"]
    return np.ascontiguousarray(y.transpose(1, 0, 2).reshape(D, TX).T)[None]
```
